# Optimizing a Trainium2 kernel written in Bass

```python
import jax, jax.numpy as jnp
from jax import lax
import numpy as np

D_MODEL = 1024
BATCH = 1
SEQ = 1024
DEPTH = 1
DEC_BATCH = 8
DEC_SEQ = 8
PAST_LEN = 256
PAGE_SIZE = 128

HEAD_DIM = 64
NSA_HEADS = 4
NSA_BLOCK = 64
NSA_TOPK = 16
NSA_WINDOW = 512
NSA_ROWS = 4
MLSTM_HEADS = 4
MLSTM_CHUNK = 64
FOX_HEADS = 4
Q_BLOCK = 128
N_BRANCH = 3
BRANCH_WIDTH = NSA_HEADS * HEAD_DIM
N_GROUPS = 4
EXPERTS_PER_GROUP = 4
N_EXPERTS = N_GROUPS * EXPERTS_PER_GROUP
TOP_K_IN_GROUP = 2
D_EXPERT = 256
FORGET_BIAS = 3.0
LN_EPS = 1e-5
NEG_INF = -1e30
TINY = 1e-30
FORCED_SCORE = 1e9
ATTN_SCALE = HEAD_DIM ** -0.5

IN_SPLITS = (
    NSA_HEADS * HEAD_DIM,
    6 * HEAD_DIM,
    NSA_HEADS * 3,
    MLSTM_HEADS * HEAD_DIM,
    MLSTM_HEADS * HEAD_DIM,
    MLSTM_HEADS * HEAD_DIM,
    MLSTM_HEADS * HEAD_DIM,
    MLSTM_HEADS,
    MLSTM_HEADS,
    FOX_HEADS * HEAD_DIM,
    FOX_HEADS * HEAD_DIM,
    FOX_HEADS * HEAD_DIM,
    FOX_HEADS,
    N_BRANCH * D_MODEL,
)
IDX_ML_F = 8
IDX_FOX_F = 12

kernel_name = 'hybrid_nsa_mlstm_fox_hmoe_step'

def _split_points():
    return [int(v) for v in np.cumsum(IN_SPLITS)[:-1]]

def _layer_norm(x, w, b):
    xf = x.astype(jnp.float32)
    mu = jnp.mean(xf, axis=-1, keepdims=True)
    var = jnp.mean(jnp.square(xf - mu), axis=-1, keepdims=True)
    y = (xf - mu) * lax.rsqrt(var + LN_EPS) * w.astype(jnp.float32) + b.astype(jnp.float32)
    return y.astype(x.dtype)

def _masked_softmax(s, mask):
    s = jnp.where(mask, s.astype(jnp.float32), NEG_INF)
    p = jnp.exp(s - jnp.max(s, axis=-1, keepdims=True)) * mask
    return p / jnp.maximum(jnp.sum(p, axis=-1, keepdims=True), TINY)

def _alibi_slopes(n):
    return jnp.exp2(-8.0 * jnp.arange(1, n + 1, dtype=jnp.float32) / n)

def _project(x, w_in, b_in):
    B, L, _ = x.shape
    f32 = jnp.float32
    z = x @ w_in + b_in
    (nq, nkv, ng, mq, mk, mv, mo, mi, mf, fq, fk, fv, ff, gm) = jnp.split(z, _split_points(), axis=-1)
    heads = lambda t, h: t.reshape(B, L, h, HEAD_DIM)
    rows = nkv.reshape(B, L, 6, HEAD_DIM)
    return dict(
        nsa_q=heads(nq, NSA_HEADS),
        nsa_rows=rows[:, :, :NSA_ROWS],
        nsa_win=rows[:, :, NSA_ROWS:],
        nsa_g=jax.nn.sigmoid(ng.astype(f32)).reshape(B, L, NSA_HEADS, 3),
        ml_q=heads(mq, MLSTM_HEADS).astype(f32),
        ml_k=heads(mk, MLSTM_HEADS).astype(f32) * ATTN_SCALE,
        ml_v=heads(mv, MLSTM_HEADS).astype(f32),
        ml_o=jax.nn.sigmoid(mo.astype(f32)).reshape(B, L, MLSTM_HEADS, HEAD_DIM),
        ml_i=mi.astype(f32),
        ml_lf=jax.nn.log_sigmoid(mf.astype(f32)),
        fox_q=heads(fq, FOX_HEADS),
        fox_k=heads(fk, FOX_HEADS),
        fox_v=heads(fv, FOX_HEADS),
        fox_lf=jax.nn.log_sigmoid(ff.astype(f32)),
        merge=jax.nn.sigmoid(gm.astype(f32)).reshape(B, L, N_BRANCH, D_MODEL))

def _nsa_compress(k, w):
    B, L, _ = k.shape
    n_cb = L // NSA_BLOCK
    blocks = k[:, :n_cb * NSA_BLOCK].reshape(B, n_cb, NSA_BLOCK, HEAD_DIM)
    return jnp.einsum('bjpd,pde->bje', blocks, w)

def _nsa_cmp_attend(q, kc, vc, pos_q, slopes):
    n_cb = kc.shape[1]
    blk_end = jnp.arange(n_cb) * NSA_BLOCK + NSA_BLOCK - 1
    dist = pos_q[:, None] - blk_end[None, :]
    s = jnp.einsum('bqhd,bjd->bhqj', q, kc) * ATTN_SCALE - slopes[:, None, None] * dist.astype(jnp.float32)
    p = _masked_softmax(s, dist >= 0)
    o = jnp.einsum('bhqj,bjd->bqhd', p.astype(vc.dtype), vc)
    return o, jnp.sum(p, axis=1)

def _nsa_select_blocks(imp, pos_q, n_sb):
    n_cb = imp.shape[-1]
    imp = jnp.pad(imp, ((0, 0), (0, 0), (0, n_sb - n_cb)))
    j = jnp.arange(n_sb)[None, :]
    cur = (pos_q // NSA_BLOCK)[:, None]
    score = jnp.where(j > cur, NEG_INF, jnp.where((j == cur) | (j == 0), FORCED_SCORE, imp))
    vals, idx = lax.top_k(score, min(NSA_TOPK, n_sb))
    return idx, vals > 0.5 * NEG_INF

def _nsa_sel_attend(q, kb, vb, idx, valid, pos_q, slopes):
    B, Q = q.shape[:2]
    bi = jnp.arange(B)[:, None, None]
    kg = kb[bi, idx].reshape(B, Q, -1, HEAD_DIM)
    vg = vb[bi, idx].reshape(B, Q, -1, HEAD_DIM)
    pos_k = (idx[..., None] * NSA_BLOCK + jnp.arange(NSA_BLOCK)).reshape(B, Q, -1)
    ok = jnp.repeat(valid, NSA_BLOCK, axis=-1) & (pos_k <= pos_q[None, :, None])
    dist = (pos_q[None, :, None] - pos_k).astype(jnp.float32)
    s = jnp.einsum('bqhd,bqkd->bhqk', q, kg) * ATTN_SCALE - slopes[None, :, None, None] * dist[:, None]
    p = _masked_softmax(s, ok[:, None])
    return jnp.einsum('bhqk,bqkd->bqhd', p.astype(vg.dtype), vg)

def _nsa_cmp_sel(q, rows, pos_q, w_ck, w_cv, slopes):
    B, Q = q.shape[:2]
    L = rows.shape[1]
    kc = _nsa_compress(rows[:, :, 0], w_ck)
    vc = _nsa_compress(rows[:, :, 1], w_cv)
    o_cmp, imp = _nsa_cmp_attend(q, kc, vc, pos_q, slopes)
    n_sb = -(-L // NSA_BLOCK)
    idx, valid = _nsa_select_blocks(imp, pos_q, n_sb)
    pad = ((0, 0), (0, n_sb * NSA_BLOCK - L), (0, 0))
    kb = jnp.pad(rows[:, :, 2], pad).reshape(B, n_sb, NSA_BLOCK, HEAD_DIM)
    vb = jnp.pad(rows[:, :, 3], pad).reshape(B, n_sb, NSA_BLOCK, HEAD_DIM)
    qb = Q_BLOCK if Q % Q_BLOCK == 0 else Q
    nqb = Q // qb

    def block(args):
        qc, ic, okc, pc = args
        return _nsa_sel_attend(qc, kb, vb, ic, okc, pc, slopes)

    xs = (q.reshape(B, nqb, qb, NSA_HEADS, HEAD_DIM).swapaxes(0, 1),
          idx.reshape(B, nqb, qb, -1).swapaxes(0, 1),
          valid.reshape(B, nqb, qb, -1).swapaxes(0, 1),
          pos_q.reshape(nqb, qb))
    o_sel = lax.map(block, xs).swapaxes(0, 1).reshape(B, Q, NSA_HEADS, HEAD_DIM)
    return o_cmp, o_sel

def _nsa_win_attend(q, k, v, pos_q, pos_k, slopes):
    dist = pos_q[:, None] - pos_k[None, :]
    ok = (dist >= 0) & (dist < NSA_WINDOW) & (pos_k[None, :] >= 0)
    s = jnp.einsum('bqhd,bkd->bhqk', q, k) * ATTN_SCALE - slopes[:, None, None] * dist.astype(jnp.float32)
    p = _masked_softmax(s, ok)
    return jnp.einsum('bhqk,bkd->bqhd', p.astype(v.dtype), v)

def _nsa_win_prompt(q, k, v, slopes):
    B, S = q.shape[:2]
    nqb = S // Q_BLOCK
    nb = NSA_WINDOW // Q_BLOCK
    pad = ((0, 0), (NSA_WINDOW, 0), (0, 0))
    kp = jnp.pad(k, pad).reshape(B, nqb + nb, Q_BLOCK, HEAD_DIM)
    vp = jnp.pad(v, pad).reshape(B, nqb + nb, Q_BLOCK, HEAD_DIM)
    band = jnp.arange(nqb)[:, None] + jnp.arange(nb + 1)[None, :]
    kband = kp[:, band].reshape(B, nqb, (nb + 1) * Q_BLOCK, HEAD_DIM)
    vband = vp[:, band].reshape(B, nqb, (nb + 1) * Q_BLOCK, HEAD_DIM)
    qblk = q.reshape(B, nqb, Q_BLOCK, NSA_HEADS, HEAD_DIM)
    pos_q = jnp.arange(S).reshape(nqb, Q_BLOCK)
    pos_k = (jnp.arange(nqb) * Q_BLOCK - NSA_WINDOW)[:, None] + jnp.arange((nb + 1) * Q_BLOCK)[None, :]
    o = jax.vmap(_nsa_win_attend, in_axes=(1, 1, 1, 0, 0, None), out_axes=1)(qblk, kband, vband, pos_q, pos_k, slopes)
    return o.reshape(B, S, NSA_HEADS, HEAD_DIM)

def _nsa_combine(g, o_cmp, o_sel, o_win):
    return jnp.einsum('blhc,cblhd->blhd', g, jnp.stack([o_cmp, o_sel, o_win]))

def _mlstm_chunk(carry, xs):
    c, n, m = carry
    q, k, v, ig, lf = xs
    L = q.shape[1]
    b = jnp.cumsum(lf, axis=1)
    causal = jnp.tril(jnp.ones((L, L), bool))[None, :, :, None]
    dmat = jnp.where(causal, b[:, :, None, :] - b[:, None, :, :] + ig[:, None, :, :], NEG_INF)
    a = b + m[:, None, :]
    m_t = jnp.maximum(a, jnp.max(dmat, axis=2))
    wq = jnp.exp(dmat - m_t[:, :, None, :]) * jnp.einsum('bthd,bshd->btsh', q, k)
    inter = jnp.exp(a - m_t)
    num = inter[..., None] * jnp.einsum('bthd,bhde->bthe', q, c) + jnp.einsum('btsh,bshe->bthe', wq, v)
    den = inter * jnp.einsum('bthd,bhd->bth', q, n) + jnp.sum(wq, axis=2)
    h = num / jnp.maximum(jnp.abs(den), jnp.exp(-m_t))[..., None]
    bl = b[:, -1]
    g = bl[:, None, :] - b + ig
    m_new = jnp.maximum(bl + m, jnp.max(g, axis=1))
    ws = jnp.exp(g - m_new[:, None, :])
    decay = jnp.exp(bl + m - m_new)
    c_new = decay[..., None, None] * c + jnp.einsum('bsh,bshd,bshe->bhde', ws, k, v)
    n_new = decay[..., None] * n + jnp.einsum('bsh,bshd->bhd', ws, k)
    return (c_new, n_new, m_new), h

def _mlstm_prompt(q, k, v, ig, lf):
    B, S, H, _ = q.shape
    ch = MLSTM_CHUNK if S % MLSTM_CHUNK == 0 else S
    nc = S // ch
    to_chunks = lambda t: t.reshape((B, nc, ch) + t.shape[2:]).swapaxes(0, 1)
    f32 = jnp.float32
    init = (jnp.zeros((B, H, HEAD_DIM, HEAD_DIM), f32), jnp.zeros((B, H, HEAD_DIM), f32), jnp.zeros((B, H), f32))
    state, h = lax.scan(_mlstm_chunk, init, tuple(to_chunks(t) for t in (q, k, v, ig, lf)))
    return h.swapaxes(0, 1).reshape(B, S, H, HEAD_DIM), state

def _mlstm_readout(h, o_gate, norm_w):
    h = o_gate * h
    mu = jnp.mean(h, axis=-1, keepdims=True)
    var = jnp.mean(jnp.square(h - mu), axis=-1, keepdims=True)
    return (h - mu) * lax.rsqrt(var + LN_EPS) * norm_w.astype(jnp.float32).reshape(MLSTM_HEADS, HEAD_DIM)

def _fox_attend(q, k, v, fq, fk, pos_q, pos_k):
    s = jnp.einsum('bqhd,bkhd->bhqk', q, k) * ATTN_SCALE
    s = s + (fq.transpose(0, 2, 1)[..., None] - fk.transpose(0, 2, 1)[:, :, None, :])
    p = _masked_softmax(s, pos_k[None, :] <= pos_q[:, None])
    return jnp.einsum('bhqk,bkhd->bqhd', p.astype(v.dtype), v)

def _fox_prompt(q, k, v, F):
    B, S = q.shape[:2]
    qb = Q_BLOCK if S % Q_BLOCK == 0 else S
    nqb = S // qb
    pos = jnp.arange(S)

    def block(args):
        qc, fc, pc = args
        return _fox_attend(qc, k, v, fc, F, pc, pos)

    xs = (q.reshape(B, nqb, qb, FOX_HEADS, HEAD_DIM).swapaxes(0, 1),
          F.reshape(B, nqb, qb, FOX_HEADS).swapaxes(0, 1),
          pos.reshape(nqb, qb))
    return lax.map(block, xs).swapaxes(0, 1).reshape(B, S, FOX_HEADS, HEAD_DIM)

def _merge(gates, o_nsa, o_ml, o_fox, w_branch, w_out, dtype):
    B, L = o_nsa.shape[:2]
    br = jnp.stack([o.reshape(B, L, BRANCH_WIDTH).astype(dtype) for o in (o_nsa, o_ml, o_fox)], axis=2)
    proj = jnp.einsum('blmc,mcd->blmd', br, w_branch)
    y = jnp.einsum('blmd,blmd->bld', gates, proj).astype(dtype)
    return y @ w_out

def _moe(x, w_group, b_group, w_expert, b_expert, w_gate, w_up, w_down):
    B, L, D = x.shape
    t = x.reshape(B * L, D)
    pg = jax.nn.softmax((t @ w_group + b_group).astype(jnp.float32), axis=-1)
    g_val, g_idx = lax.top_k(pg, 1)
    le = (t @ w_expert + b_expert).astype(jnp.float32).reshape(-1, N_GROUPS, EXPERTS_PER_GROUP)
    le = jnp.take_along_axis(le, g_idx[:, :, None], axis=1)[:, 0]
    e_val, e_idx = lax.top_k(jax.nn.softmax(le, axis=-1), TOP_K_IN_GROUP)
    e_w = g_val * e_val / jnp.sum(e_val, axis=-1, keepdims=True)
    gate = jnp.sum(jax.nn.one_hot(g_idx * EXPERTS_PER_GROUP + e_idx, N_EXPERTS, dtype=jnp.float32) * e_w[..., None], axis=1)
    h = jax.nn.silu(jnp.einsum('td,edf->tef', t, w_gate)) * jnp.einsum('td,edf->tef', t, w_up)
    h = h * gate[:, :, None].astype(h.dtype)
    return jnp.einsum('tef,efd->td', h, w_down).reshape(B, L, D)

def _mixers_prompt(x, w_in, b_in, w_ck, w_cv, ml_norm_w, w_branch, w_out, slopes):
    B, S, _ = x.shape
    pr = _project(x, w_in, b_in)
    pos = jnp.arange(S)
    o_cmp, o_sel = _nsa_cmp_sel(pr['nsa_q'], pr['nsa_rows'], pos, w_ck, w_cv, slopes)
    o_win = _nsa_win_prompt(pr['nsa_q'], pr['nsa_win'][:, :, 0], pr['nsa_win'][:, :, 1], slopes)
    o_nsa = _nsa_combine(pr['nsa_g'], o_cmp, o_sel, o_win)
    h, (c, n, m) = _mlstm_prompt(pr['ml_q'], pr['ml_k'], pr['ml_v'], pr['ml_i'], pr['ml_lf'])
    o_ml = _mlstm_readout(h, pr['ml_o'], ml_norm_w)
    o_fox = _fox_prompt(pr['fox_q'], pr['fox_k'], pr['fox_v'], jnp.cumsum(pr['fox_lf'], axis=1))
    out = _merge(pr['merge'], o_nsa, o_ml, o_fox, w_branch, w_out, x.dtype)
    w_keep = min(NSA_WINDOW, S)
    new = (pr['nsa_rows'], pr['nsa_win'][:, S - w_keep:], jnp.stack([pr['fox_k'], pr['fox_v']], axis=2),
           pr['fox_lf'], c, n, m)
    return out, new

def _mixers_sample(x, c_nsa, c_win, c_fox_kv, c_fox_lf, s_c, s_n, s_m, page_table,
                   w_in, b_in, w_ck, w_cv, ml_norm_w, w_branch, w_out, slopes):
    DB, T, _ = x.shape
    past = page_table.shape[1] * PAGE_SIZE
    f32 = jnp.float32
    pr = _project(x, w_in, b_in)
    pos_q = past + jnp.arange(T)
    rows_past = c_nsa[page_table].reshape(DB, past, NSA_ROWS, HEAD_DIM)
    rows_all = jnp.concatenate([rows_past, pr['nsa_rows'].astype(rows_past.dtype)], axis=1)
    o_cmp, o_sel = _nsa_cmp_sel(pr['nsa_q'], rows_all, pos_q, w_ck, w_cv, slopes)
    wb = c_win.shape[1]
    win_all = jnp.concatenate([c_win, pr['nsa_win'].astype(c_win.dtype)], axis=1)
    pos_k = past - wb + jnp.arange(wb + T)
    o_win = _nsa_win_attend(pr['nsa_q'], win_all[:, :, 0], win_all[:, :, 1], pos_q, pos_k, slopes)
    o_nsa = _nsa_combine(pr['nsa_g'], o_cmp, o_sel, o_win)
    (c, n, m), h = _mlstm_chunk((s_c.astype(f32), s_n.astype(f32), s_m.astype(f32)),
                                (pr['ml_q'], pr['ml_k'], pr['ml_v'], pr['ml_i'], pr['ml_lf']))
    o_ml = _mlstm_readout(h, pr['ml_o'], ml_norm_w)
    kv_past = c_fox_kv[page_table].reshape(DB, past, 2, FOX_HEADS, HEAD_DIM)
    k_all = jnp.concatenate([kv_past[:, :, 0], pr['fox_k'].astype(kv_past.dtype)], axis=1)
    v_all = jnp.concatenate([kv_past[:, :, 1], pr['fox_v'].astype(kv_past.dtype)], axis=1)
    lf_all = jnp.concatenate([c_fox_lf[page_table].reshape(DB, past, FOX_HEADS).astype(f32), pr['fox_lf']], axis=1)
    F = jnp.cumsum(lf_all, axis=1)
    o_fox = _fox_attend(pr['fox_q'], k_all, v_all, F[:, past:], F, pos_q, jnp.arange(past + T))
    out = _merge(pr['merge'], o_nsa, o_ml, o_fox, w_branch, w_out, x.dtype)
    new = (pr['nsa_rows'], win_all[:, T:], jnp.stack([pr['fox_k'], pr['fox_v']], axis=2),
           pr['fox_lf'], c, n, m)
    return out, new

def _stack_layers(states):
    return tuple(jnp.stack(list(a)) for a in zip(*states))

def setup_inputs(seed: int = 0) -> dict:
    key = jax.random.key(seed)
    keys = iter(jax.random.split(key, 40))
    f32 = jnp.float32

    def nrm(shape, scale):
        return jax.random.normal(next(keys), shape, f32) * scale

    beta = (8.0 * DEPTH) ** -0.25
    n_pages = PAST_LEN // PAGE_SIZE
    n_used = DEC_BATCH * n_pages
    n_phys = n_used + max(n_used // 4, 1)
    page_table = jax.random.permutation(next(keys), n_phys)[:n_used].reshape(DEC_BATCH, n_pages).astype(jnp.int32)
    win_buf = min(NSA_WINDOW, PAST_LEN)
    n_in = sum(IN_SPLITS)
    starts = np.concatenate([[0], np.cumsum(IN_SPLITS)])
    offset = np.zeros((n_in,), np.float32)
    offset[starts[IDX_ML_F]:starts[IDX_ML_F + 1]] = FORGET_BIAS
    offset[starts[IDX_FOX_F]:starts[IDX_FOX_F + 1]] = FORGET_BIAS
    return {
        'x_prompt': nrm((BATCH, SEQ, D_MODEL), 1.0),
        'x_sample': nrm((DEC_BATCH, DEC_SEQ, D_MODEL), 1.0),
        'cache_nsa': nrm((DEPTH, n_phys, PAGE_SIZE, NSA_ROWS, HEAD_DIM), 1.0),
        'cache_nsa_win': nrm((DEPTH, DEC_BATCH, win_buf, 2, HEAD_DIM), 1.0),
        'cache_fox_kv': nrm((DEPTH, n_phys, PAGE_SIZE, 2, FOX_HEADS, HEAD_DIM), 1.0),
        'cache_fox_logf': jax.nn.log_sigmoid(FORGET_BIAS + nrm((DEPTH, n_phys, PAGE_SIZE, FOX_HEADS), 1.0)),
        'state_mlstm_c': nrm((DEPTH, DEC_BATCH, MLSTM_HEADS, HEAD_DIM, HEAD_DIM), 1.0),
        'state_mlstm_n': nrm((DEPTH, DEC_BATCH, MLSTM_HEADS, HEAD_DIM), 1.0),
        'state_mlstm_m': nrm((DEPTH, DEC_BATCH, MLSTM_HEADS), 1.0),
        'page_table': page_table,
        'ln_in_w': 1.0 + nrm((D_MODEL,), 0.02),
        'ln_in_b': nrm((D_MODEL,), 0.02),
        'w_in': nrm((DEPTH, D_MODEL, n_in), D_MODEL ** -0.5),
        'b_in': nrm((DEPTH, n_in), 0.02) + jnp.asarray(offset),
        'nsa_w_ck': nrm((DEPTH, NSA_BLOCK, HEAD_DIM, HEAD_DIM), (NSA_BLOCK * HEAD_DIM) ** -0.5),
        'nsa_w_cv': nrm((DEPTH, NSA_BLOCK, HEAD_DIM, HEAD_DIM), (NSA_BLOCK * HEAD_DIM) ** -0.5),
        'mlstm_norm_w': 1.0 + nrm((DEPTH, MLSTM_HEADS * HEAD_DIM), 0.02),
        'w_branch': nrm((DEPTH, N_BRANCH, BRANCH_WIDTH, D_MODEL), beta * BRANCH_WIDTH ** -0.5),
        'w_out': nrm((DEPTH, D_MODEL, D_MODEL), beta * D_MODEL ** -0.5),
        'ln1_w': 1.0 + nrm((DEPTH, D_MODEL), 0.02),
        'ln1_b': nrm((DEPTH, D_MODEL), 0.02),
        'moe_w_group': nrm((DEPTH, D_MODEL, N_GROUPS), D_MODEL ** -0.5),
        'moe_b_group': nrm((DEPTH, N_GROUPS), 0.01),
        'moe_w_expert': nrm((DEPTH, D_MODEL, N_EXPERTS), D_MODEL ** -0.5),
        'moe_b_expert': nrm((DEPTH, N_EXPERTS), 0.01),
        'moe_w_gate': nrm((DEPTH, N_EXPERTS, D_MODEL, D_EXPERT), D_MODEL ** -0.5),
        'moe_w_up': nrm((DEPTH, N_EXPERTS, D_MODEL, D_EXPERT), D_MODEL ** -0.5),
        'moe_w_down': nrm((DEPTH, N_EXPERTS, D_EXPERT, D_MODEL), beta * D_EXPERT ** -0.5),
        'ln2_w': 1.0 + nrm((DEPTH, D_MODEL), 0.02),
        'ln2_b': nrm((DEPTH, D_MODEL), 0.02),
    }

def reference(x_prompt, x_sample, cache_nsa, cache_nsa_win, cache_fox_kv, cache_fox_logf,
              state_mlstm_c, state_mlstm_n, state_mlstm_m, page_table,
              ln_in_w, ln_in_b, w_in, b_in, nsa_w_ck, nsa_w_cv, mlstm_norm_w, w_branch, w_out,
              ln1_w, ln1_b, moe_w_group, moe_b_group, moe_w_expert, moe_b_expert,
              moe_w_gate, moe_w_up, moe_w_down, ln2_w, ln2_b):
    alpha = (2.0 * DEPTH) ** 0.25
    slopes = _alibi_slopes(NSA_HEADS)
    xp = _layer_norm(x_prompt, ln_in_w, ln_in_b)
    xs = _layer_norm(x_sample, ln_in_w, ln_in_b)
    new_p, new_s = [], []
    for l in range(DEPTH):
        mix_w = (w_in[l], b_in[l], nsa_w_ck[l], nsa_w_cv[l], mlstm_norm_w[l], w_branch[l], w_out[l])
        moe_w = (moe_w_group[l], moe_b_group[l], moe_w_expert[l], moe_b_expert[l],
                 moe_w_gate[l], moe_w_up[l], moe_w_down[l])
        mix_p, st_p = _mixers_prompt(xp, *mix_w, slopes)
        xp = _layer_norm(alpha * xp + mix_p, ln1_w[l], ln1_b[l])
        xp = _layer_norm(alpha * xp + _moe(xp, *moe_w), ln2_w[l], ln2_b[l])
        mix_s, st_s = _mixers_sample(xs, cache_nsa[l], cache_nsa_win[l], cache_fox_kv[l], cache_fox_logf[l],
                                     state_mlstm_c[l], state_mlstm_n[l], state_mlstm_m[l], page_table,
                                     *mix_w, slopes)
        xs = _layer_norm(alpha * xs + mix_s, ln1_w[l], ln1_b[l])
        xs = _layer_norm(alpha * xs + _moe(xs, *moe_w), ln2_w[l], ln2_b[l])
        new_p.append(st_p)
        new_s.append(st_s)
    (p_nsa_rows, p_nsa_win, p_fox_kv, p_fox_logf, p_mlstm_c, p_mlstm_n, p_mlstm_m) = _stack_layers(new_p)
    (s_nsa_rows, s_nsa_win, s_fox_kv, s_fox_logf, s_mlstm_c, s_mlstm_n, s_mlstm_m) = _stack_layers(new_s)
    return (xp, xs, p_nsa_rows, p_nsa_win, p_fox_kv, p_fox_logf, p_mlstm_c, p_mlstm_n, p_mlstm_m,
            s_nsa_rows, s_nsa_win, s_fox_kv, s_fox_logf, s_mlstm_c, s_mlstm_n, s_mlstm_m)


_drawn_inputs = setup_inputs


def setup_inputs(seed=0):
    import zlib

    import numpy as np

    out = dict(_drawn_inputs(seed))
    spreads = {}
    factors = {'cache_fox_logf': 76.04,
     'mlstm_norm_w': 17.084,
     'moe_b_group': 5.564,
     'moe_b_expert': 18.84,
     'ln2_w': 20.556,
     'ln2_b': 21.987,
     'cache_fox_kv': 3.382,
     'nsa_w_ck': 6.559}
    for name, (base, spread) in spreads.items():
        noise = np.random.default_rng([zlib.crc32(name.encode()), seed]).standard_normal(out[name].shape)
        drawn = base * np.exp(spread * noise) if base else spread * noise
        out[name] = __import__('jax').numpy.asarray(drawn.astype(out[name].dtype))
    for name, factor in factors.items():
        out[name] = (out[name] * factor).astype(out[name].dtype)
    return out
```

```python
from contextlib import ExitStack

import numpy as np
import concourse.bass as bass
from concourse import mybir

F32 = mybir.dt.float32
I32 = mybir.dt.int32
ALU = mybir.AluOpType
ACT = mybir.ActivationFunctionType
AX = mybir.AxisListType

P = 128
D = 1024
KD = D // P
SEQ, DB, DT = 1024, 8, 8
PT = SEQ // P
ND = DB * DT
NT = PT + 1
T = SEQ + ND
H, HD = 4, 64
BW = H * HD
BLK = 64
NCB = SEQ // BLK
PAST = 256
PAGE = 128
NPG = PAST // PAGE
DCB = PAST // BLK
WIN = 512
SCALE = HD ** -0.5
EPS = 1e-5
TINY = 1e-30
NEG = -1e30
FLOOR = -1e20
ALPHA = 2.0 ** 0.25
NE, FE = 16, 256
GROUPS, PER = 4, 4
SLOPES = [2.0 ** (-8.0 * (h + 1) / H) for h in range(H)]

C_NQ, C_NKV, C_MQ, C_MK, C_MV, C_MO, C_FQ, C_FK, C_FV, C_GM = 0, 256, 652, 908, 1164, 1420, 1684, 1940, 2196, 2456
NIN = C_GM + 3 * D
Z_KC, Z_VC, Z_KS, Z_VS, Z_KW, Z_VW, Z_NG = 0, 64, 128, 192, 256, 320, 384
Z_MK = 396
Z_MV = 652
VW1 = HD + 1
Z_MO = Z_MV + H * VW1
Z_MI = Z_MO + BW
Z_MF = Z_MI + H
Z_FK = Z_MF + H
Z_FV = Z_FK + BW
Z_FF = Z_FV + BW
ZW = Z_FF + H
CHUNKS = [(True, C_NQ, 256, 0), (False, 256, 256, 0), (False, 512, 140, 256),
          (True, C_MQ, 256, 1), (False, C_MK, 256, Z_MK), (False, C_MV, 256, Z_MV), (False, C_MO, 264, Z_MO),
          (True, C_FQ, 256, 2), (False, C_FK, 256, Z_FK), (False, C_FV, 260, Z_FV)]
CW = 264
NCH = [(0, 512), (512, 512), (1024, ND)]


def rows(t):
    return P if t < PT else ND


def const_tables():
    p = np.arange(P)
    c = np.arange(P)
    out, at, cols = {}, {}, 0

    def put(name, a):
        nonlocal cols
        a = np.asarray(a, np.float32)
        full = np.zeros((P, a.shape[1]), np.float32)
        full[:a.shape[0]] = a
        out[name], at[name] = full, (cols, cols + a.shape[1])
        cols += a.shape[1]

    put("ident", np.eye(P))
    put("ones", np.ones((P, P)))
    put("minus_half", np.full((P, 16), -0.5))
    put("upto", p[:, None] <= c[None, :])
    put("after", p[:, None] > c[None, :])
    put("mask_future", np.where(c[None, :] > p[:, None], NEG, 0.0))
    put("mask_future_t", np.where(p[:, None] > c[None, :], NEG, 0.0))
    put("mask_window", np.where(c[None, :] <= p[:, None], NEG, 0.0))
    cb = np.full((P, PT, H, 32), NEG)
    for i in range(PT):
        for h in range(H):
            for j in range(NCB):
                dist = i * P + p - (j * BLK + BLK - 1)
                cb[:, i, h, j] = np.where(dist >= 0, -SLOPES[h] * dist, NEG)
    put("cmp_bias", cb.reshape(P, -1))
    put("head_bcast", np.repeat(np.eye(H), P, axis=1))
    split = cols
    b4, hh, tt = p // 32, (p // 8) % 4, p % 8
    slope = np.array(SLOPES)[hh]
    sb = np.zeros((P, 2, PAST + ND))
    cd = np.zeros((P, 2, DB * DCB))
    fb = np.zeros((P, 2, PAST + ND))
    mn = np.zeros((P, 2, ND))
    k = np.arange(PAST)
    n = np.arange(ND)
    for g in range(2):
        b = 4 * g + b4
        sb[:, g, :PAST] = -slope[:, None] * (PAST + tt[:, None] - k[None, :])
        own = (n[None, :] // DT == b[:, None]) & (n[None, :] % DT <= tt[:, None])
        sb[:, g, PAST:] = np.where(own, -slope[:, None] * (tt[:, None] - n[None, :] % DT), NEG)
        mn[:, g] = np.where(own, 0.0, NEG)
        j = np.arange(DB * DCB)
        dist = PAST + tt[:, None] - (j[None, :] % DCB * BLK + BLK - 1)
        fb[:, g, PAST:] = mn[:, g]
        cd[:, g] = np.where(j[None, :] // DCB == b[:, None], -slope[:, None] * dist, NEG)
    put("dec_bias", sb.reshape(P, -1))
    put("dec_fox_bias", fb.reshape(P, -1))
    put("dec_cmp_bias", cd.reshape(P, -1))
    put("dec_mask", mn.reshape(P, -1))
    put("head_of_row", hh[:, None] == np.arange(H)[None, :])
    bn, tn = n // DT, n % DT
    brow = np.concatenate([b4, 4 + b4])
    trow = np.concatenate([tt, tt])
    put("row_of_token", (bn[:, None] == brow) & (tn[:, None] == trow))
    put("upto_row", (bn[:, None] == brow) & (tn[:, None] <= trow))
    put("batch_of_row", bn[:, None] == brow)
    put("dec_after", (bn[:, None] == bn[None, :]) & (tn[:, None] > tn[None, :]))
    put("batch_of_token", bn[:, None] == np.arange(DB)[None, :])
    put("batch_to_row", np.arange(DB)[:, None] == brow)
    put("head_rows", np.arange(H)[:, None] == np.arange(BW)[None, :] // HD)
    table = np.concatenate([out[n] for n in out], axis=1)
    dist = (PT - 1) * P + p[:, None] - np.arange(SEQ)[None, :]
    alibi = np.stack([np.where(dist >= 0, -s * dist, NEG) for s in SLOPES], axis=1).astype(np.float32)
    return np.ascontiguousarray(table), at, split, np.ascontiguousarray(alibi)


TABLE, TABLE_AT, SPLIT, ALIBI = const_tables()
TABLE_W = TABLE.shape[1]


class Core:

    def __init__(self, nc, stack, io):
        self.nc, self.io, self.used = nc, io, []
        self.const = stack.enter_context(nc.sbuf_tensor("const", [P, SPLIT], F32))
        self.dec_const = None
        self.psum = stack.enter_context(nc.psum_tensor("psum", [P, 8, 512], F32))
        self.ps = [self.psum[:, i, :] for i in range(8)]
        self.xn_dram = nc.dram_tensor("xn_scratch", [NT * P, D], F32).ap()
        self.xt_dram = nc.dram_tensor("xt_scratch", [P, KD * T], F32).ap()
        self.br_dram = nc.dram_tensor("branch_scratch", [P, 6 * T], F32).ap()

    def c(self, name, n=P, lo=0, hi=None):
        a, b = TABLE_AT[name]
        if a >= SPLIT:
            return self.dec_const[0:n, a - SPLIT + lo:(b - SPLIT if hi is None else a - SPLIT + hi)]
        return self.const[0:n, a + lo:(b if hi is None else a + hi)]


def phase(k, tag, sbs, sems):
    nc, st = k.nc, ExitStack()
    b = {n: st.enter_context(nc.sbuf_tensor(f"{tag}_{n}", shape, I32 if n == "page_table" else F32)) for n, shape in sbs.items()}
    s = {n: nc.alloc_semaphore(f"{tag}_{n}") for n in sems}
    k.used += s.values()
    return st, b, s


def normalise_input(k, xt):
    nc, io = k.nc, k.io
    XB = NT
    st, b, s = phase(k, "ln_in", dict(
        x_in=[P, XB, D], ln_w=[P, D], ln_b=[P, D], lnw_col=[P, KD], lnb_col=[P, KD], x_norm=[P, 2, D],
        stats=[P, 12], mean_var=[P, NT, 2], var_eps=[P, NT], rstd=[P, NT]),
        ["const_loaded", "lnin_par", "stats_done", "mv_done", "ve_done", "rstd_done", "xhat_done", "xt_psum", "xt_done",
         "xscaled", "xnorm_done"] + [f"x_loaded{i}" for i in range(XB)] + [f"xnorm_stored{i}" for i in range(2)])
    groups = [(0, 4), (4, 4), (8, 1)]
    src = lambda t: io["x_prompt"][0, t * P:(t + 1) * P, :] if t < PT else io["x_sample"].rearrange("b t d -> (b t) d")
    with st, nc.Block() as block:
        @block.sync
        def _(sp):
            def load(t):
                sp.dma_start(b["x_in"][0:rows(t), t % XB, :], src(t)).then_inc(s[f"x_loaded{t % XB}"], 16)
            load(0)
            sp.dma_start(k.const[:, :], io["table"][:, 0:SPLIT]).then_inc(s["const_loaded"], 16)
            for t in range(1, 4):
                load(t)
            with nc.allow_non_contiguous_dma(reason="1024 values to columns"):
                sp.dma_start(b["lnw_col"][:, :], io["ln_in_w"].rearrange("(k p) -> p k", p=P)).then_inc(s["lnin_par"], 16)
                sp.dma_start(b["lnb_col"][:, :], io["ln_in_b"].rearrange("(k p) -> p k", p=P)).then_inc(s["lnin_par"], 16)
            sp.dma_start(b["ln_w"][:, :], io["ln_in_w"].partition_broadcast(P)).then_inc(s["lnin_par"], 16)
            sp.dma_start(b["ln_b"][:, :], io["ln_in_b"].partition_broadcast(P)).then_inc(s["lnin_par"], 16)
            for t in range(4, NT):
                load(t)
            for t in range(NT):
                sp.wait_ge(s["xnorm_done"], t + 1)
                sp.dma_start(k.xn_dram[t * P:t * P + rows(t), :], b["x_norm"][0:rows(t), t % 2, :]).then_inc(s[f"xnorm_stored{t % 2}"], 16)
            sp.wait_ge(s["xnorm_stored0"], 16 * ((NT + 1) // 2))
            sp.wait_ge(s["xnorm_stored1"], 16 * (NT // 2))

        @block.vector
        def _(dve):
            def statistics(t):
                r = rows(t)
                x = b["x_in"][0:r, t % XB, :]
                dve.wait_ge(s[f"x_loaded{t % XB}"], 16 * (t // XB + 1))
                nc.vector.bn_stats(b["stats"][0:r, 0:6], x[:, 0:512]).then_inc(s["stats_done"], 1)
                nc.vector.bn_stats(b["stats"][0:r, 6:12], x[:, 512:1024]).then_inc(s["stats_done"], 1)
                dve.wait_ge(s["stats_done"], 2 * t + 2)
                nc.vector.bn_aggr(b["mean_var"][0:r, t, :], b["stats"][0:r, :]).then_inc(s["mv_done"], 1)
                dve.wait_ge(s["mv_done"], t + 1)
                nc.vector.tensor_scalar(b["var_eps"][0:r, t:t + 1], b["mean_var"][0:r, t, 1:2], EPS, None, ALU.add).then_inc(s["ve_done"], 1)

            statistics(0)
            for t in range(NT):
                if t + 1 < NT:
                    statistics(t + 1)
                r = rows(t)
                x = b["x_in"][0:r, t % XB, :]
                dve.wait_ge(s["rstd_done"], t + 1)
                nc.vector.tensor_scalar(x, x, b["mean_var"][0:r, t, 0:1], b["rstd"][0:r, t:t + 1], ALU.subtract, ALU.mult).then_inc(s["xhat_done"], 1)

        @block.gpsimd
        def _(pool):
            pool.wait_ge(s["lnin_par"], 64)
            pool.wait_ge(s["const_loaded"], 16)

            def root(t):
                r = rows(t)
                pool.wait_ge(s["ve_done"], t + 1)
                nc.gpsimd.tensor_tensor(b["rstd"][0:r, t:t + 1], b["var_eps"][0:r, t:t + 1], k.c("minus_half", r, 0, 1), ALU.pow).then_inc(s["rstd_done"], 1)

            root(0)
            for t in range(NT):
                if t + 1 < NT:
                    root(t + 1)
                r = rows(t)
                xn = b["x_norm"][0:r, t % 2, :]
                pool.wait_ge(s["xhat_done"], t + 1)
                if t >= 2:
                    pool.wait_ge(s[f"xnorm_stored{t % 2}"], 16 * (t // 2))
                nc.gpsimd.tensor_tensor(xn, b["x_in"][0:r, t % XB, :], b["ln_w"][0:r, :], ALU.mult).then_inc(s["xscaled"], 1)
                pool.wait_ge(s["xscaled"], t + 1)
                nc.gpsimd.tensor_tensor(xn, xn, b["ln_b"][0:r, :], ALU.add).then_inc(s["xnorm_done"], 1)

        @block.tensor
        def _(pe):
            pe.wait_ge(s["const_loaded"], 16)
            n = 0
            for t0, cnt in groups:
                pe.wait_ge(s["xhat_done"], t0 + cnt)
                for kk in range(KD):
                    if n >= 8:
                        pe.wait_ge(s["xt_done"], n - 7)
                    for j in range(cnt):
                        r = rows(t0 + j)
                        mm = nc.tensor.transpose(k.ps[n % 8][:, j * P:j * P + r], b["x_in"][0:r, (t0 + j) % XB, kk * P:(kk + 1) * P], k.c("ident", r, 0, r))
                    mm.then_inc(s["xt_psum"], 1)
                    n += 1

        @block.scalar
        def _(act):
            act.wait_ge(s["lnin_par"], 64)
            n = 0
            for t0, cnt in groups:
                w = sum(rows(t0 + j) for j in range(cnt))
                for kk in range(KD):
                    act.wait_ge(s["xt_psum"], n + 1)
                    nc.scalar.activation(xt[:, kk, t0 * P:t0 * P + w], k.ps[n % 8][:, 0:w], ACT.Identity,
                                         bias=b["lnb_col"][:, kk:kk + 1], scale=b["lnw_col"][:, kk:kk + 1]).then_inc(s["xt_done"], 1)
                    n += 1


def project(k, xt, z, tb, zd, td):
    nc, io = k.nc, k.io
    nchunk = len(CHUNKS)
    st, b, s = phase(k, "proj", dict(
        w_chunk=[P, 2, KD, CW], bias_z=[P, C_GM], bias_q=[P, 6]),
        ["bias_loaded", "mm_done", "feat_done", "tok_done", "turned", "turn_copied", "pj_stored"] + [f"w_loaded{i}" for i in range(2)])
    units = []
    for ci, (feat, c0, w, _) in enumerate(CHUNKS):
        if feat:
            units += [(ci, blk, n) for blk in range(2) for n in range(3)]
        else:
            units += [(ci, -1, t) for t in range(NT)]
    last = {ci: max(u for u, x in enumerate(units) if x[0] == ci) for ci in range(nchunk)}
    evac = []
    cf = ct = 0
    for ci, blk, n in units:
        if CHUNKS[ci][0]:
            cf += 1
            evac.append(("feat_done", cf))
        else:
            ct += 1
            evac.append(("tok_done", ct))
    MB = 6
    turns = [("kcv", Z_KC), ("ksel", Z_KS), ("kwin", Z_KW), ("mk0", Z_MK), ("mk1", Z_MK + P), ("fk0", Z_FK), ("fk1", Z_FK + P)]
    tgroups = [(0, 4), (4, 4), (8, 1)]

    def zz(t, c0, c1):
        return z[:, t, c0:c1] if t < PT else zd[0:ND, 0, c0:c1]

    with st, nc.Block() as block:
        @block.sync
        def _(sp):
            def load(ci):
                _, c0, w, _ = CHUNKS[ci]
                if ci >= 2:
                    sp.wait_ge(s["mm_done"], last[ci - 2] + 1)
                sp.dma_start(b["w_chunk"][:, ci % 2, :, 0:w], io["w_in"][0].rearrange("(k p) n -> p k n", p=P)[:, :, c0:c0 + w]).then_inc(s[f"w_loaded{ci % 2}"], 16)
            load(0)
            with nc.allow_non_contiguous_dma(reason="bias columns"):
                for j, c0 in enumerate((C_NQ, C_MQ, C_FQ)):
                    sp.dma_start(b["bias_q"][:, 2 * j:2 * j + 2], io["b_in"][0, c0:c0 + 256].rearrange("(k p) -> p k", p=P)).then_inc(s["bias_loaded"], 16)
            sp.dma_start(b["bias_z"][:, :], io["b_in"][0, 0:C_GM].partition_broadcast(P)).then_inc(s["bias_loaded"], 16)
            for ci in range(1, nchunk):
                load(ci)
            sp.dma_start(k.xt_dram, xt[:, :, :].rearrange("p k t -> p (k t)")).then_inc(s["pj_stored"], 16)
            sp.wait_ge(s["tok_done"], ct)
            tok = lambda c0, c1, a=0, e=PT: z[:, a:e, c0:c1]
            dec = lambda c0, c1: zd[0:ND, 0, c0:c1]
            n = 1
            sp.dma_start(io["p_nsa_rows"].rearrange("x y (t p) r d -> (x y p) t (r d)", p=P), tok(0, 256)).then_inc(s["pj_stored"], 16)
            sp.dma_start(io["p_nsa_win"].rearrange("x y (t p) r d -> (x y p) t (r d)", p=P), tok(Z_KW, Z_KW + 128, 4, 8)).then_inc(s["pj_stored"], 16)
            sp.dma_start(io["p_fox_kv"].rearrange("x y (t p) r h d -> (x y p) t (r h d)", p=P), tok(Z_FK, Z_FK + 512)).then_inc(s["pj_stored"], 16)
            sp.dma_start(io["s_nsa_rows"].rearrange("x b t r d -> (x b t) (r d)"), dec(0, 256)).then_inc(s["pj_stored"], 16)
            sp.dma_start(io["s_fox_kv"].rearrange("x b t r h d -> (x b t) (r h d)"), dec(Z_FK, Z_FK + 512)).then_inc(s["pj_stored"], 16)
            n += 5
            win = io["s_nsa_win"].rearrange("x b c r d -> (x b) c (r d)")
            sp.dma_start(win[:, 0:PAST - DT, :], io["cache_nsa_win"].rearrange("x b c r d -> (x b) c (r d)")[:, DT:PAST, :]).then_inc(s["pj_stored"], 16)
            n += 1
            for bb in range(DB):
                sp.dma_start(win[bb, PAST - DT:PAST, :], zd[bb * DT:(bb + 1) * DT, 0, Z_KW:Z_KW + 128]).then_inc(s["pj_stored"], 16)
                n += 1
            sp.wait_ge(s["pj_stored"], 16 * n)

        @block.tensor
        def _(pe):
            for u, (ci, blk, n) in enumerate(units):
                w = CHUNKS[ci][2]
                if u == 0 or units[u - 1][0] != ci:
                    pe.wait_ge(s[f"w_loaded{ci % 2}"], 16 * (ci // 2 + 1))
                if u >= MB:
                    pe.wait_ge(s[evac[u - MB][0]], evac[u - MB][1])
                for kk in range(KD):
                    if blk >= 0:
                        a, m = NCH[n]
                        mm = nc.tensor.matmul(k.ps[u % MB][:, 0:m], b["w_chunk"][:, ci % 2, kk, blk * P:(blk + 1) * P], xt[:, kk, a:a + m],
                                              start=(kk == 0), stop=(kk == KD - 1))
                    else:
                        r = rows(n)
                        mm = nc.tensor.matmul(k.ps[u % MB][0:r, 0:w], xt[:, kk, n * P:n * P + r], b["w_chunk"][:, ci % 2, kk, 0:w],
                                              start=(kk == 0), stop=(kk == KD - 1))
                mm.then_inc(s["mm_done"], 1)
            pe.wait_ge(s["tok_done"], ct)
            n = 0
            for name, c0 in turns:
                for t0, cnt in tgroups:
                    if n >= 2:
                        pe.wait_ge(s["turn_copied"], n - 1)
                    for j in range(cnt):
                        r = rows(t0 + j)
                        mm = nc.tensor.transpose(k.ps[6 + n % 2][:, j * P:j * P + r], zz(t0 + j, c0, c0 + P), k.c("ident", r, 0, r))
                    mm.then_inc(s["turned"], 1)
                    n += 1

        @block.vector
        def _(dve):
            dve.wait_ge(s["bias_loaded"], 64)
            for u, (ci, blk, t) in enumerate(units):
                feat, c0, w, z0 = CHUNKS[ci]
                if feat:
                    continue
                r = rows(t)
                dve.wait_ge(s["mm_done"], u + 1)
                src, bias, dst = k.ps[u % MB][0:r, 0:w], b["bias_z"][0:r, c0:c0 + w], zz(t, z0, z0 + w)
                if c0 == C_MV:
                    src, bias = (a.rearrange("p (h d) -> p h d", h=H) for a in (src, bias))
                    dst = zz(t, z0, z0 + H * VW1).rearrange("p (h d) -> p h d", h=H)[:, :, 0:HD]
                nc.vector.tensor_tensor(dst, src, bias, ALU.add).then_inc(s["tok_done"], 1)

        @block.gpsimd
        def _(pool):
            for x in (z[:, :, Z_MV:Z_MV + H * VW1], zd[:, :, Z_MV:Z_MV + H * VW1]):
                nc.gpsimd.memset(x.rearrange("p t (h d) -> p t h d", h=H)[:, :, :, HD:VW1], 1.0)

        @block.scalar
        def _(act):
            act.wait_ge(s["bias_loaded"], 64)
            for u, (ci, blk, n) in enumerate(units):
                feat, c0, w, which = CHUNKS[ci]
                if not feat:
                    continue
                a, m = NCH[n]
                act.wait_ge(s["mm_done"], u + 1)
                name = ("nq", "mq", "fq")[which]
                dst = tb[name][:, blk, a:a + m] if n < 2 else td[name][:, blk, :]
                nc.scalar.activation(dst, k.ps[u % MB][:, 0:m], ACT.Identity, bias=b["bias_q"][:, 2 * which + blk:2 * which + blk + 1]).then_inc(s["feat_done"], 1)
            n = 0
            for name, c0 in turns:
                for t0, cnt in tgroups:
                    w = sum(rows(t0 + j) for j in range(cnt))
                    act.wait_ge(s["turned"], n + 1)
                    src = k.ps[6 + n % 2]
                    dst, a = (tb, t0 * P) if t0 < PT else (td, 0)
                    if name == "kcv" and t0 >= PT:
                        nc.scalar.copy(dst["kcv"][:, 0:w], src[:, 0:w]).then_inc(s["turn_copied"], 1)
                    elif name in ("ksel", "kwin"):
                        nc.scalar.mul(dst[name][0:HD, a:a + w], src[0:HD, 0:w], SCALE)
                        nc.scalar.mul(dst[name][HD:P, a:a + w], src[0:HD, 0:w], SCALE).then_inc(s["turn_copied"], 1)
                    elif name == "kcv":
                        nc.scalar.copy(dst[name][:, a:a + w], src[:, 0:w]).then_inc(s["turn_copied"], 1)
                    else:
                        nc.scalar.mul(dst[name[:2]][:, int(name[2]), a:a + w], src[:, 0:w], SCALE).then_inc(s["turn_copied"], 1)
                    n += 1


def log_sigmoid_and_gates(k, z, zd, a):
    nc, io = k.nc, k.io
    st, b, s = phase(k, "gates", dict(neg=[P, NT, 8], neg_abs=[P, NT, 8], softplus=[P, NT, 8], least=[P, NT, 8]),
                     ["neg_done", "na_done", "e_done", "sp_done", "least_done", "sc_done", "gate_exp", "gate_one", "gate_done", "logf_stored"])
    parts = [(P, 0, PT), (ND, PT, NT)]
    zz = lambda t0, c0, c1: z[:, :, c0:c1] if t0 < PT else zd[0:ND, :, c0:c1]
    with st, nc.Block() as block:
        @block.vector
        def _(dve):
            for r, t0, t1 in parts:
                for j, c0 in enumerate((Z_MF, Z_FF)):
                    x = zz(t0, c0, c0 + H)
                    nc.vector.tensor_scalar(b["neg"][0:r, t0:t1, 4 * j:4 * j + 4], x, -1.0, None, ALU.mult).then_inc(s["neg_done"], 1)
                    nc.vector.tensor_scalar(b["least"][0:r, t0:t1, 4 * j:4 * j + 4], x, 0.0, None, ALU.min).then_inc(s["least_done"], 1)
                nc.vector.tensor_copy(a["sc"][0:r, t0:t1, 0:4], zz(t0, Z_MI, Z_MI + H))
            dve.wait_ge(s["least_done"], 4)
            dve.wait_ge(s["neg_done"], 4)
            for r, t0, t1 in parts:
                for j, c0 in enumerate((Z_MF, Z_FF)):
                    c = slice(4 * j, 4 * j + 4)
                    nc.vector.tensor_tensor(b["neg_abs"][0:r, t0:t1, c], zz(t0, c0, c0 + H), b["neg"][0:r, t0:t1, c], ALU.min).then_inc(s["na_done"], 1)
            dve.wait_ge(s["sp_done"], 2)
            for r, t0, t1 in parts:
                nc.vector.tensor_tensor(a["sc"][0:r, t0:t1, 4:12], b["least"][0:r, t0:t1, :], b["softplus"][0:r, t0:t1, :], ALU.subtract).then_inc(s["sc_done"], 1)
            n = 0
            for c0, w in ((Z_NG, 12), (Z_MO, BW)):
                for r, t0, t1 in parts:
                    x = zz(t0, c0, c0 + w)
                    n += 1
                    dve.wait_ge(s["gate_exp"], n)
                    nc.vector.tensor_scalar(x, x, 1.0, None, ALU.add).then_inc(s["gate_one"], 1)
                    dve.wait_ge(s["gate_one"], n)
                    nc.vector.reciprocal(x, x).then_inc(s["gate_done"], 1)

        @block.scalar
        def _(act):
            act.wait_ge(s["na_done"], 4)
            for r, t0, t1 in parts:
                nc.scalar.activation(b["neg_abs"][0:r, t0:t1, :], b["neg_abs"][0:r, t0:t1, :], ACT.Exp).then_inc(s["e_done"], 1)
            act.wait_ge(s["e_done"], 2)
            for r, t0, t1 in parts:
                nc.scalar.activation(b["softplus"][0:r, t0:t1, :], b["neg_abs"][0:r, t0:t1, :], ACT.Ln, bias=1.0).then_inc(s["sp_done"], 1)
            for c0, w in ((Z_NG, 12), (Z_MO, BW)):
                for r, t0, t1 in parts:
                    x = zz(t0, c0, c0 + w)
                    nc.scalar.activation(x, x, ACT.Exp, scale=-1.0).then_inc(s["gate_exp"], 1)

        @block.sync
        def _(sp):
            sp.wait_ge(s["sc_done"], 2)
            sp.dma_start(io["p_fox_logf"].rearrange("x y (t p) h -> (x y p) t h", p=P), a["sc"][:, 0:PT, 8:12]).then_inc(s["logf_stored"], 16)
            sp.dma_start(io["s_fox_logf"].rearrange("x b t h -> (x b t) h"), a["sc"][0:ND, PT, 8:12]).then_inc(s["logf_stored"], 16)
            sp.wait_ge(s["logf_stored"], 32)


def prompt_setup(k, z, tb, a):
    nc, io = k.nc, k.io
    st, b, s = phase(k, "setup", dict(
        sums=[P, PT, 8], neg_f=[P, PT, H], u_rows=[H, SEQ], f_rows=[H, SEQ], cm_rows=[H, SEQ], m_tok=[P, PT, H],
        w_state=[P, PT, H], w_cmp=[P, BLK, HD], state=[HD, H, VW1]),
        ["sums_mm", "sums_done", "u_done", "f_done", "rows_mm", "rows_done", "cm_done", "bc_mm", "bc_done", "cmt_mm", "m_done",
         "ws_arg", "ws_exp", "ws_done", "kw_done", "state_mm", "state_done", "wc_loaded", "kc_mm", "vc_mm", "cmp_zero",
         "setup_stored"])
    sc = a["sc"]
    with st, nc.Block() as block:
        @block.sync
        def _(sp):
            sp.dma_start(b["w_cmp"][0:HD], io["nsa_w_ck"][0].rearrange("p d e -> d p e")).then_inc(s["wc_loaded"], 16)
            sp.dma_start(b["w_cmp"][HD:P], io["nsa_w_cv"][0].rearrange("p d e -> d p e")).then_inc(s["wc_loaded"], 16)
            sp.wait_ge(s["m_done"], 1)
            sp.dma_start(io["p_mlstm_m"].rearrange("x y h -> (x y) h"), b["m_tok"][P - 1:P, PT - 1, :]).then_inc(s["setup_stored"], 16)
            sp.wait_ge(s["state_done"], H)
            sp.dma_start(io["p_mlstm_c"].rearrange("x y h d e -> (x y d) h e"), b["state"][:, :, 0:HD]).then_inc(s["setup_stored"], 16)
            with nc.allow_non_contiguous_dma(reason="the normaliser is a column of the state"):
                sp.dma_start(io["p_mlstm_n"].rearrange("x y h d -> (x y d) h"), b["state"][:, :, HD]).then_inc(s["setup_stored"], 16)
            sp.wait_ge(s["setup_stored"], 48)

        @block.tensor
        def _(pe):
            for i in range(PT):
                for j in range(i + 1):
                    lhs = k.c("upto") if j == 0 else k.c("ones")
                    rhs = sc[:, i if j == 0 else j - 1, 4:12]
                    mm = nc.tensor.matmul(k.ps[0][:, 8 * i:8 * i + 8], lhs, rhs, start=(j == 0), stop=(j == i))
            mm.then_inc(s["sums_mm"], 1)
            pe.wait_ge(s["wc_loaded"], 32)
            for p in range(BLK):
                mm = nc.tensor.matmul(k.ps[6][0:HD, 0:NCB], b["w_cmp"][0:HD, p, :], tb["kcv"][0:HD, p:SEQ:BLK], start=(p == 0), stop=(p == BLK - 1))
            mm.then_inc(s["kc_mm"], 1)
            for p in range(BLK):
                mm = nc.tensor.matmul(k.ps[7][0:NCB, 0:HD], tb["kcv"][HD:P, p:SEQ:BLK], b["w_cmp"][HD:P, p, :], start=(p == 0), stop=(p == BLK - 1))
            mm.then_inc(s["vc_mm"], 1)
            pe.wait_ge(s["u_done"], 1)
            pe.wait_ge(s["f_done"], 1)
            for n, src in enumerate((a["u"], b["neg_f"])):
                for i in range(PT):
                    mm = nc.tensor.transpose(k.ps[1 + 2 * n + i // 4][0:H, i % 4 * P:i % 4 * P + P], src[:, i, :], k.c("ident"))
                mm.then_inc(s["rows_mm"], 1)
            pe.wait_ge(s["cm_done"], 1)
            for i in range(PT):
                mm = nc.tensor.transpose(k.ps[5][:, 4 * i:4 * i + 4], b["cm_rows"][:, i * P:(i + 1) * P], k.c("ident", H, 0, H))
            mm.then_inc(s["cmt_mm"], 1)
            pe.wait_ge(s["rows_done"], 4)
            n = 0
            for src in (b["cm_rows"], b["f_rows"]):
                for h in range(H):
                    for half in range(2):
                        if n >= 4:
                            pe.wait_ge(s["bc_done"], n - 3)
                        nc.tensor.matmul(k.ps[1 + n % 4][:, :], k.c("head_bcast", H, h * P, (h + 1) * P), src[:, half * 512:(half + 1) * 512],
                                         start=True, stop=True).then_inc(s["bc_mm"], 1)
                        n += 1
            pe.wait_ge(s["kw_done"], PT)
            for h in range(H):
                if h == 0:
                    pe.wait_ge(s["sums_done"], 1)
                if h == 1:
                    pe.wait_ge(s["m_done"], 1)
                bank = k.ps[(0, 5)[h % 2]]
                if h >= 2:
                    pe.wait_ge(s["state_done"], h - 1)
                for j in range(PT):
                    mm = nc.tensor.matmul(bank[0:HD, 0:VW1], z[:, j, Z_MK + h * HD:Z_MK + (h + 1) * HD],
                                          z[:, j, Z_MV + h * VW1:Z_MV + (h + 1) * VW1], start=(j == 0), stop=(j == PT - 1))
                mm.then_inc(s["state_mm"], 1)

        @block.vector
        def _(dve):
            dve.wait_ge(s["sums_mm"], 1)
            nc.vector.tensor_copy(b["sums"][:, :, :], k.ps[0][:, 0:64].rearrange("p (t c) -> p t c", t=PT)).then_inc(s["sums_done"], 1)
            dve.wait_ge(s["sums_done"], 1)
            nc.vector.tensor_tensor(a["u"][:, :, :], sc[:, 0:PT, 0:4], b["sums"][:, :, 0:4], ALU.subtract).then_inc(s["u_done"], 1)
            nc.vector.tensor_scalar(b["neg_f"][:, :, :], b["sums"][:, :, 4:8], -1.0, None, ALU.mult).then_inc(s["f_done"], 1)
            nc.vector.memset(a["kc"][:, :], 0.0).then_inc(s["cmp_zero"], 1)
            nc.vector.memset(a["vc"][:, :], 0.0).then_inc(s["cmp_zero"], 1)
            dve.wait_ge(s["cmp_zero"], 2)
            dve.wait_ge(s["kc_mm"], 1)
            dve.wait_ge(s["vc_mm"], 1)
            for half in range(2):
                nc.vector.tensor_scalar(a["kc"][half * HD:(half + 1) * HD, 0:NCB], k.ps[6][0:HD, 0:NCB], SCALE, None, ALU.mult)
            for h in range(H):
                nc.vector.tensor_copy(a["vc"][32 * h:32 * h + NCB, h * HD:(h + 1) * HD], k.ps[7][0:NCB, 0:HD])
            dve.wait_ge(s["rows_mm"], 2)
            for n, dst in enumerate((b["u_rows"], b["f_rows"])):
                for half in range(2):
                    nc.vector.tensor_copy(dst[:, half * 512:(half + 1) * 512], k.ps[1 + 2 * n + half][0:H, :]).then_inc(s["rows_done"], 1)
            dve.wait_ge(s["rows_done"], 2)
            nc.vector.tensor_tensor_scan(b["cm_rows"][:, :], b["u_rows"][:, :], b["u_rows"][:, :], 0.0, ALU.max, ALU.max).then_inc(s["cm_done"], 1)
            dve.wait_ge(s["cmt_mm"], 1)
            nc.vector.tensor_tensor(b["m_tok"][:, :, :], k.ps[5][:, 0:32].rearrange("p (t c) -> p t c", t=PT), b["sums"][:, :, 0:4], ALU.add).then_inc(s["m_done"], 1)
            dve.wait_ge(s["bc_done"], 8)
            nc.vector.tensor_tensor(b["w_state"][:, :, :], a["u"][:, :, :],
                                    a["cm"][:, :, SEQ - 1].unsqueeze(1).to_broadcast([P, PT, H]), ALU.add).then_inc(s["ws_arg"], 1)
            dve.wait_ge(s["ws_exp"], 1)
            nc.vector.tensor_scalar(b["w_state"][:, :, :], b["w_state"][:, :, :], SCALE, None, ALU.mult).then_inc(s["ws_done"], 1)
            dve.wait_ge(s["ws_done"], 1)
            for j in range(PT):
                kk = z[:, j, Z_MK:Z_MK + BW].rearrange("p (h d) -> p h d", h=H)
                nc.vector.tensor_tensor(kk, kk, b["w_state"][:, j, :].unsqueeze(2).to_broadcast([P, H, HD]), ALU.mult).then_inc(s["kw_done"], 1)
            for h in range(H):
                dve.wait_ge(s["state_mm"], h + 1)
                nc.vector.tensor_copy(b["state"][:, h, :], k.ps[(0, 5)[h % 2]][0:HD, 0:VW1]).then_inc(s["state_done"], 1)

        @block.scalar
        def _(act):
            n = 0
            for sign, dst in ((-1.0, a["cm"]), (1.0, a["fneg"])):
                for h in range(H):
                    for half in range(2):
                        act.wait_ge(s["bc_mm"], n + 1)
                        nc.scalar.mul(dst[:, h, half * 512:(half + 1) * 512], k.ps[1 + n % 4][:, :], sign).then_inc(s["bc_done"], 1)
                        n += 1
                        if n == 8:
                            act.wait_ge(s["ws_arg"], 1)
                            nc.scalar.activation(b["w_state"][:, :, :], b["w_state"][:, :, :], ACT.Exp).then_inc(s["ws_exp"], 1)
            act.wait_ge(s["m_done"], 1)
            nc.scalar.activation(a["exp_neg_m"][:, :, :], b["m_tok"][:, :, :], ACT.Exp, scale=-1.0)


def prompt_attention(k, z, tb, a):
    nc, io = k.nc, k.io
    st, b, s = phase(k, "attn", dict(
        scores=[P, 2, SEQ], probs_t=[P, 2, SEQ], alibi=[P, H, SEQ], neg_max=[P, 2], row_max=[P, 2], row_sum=[P, 4], gate=[P, 2],
        br=[P, 2, 3 * BW], br_t=[P, 6, P], cmp_s=[P, H, 32], cmp_t=[P, P], cmp_max=[P, H], cmp_sum=[P, H],
        ml_stats=[P, H, 6], ml_mv=[P, H, 2], ml_ve=[P, H], ml_rstd=[P, H], norm_w=[P, BW]),
        ["alibi_loaded", "scores_mm", "biased", "max_negated", "exped", "masked", "weighted", "turned", "turn_copied", "pv_mm",
         "den_neg", "sum_floor", "sum_inv", "gated", "out_done", "cmp_even", "cmp_mm", "cmp_biased", "cmp_max_done", "cmp_floor", "cmp_shift", "cmp_exp",
         "cmp_sum_done", "cmp_sum_floor", "cmp_inv", "cmp_gate", "cmp_p", "cmp_turned", "cmp_copied", "cmp_pv", "cmp_out",
         "ml_stat", "ml_agg", "ml_ve_done", "ml_rs", "ml_normed", "tile_done", "br_turned", "br_copied", "br_stored"])
    KINDS = ["fox", "ml", "sel", "win"]
    units = [(kind, h, i) for i in range(PT) for kind in KINDS for h in range(H)]
    PER_TILE = len(KINDS) * H
    N = len(units)

    def nblk(u):
        kind, h, i = units[u]
        return min(i + 1, WIN // P + 1) if kind == "win" else i + 1

    def first(u):
        return units[u][2] + 1 - nblk(u)

    halves = []
    for u in range(N):
        if units[u][0] != "ml":
            halves += [(u, x, min(4, nblk(u) - x)) for x in range(0, nblk(u), 4)]
    upto_half = lambda u: sum(1 for x in halves if x[0] <= u)
    ml_upto = lambda u: sum(1 for x in units[:u + 1] if x[0] == "ml")
    sm_upto = lambda u: u + 1 - ml_upto(u)
    hrow = lambda h: (h % 2) * HD

    ring, ring_at = [], {}

    def use(key, sem, value):
        ring_at[key] = len(ring)
        ring.append((sem, value))

    for v in range(N + 2):
        if 1 <= v <= N:
            for q, x in enumerate(halves):
                if x[0] == v - 1:
                    use(("half", q), "turn_copied", q + 1)
        i, x = v // PER_TILE, v % PER_TILE
        if i < PT:
            if x == 0:
                use(("cmp_s", i), "cmp_biased", i + 1)
            if x == 3:
                use(("cmp_t", i), "cmp_copied", i + 1)
            if x == 5:
                use(("cmp_v", i), "cmp_out", i + 1)
            if i >= 1 and x in (6, 8):
                use(("br", 2 * (i - 1) + (x - 6) // 2), "br_copied", 2 * (i - 1) + (x - 6) // 2 + 1)
    for r in range(2):
        use(("br", 2 * (PT - 1) + r), "br_copied", 2 * (PT - 1) + r + 1)

    def bank_of(key):
        return k.ps[4 + ring_at[key] % 2]

    def bank_free(pe, key):
        n = ring_at[key]
        if n >= 2:
            pe.wait_ge(s[ring[n - 2][0]], ring[n - 2][1])
        return k.ps[4 + n % 2]

    with st, nc.Block() as block:
        @block.sync
        def _(sp):
            sp.dma_start(b["alibi"][:, :, :], io["alibi"]).then_inc(s["alibi_loaded"], 16)
            sp.dma_start(b["norm_w"][:, :], io["mlstm_norm_w"][0].partition_broadcast(P)).then_inc(s["alibi_loaded"], 16)
            for i in range(PT):
                sp.wait_ge(s["br_copied"], 2 * (i + 1))
                sp.dma_start(k.br_dram.rearrange("p (c t) -> p c t", c=6)[:, :, i * P:(i + 1) * P], b["br_t"][:, :, :]).then_inc(s["br_stored"], 16)
            sp.wait_ge(s["br_stored"], 16 * PT)

        @block.tensor
        def _(pe):
            def scores(u):
                kind, h, i = units[u]
                if u >= 2:
                    pe.wait_ge(s["biased"], u - 1)
                    if units[u - 2][0] == "ml":
                        pe.wait_ge(s["weighted"], ml_upto(u - 2))
                bank = k.ps[2 * (u % 2):2 * (u % 2) + 2]
                hr, nb, f = hrow(h), nblk(u), first(u)
                if kind == "ml":
                    q = tb["mq"][hr:hr + HD, h // 2, i * P:(i + 1) * P]
                    for x in range(nb):
                        mm = nc.tensor.matmul(bank[x // 4][:, x % 4 * P:x % 4 * P + P], tb["mk"][hr:hr + HD, h // 2, x * P:(x + 1) * P], q, start=True, stop=True)
                else:
                    q = tb["fq" if kind == "fox" else "nq"][hr:hr + HD, h // 2, i * P:(i + 1) * P]
                    key = tb["fk"][hr:hr + HD, h // 2] if kind == "fox" else tb["k" + kind][hr:hr + HD]
                    masks = {nb - 1: "mask_future"} if kind == "fox" else {0: "mask_window"} if kind == "win" and nb > WIN // P else {}
                    x = 0
                    while x < nb:
                        e = x + 1
                        while x not in masks and e < nb and e not in masks and e % 4:
                            e += 1
                        out = bank[x // 4][:, x % 4 * P:(x % 4 + e - x) * P]
                        mm = nc.tensor.matmul(out, q, key[:, (f + x) * P:(f + e) * P], start=True, stop=x not in masks)
                        if x in masks:
                            mm = nc.tensor.matmul(out, k.c("ident"), k.c(masks[x]), start=False, stop=True)
                        x = e
                mm.then_inc(s["scores_mm"], 1)

            def turn(u):
                if units[u][0] == "ml":
                    return
                pe.wait_ge(s["exped"], u + 1)
                for q, (uu, x, w) in enumerate(halves):
                    if uu != u:
                        continue
                    bank = bank_free(pe, ("half", q))
                    for y in range(w):
                        mm = nc.tensor.transpose(bank[:, y * P:(y + 1) * P], b["scores"][:, u % 2, (x + y) * P:(x + y + 1) * P], k.c("ident"))
                    mm.then_inc(s["turned"], 1)

            def values(u):
                kind, h, i = units[u]
                if kind == "ml":
                    pe.wait_ge(s["weighted"], ml_upto(u))
                else:
                    pe.wait_ge(s["turn_copied"], upto_half(u))
                if u >= 2:
                    pe.wait_ge(s["out_done"], u - 1)
                c0 = {"ml": Z_MV + h * VW1, "fox": Z_FV + h * HD, "sel": Z_VS, "win": Z_VW}[kind]
                w = VW1 if kind == "ml" else HD
                for x in range(nblk(u)):
                    mm = nc.tensor.matmul(k.ps[6 + u % 2][:, 0:w], b["probs_t"][:, u % 2, x * P:(x + 1) * P], z[:, first(u) + x, c0:c0 + w],
                                          start=(x == 0), stop=(x == nblk(u) - 1))
                mm.then_inc(s["pv_mm"], 1)

            def cmp_scores(i):
                bank = bank_free(pe, ("cmp_s", i))
                for h in (0, 2, 1, 3):
                    hr = hrow(h)
                    if h == 1:
                        mm.then_inc(s["cmp_even"], 1)
                        pe.wait_ge(s["cmp_even"], i + 1)
                    mm = nc.tensor.matmul(bank[:, 32 * h:32 * h + 32], tb["nq"][hr:hr + HD, h // 2, i * P:(i + 1) * P], a["kc"][hr:hr + HD, :], start=True, stop=True)
                mm.then_inc(s["cmp_mm"], 1)

            def cmp_turn(i):
                pe.wait_ge(s["cmp_p"], i + 1)
                nc.tensor.transpose(bank_free(pe, ("cmp_t", i))[:, 0:P], b["cmp_s"][:, :, :].rearrange("p h j -> p (h j)"), k.c("ident")).then_inc(s["cmp_turned"], 1)

            def cmp_values(i):
                pe.wait_ge(s["cmp_copied"], i + 1)
                nc.tensor.matmul(bank_free(pe, ("cmp_v", i))[:, 0:BW], b["cmp_t"][:, :], a["vc"][:, :], start=True, stop=True).then_inc(s["cmp_pv"], 1)

            def branch_turn(i, r):
                if r == 0:
                    pe.wait_ge(s["tile_done"], i + 1)
                bank = bank_free(pe, ("br", 2 * i + r))
                for x in range(4 if r == 0 else 2):
                    mm = nc.tensor.transpose(bank[:, x * P:(x + 1) * P], b["br"][:, i % 2, (4 * r + x) * P:(4 * r + x + 1) * P], k.c("ident"))
                mm.then_inc(s["br_turned"], 1)

            for v in range(N + 2):
                if v < N:
                    scores(v)
                if 1 <= v <= N:
                    turn(v - 1)
                if v >= 2:
                    values(v - 2)
                i, x = v // PER_TILE, v % PER_TILE
                if i < PT:
                    if x == 0:
                        cmp_scores(i)
                    if x == 3:
                        cmp_turn(i)
                    if x == 5:
                        cmp_values(i)
                if i >= 1 and x in (6, 8) and i < PT:
                    branch_turn(i - 1, (x - 6) // 2)
            for r in range(2):
                branch_turn(PT - 1, r)

        @block.vector
        def _(dve):
            def bias(u):
                kind, h, i = units[u]
                w, f = nblk(u) * P, first(u)
                dve.wait_ge(s["scores_mm"], u + 1)
                if u >= 2:
                    if units[u - 2][0] == "ml":
                        dve.wait_ge(s["weighted"], ml_upto(u - 2))
                    else:
                        dve.wait_ge(s["turned"], upto_half(u - 2))
                dst = b["scores"][:, u % 2, 0:w]
                if kind == "ml":
                    nc.vector.tensor_tensor(dst.rearrange("p (j q) -> p j q", q=P), a["cm"][:, h, i * P:(i + 1) * P].unsqueeze(1).to_broadcast([P, nblk(u), P]),
                                            a["u"][:, 0:nblk(u), h:h + 1].to_broadcast([P, nblk(u), P]), ALU.add).then_inc(s["masked"], 1)
                    dve.wait_ge(s["masked"], ml_upto(u))
                    last = b["scores"][:, u % 2, w - P:w]
                    nc.vector.tensor_tensor(last, last, k.c("mask_future_t"), ALU.add).then_inc(s["biased"], 1)
                    return
                mx = b["row_max"][:, u % 2:u % 2 + 1]
                if kind == "fox":
                    add = a["fneg"][:, h, 0:w]
                else:
                    add = b["alibi"][:, h, SEQ - w:SEQ]
                src = k.psum[:, 2 * (u % 2):2 * (u % 2) + 2, :].rearrange("p b c -> p (b c)")[:, 0:w]
                nc.vector.tensor_tensor_reduce(dst, src, add, 1.0, -3e38, ALU.add, ALU.max, mx).then_inc(s["biased"], 1)
                dve.wait_ge(s["biased"], u + 1)
                nc.vector.tensor_scalar(b["neg_max"][:, u % 2:u % 2 + 1], mx, -1.0, None, ALU.mult).then_inc(s["max_negated"], 1)

            def weight(u):
                if units[u][0] != "ml":
                    return
                w = nblk(u) * P
                dve.wait_ge(s["exped"], u + 1)
                if u >= 2:
                    dve.wait_ge(s["pv_mm"], u - 1)
                src = k.psum[:, 2 * (u % 2):2 * (u % 2) + 2, :].rearrange("p b c -> p (b c)")[:, 0:w]
                nc.vector.tensor_tensor(b["probs_t"][:, u % 2, 0:w], src, b["scores"][:, u % 2, 0:w], ALU.mult).then_inc(s["weighted"], 1)

            def output(u):
                kind, h, i = units[u]
                sl = slice(u % 4, u % 4 + 1)
                if kind == "ml":
                    dve.wait_ge(s["pv_mm"], u + 1)
                    den = k.ps[6 + u % 2][:, HD:VW1]
                    nc.vector.tensor_scalar(b["row_sum"][:, sl], den, -1.0, None, ALU.mult).then_inc(s["den_neg"], 1)
                    dve.wait_ge(s["den_neg"], ml_upto(u))
                    nc.vector.scalar_tensor_tensor(b["row_sum"][:, sl], den, a["exp_neg_m"][:, i, h:h + 1], b["row_sum"][:, sl], ALU.max, ALU.max).then_inc(s["sum_floor"], 1)
                else:
                    dve.wait_ge(s["exped"], u + 1)
                    nc.vector.tensor_scalar(b["row_sum"][:, sl], b["row_sum"][:, sl], TINY, None, ALU.max).then_inc(s["sum_floor"], 1)
                dve.wait_ge(s["sum_floor"], u + 1)
                nc.vector.reciprocal(b["row_sum"][:, sl], b["row_sum"][:, sl]).then_inc(s["sum_inv"], 1)
                dve.wait_ge(s["sum_inv"], u + 1)
                dve.wait_ge(s["pv_mm"], u + 1)
                pv = k.ps[6 + u % 2][:, 0:HD]
                r = b["row_sum"][:, sl]
                if kind == "ml":
                    nc.vector.scalar_tensor_tensor(b["br"][:, i % 2, BW + h * HD:BW + (h + 1) * HD], pv, r, z[:, i, Z_MO + h * HD:Z_MO + (h + 1) * HD], ALU.mult, ALU.mult).then_inc(s["out_done"], 1)
                elif kind == "fox":
                    if h == 0 and i >= 2:
                        dve.wait_ge(s["br_turned"], 2 * (i - 1))
                    nc.vector.tensor_scalar(b["br"][:, i % 2, 2 * BW + h * HD:2 * BW + (h + 1) * HD], pv, r, None, ALU.mult).then_inc(s["out_done"], 1)
                else:
                    g = Z_NG + 3 * h + (1 if kind == "sel" else 2)
                    nc.vector.tensor_tensor(b["gate"][:, u % 2:u % 2 + 1], r, z[:, i, g:g + 1], ALU.mult).then_inc(s["gated"], 1)
                    dve.wait_ge(s["gated"], sum(1 for x in units[:u + 1] if x[0] in ("sel", "win")))
                    dst = b["br"][:, i % 2, h * HD:(h + 1) * HD]
                    dve.wait_ge(s["cmp_out"], i + 1)
                    if kind == "win":
                        dve.wait_ge(s["out_done"], u - H + 1)
                    nc.vector.scalar_tensor_tensor(dst, pv, b["gate"][:, u % 2:u % 2 + 1], dst, ALU.mult, ALU.add).then_inc(s["out_done"], 1)

            def cmp_weights(i, step):
                cs = b["cmp_s"]
                bc = lambda t: t[:, :].unsqueeze(2).to_broadcast([P, H, 32])
                if step == 0:
                    dve.wait_ge(s["cmp_mm"], i + 1)
                    if i >= 1:
                        dve.wait_ge(s["cmp_turned"], i)
                    nc.vector.tensor_tensor(cs[:, :, :], bank_of(("cmp_s", i))[:, 0:P].rearrange("p (h j) -> p h j", h=H),
                                            k.c("cmp_bias", P, i * P, (i + 1) * P).rearrange("p (h j) -> p h j", h=H), ALU.add).then_inc(s["cmp_biased"], 1)
                    dve.wait_ge(s["cmp_biased"], i + 1)
                    nc.vector.tensor_reduce(b["cmp_max"][:, :], cs[:, :, :], AX.X, ALU.max).then_inc(s["cmp_max_done"], 1)
                    dve.wait_ge(s["cmp_max_done"], i + 1)
                    nc.vector.tensor_scalar(b["cmp_max"][:, :], b["cmp_max"][:, :], FLOOR, None, ALU.max).then_inc(s["cmp_floor"], 1)
                    dve.wait_ge(s["cmp_floor"], i + 1)
                    nc.vector.tensor_tensor(cs[:, :, :], cs[:, :, :], bc(b["cmp_max"]), ALU.subtract).then_inc(s["cmp_shift"], 1)
                else:
                    dve.wait_ge(s["cmp_exp"], i + 1)
                    nc.vector.tensor_reduce(b["cmp_sum"][:, :], cs[:, :, :], AX.X, ALU.add).then_inc(s["cmp_sum_done"], 1)
                    dve.wait_ge(s["cmp_sum_done"], i + 1)
                    nc.vector.tensor_scalar(b["cmp_sum"][:, :], b["cmp_sum"][:, :], TINY, None, ALU.max).then_inc(s["cmp_sum_floor"], 1)
                    dve.wait_ge(s["cmp_sum_floor"], i + 1)
                    nc.vector.reciprocal(b["cmp_sum"][:, :], b["cmp_sum"][:, :]).then_inc(s["cmp_inv"], 1)
                    dve.wait_ge(s["cmp_inv"], i + 1)
                    nc.vector.tensor_tensor(b["cmp_sum"][:, :], b["cmp_sum"][:, :], z[:, i, Z_NG:Z_NG + 3 * H:3], ALU.mult).then_inc(s["cmp_gate"], 1)
                    dve.wait_ge(s["cmp_gate"], i + 1)
                    nc.vector.tensor_tensor(cs[:, :, :], cs[:, :, :], bc(b["cmp_sum"]), ALU.mult).then_inc(s["cmp_p"], 1)

            def cmp_output(i):
                dve.wait_ge(s["cmp_pv"], i + 1)
                if i >= 2:
                    dve.wait_ge(s["br_turned"], 2 * (i - 1))
                nc.vector.tensor_copy(b["br"][:, i % 2, 0:BW], bank_of(("cmp_v", i))[:, 0:BW]).then_inc(s["cmp_out"], 1)

            def mlstm_norm(i):
                dve.wait_ge(s["out_done"], i * PER_TILE + 2 * H)
                y = b["br"][:, i % 2, BW:2 * BW].rearrange("p (h d) -> p h d", h=H)
                for h in range(H):
                    nc.vector.bn_stats(b["ml_stats"][:, h, :], y[:, h, :]).then_inc(s["ml_stat"], 1)
                dve.wait_ge(s["ml_stat"], H * (i + 1))
                for h in range(H):
                    nc.vector.bn_aggr(b["ml_mv"][:, h, :], b["ml_stats"][:, h, :]).then_inc(s["ml_agg"], 1)
                dve.wait_ge(s["ml_agg"], H * (i + 1))
                nc.vector.tensor_scalar(b["ml_ve"][:, :], b["ml_mv"][:, :, 1], EPS, None, ALU.add).then_inc(s["ml_ve_done"], 1)
                dve.wait_ge(s["ml_rs"], i + 1)
                for h in range(H):
                    nc.vector.tensor_scalar(y[:, h, :], y[:, h, :], b["ml_mv"][:, h, 0:1], b["ml_rstd"][:, h:h + 1], ALU.subtract, ALU.mult).then_inc(s["ml_normed"], 1)
                dve.wait_ge(s["ml_normed"], H * (i + 1))
                yy = b["br"][:, i % 2, BW:2 * BW]
                nc.vector.tensor_tensor(yy, yy, b["norm_w"][:, :], ALU.mult).then_inc(s["tile_done"], 1)

            dve.wait_ge(s["alibi_loaded"], 32)
            for v in range(N + 2):
                i, x = v // PER_TILE, v % PER_TILE
                if i < PT:
                    if x == 1:
                        cmp_weights(i, 0)
                    if x == 3:
                        cmp_weights(i, 1)
                    if x == 6:
                        cmp_output(i)
                if v < N:
                    bias(v)
                if 1 <= v <= N:
                    weight(v - 1)
                if v >= 2:
                    output(v - 2)
                if v >= 2 and (v - 2) % PER_TILE == PER_TILE - 1:
                    mlstm_norm((v - 2) // PER_TILE)

        @block.gpsimd
        def _(pool):
            for i in range(PT):
                pool.wait_ge(s["ml_ve_done"], i + 1)
                nc.gpsimd.tensor_tensor(b["ml_rstd"][:, :], b["ml_ve"][:, :], k.c("minus_half", P, 0, H), ALU.pow).then_inc(s["ml_rs"], 1)

        @block.scalar
        def _(act):
            def exponent(u):
                w = nblk(u) * P
                row = b["scores"][:, u % 2, 0:w]
                if units[u][0] == "ml":
                    act.wait_ge(s["biased"], u + 1)
                    nc.scalar.activation(row, row, ACT.Exp).then_inc(s["exped"], 1)
                else:
                    act.wait_ge(s["max_negated"], sm_upto(u))
                    if u >= 4:
                        act.wait_ge(s["out_done"], u - 3)
                    nc.scalar.activation(row, row, ACT.Exp, bias=b["neg_max"][:, u % 2:u % 2 + 1], accum_out=b["row_sum"][:, u % 4:u % 4 + 1]).then_inc(s["exped"], 1)

            def copy_turned(u):
                if u >= 2:
                    act.wait_ge(s["pv_mm"], u - 1)
                for q, (uu, x, w) in enumerate(halves):
                    if uu == u:
                        act.wait_ge(s["turned"], q + 1)
                        nc.scalar.copy(b["probs_t"][:, u % 2, x * P:(x + w) * P], bank_of(("half", q))[:, 0:w * P]).then_inc(s["turn_copied"], 1)

            def branch_copy(i, r):
                act.wait_ge(s["br_turned"], 2 * i + r + 1)
                if i >= 1 and r == 0:
                    act.wait_ge(s["br_stored"], 16 * i)
                w = 4 if r == 0 else 2
                nc.scalar.copy(b["br_t"][:, 4 * r:4 * r + w, :], bank_of(("br", 2 * i + r))[:, 0:w * P].rearrange("p (c t) -> p c t", c=w)).then_inc(s["br_copied"], 1)

            for v in range(N + 2):
                i, x = v // PER_TILE, v % PER_TILE
                if i < PT and x == 4:
                    act.wait_ge(s["cmp_turned"], i + 1)
                    if i >= 1:
                        act.wait_ge(s["cmp_pv"], i)
                    nc.scalar.copy(b["cmp_t"][:, :], bank_of(("cmp_t", i))[:, 0:P]).then_inc(s["cmp_copied"], 1)
                if 1 <= i < PT and x in (7, 9):
                    branch_copy(i - 1, (x - 7) // 2)
                if v < N:
                    exponent(v)
                if 1 <= v <= N and units[v - 1][0] != "ml":
                    copy_turned(v - 1)
                if i < PT and x == 1:
                    act.wait_ge(s["cmp_shift"], i + 1)
                    nc.scalar.activation(b["cmp_s"][:, :, :], b["cmp_s"][:, :, :], ACT.Exp).then_inc(s["cmp_exp"], 1)
            for r in range(2):
                branch_copy(PT - 1, r)


def decode_mixers(k, zd, td, a):
    nc, io = k.nc, k.io
    G, NP = 2, DB * NPG
    W = PAST + ND
    st, b, s = phase(k, "dec", dict(
        page_table=[1, NP], dec_table=[P, TABLE_W - SPLIT], pages=[P, NP, 4 * HD], fox_pages=[P, NP, 2 * BW], logf_pages=[P, NP, H], win_pages=[P, NP, 2 * HD],
        kcv_t=[P, NP * P], ksel_t=[HD, NP * P], kwin_t=[HD, NP * P], fk_t=[P, 2, NP * P], w_cmp=[P, BLK, HD],
        q_n=[HD, DB, H, DT], q_f=[P, 2, DB, H, DT], q_m=[P, 2, DB, H, DT],
        logf_rows=[P, NP, H, DT], x_fox=[ND, DB, H, DT], x_ml=[ND, DB, H, DT], x_in=[ND, DB, H, DT],
        kc_d=[HD, DB * DCB], vc_d=[DB * DCB, HD], probs=[P, 2, W], probs_t=[P, 3, P],
        row=[P, 16], gates=[P, 3 * H], gate3=[P, 3], gate_tmp=[P, 3 * H], ml_d=[P, ND], ml_w=[P, ND], ml_wt=[ND, P],
        mem=[P, 2, DB, VW1], mem_new=[P, 2, DB, VW1], m_bh=[DB, H], m_hb=[H, DB],
        norm_wd=[P, BW], norm_row=[P, HD], num=[P, VW1], o_row=[P, HD], stat=[P, 6], mv=[P, 2], res=[P, 3, HD], br_d=[P, 6, ND],
        tok_g=[ND, H], g_rows=[H, ND], lf_rows=[H, ND], bl=[H, DB], gmax=[H, DB], m_new=[H, DB], decay=[H, DB], ws_rows=[H, ND],
        ws_tok=[ND, H], k_w=[ND, BW], v_own=[ND, 2, H * VW1], decay_col=[P, 2, DB]),
        ["dtab_loaded", "ptab_loaded", "pages_loaded", "fox_loaded", "logf_loaded", "win_loaded", "wcd_loaded", "mem_loaded", "nwd_loaded",
         "d_turned", "d_act_copied", "d_dve_copied", "zeroed", "q_ready", "x_ready", "kcd_mm", "kcd_done", "d_scores", "d_negmax",
         "d_exp", "d_ptrn", "d_pcopied", "d_pv", "d_ml_mm", 
         "am_row", "ml_exp", "ml_weighted", "ml_wturned", "ml_wcopied", "ml_pv", "acc",
         "drs_ve", "drs", "res_done", "res_turned", "res_copied", "nw_acc", "o_mm",
         "st_mm", "st_dve", "st_act", "st_up", "v_own_done", "mem_done", "dec_stored"])
    tj = [(kind, p0) for kind in ("kcv", "ksel", "fk0", "fk1", "kwin") for p0 in range(0, NP, 4)]
    turn_sem = lambda n: ("d_act_copied" if n % 2 == 0 else "d_dve_copied", n // 2 + 1)

    def turned_place(kind, p0):
        c = slice(p0 * P, (p0 + 4) * P)
        return {"kcv": b["kcv_t"][:, c], "ksel": b["ksel_t"][:, c], "kwin": b["kwin_t"][:, c], "fk0": b["fk_t"][:, 0, c], "fk1": b["fk_t"][:, 1, c]}[kind]

    KINDS = ["cmp", "sel", "win", "fox"]
    NK = len(KINDS)
    s_at = {"cmp": k.ps[3][:, 160:192], "sel": k.ps[0][:, 0:W], "win": k.ps[1][:, 0:W], "fox": k.ps[2][:, 0:W]}
    v_at = {"cmp": (384, 448), "sel": (0, 64), "win": (64, 128), "fox": (128, 384)}
    bias_of = {"cmp": "dec_cmp_bias", "sel": "dec_bias", "win": "dec_bias", "fox": "dec_fox_bias"}
    rowc = lambda x, n=1: b["row"][:, x:x + n]
    R_MAX, R_NEG, R_SUM, R_A, R_MT, R_NM, R_AM, R_INT, R_ENM, R_DEN, R_RSTD, R_MLMAX, R_VE = 0, 1, 2, 4, 5, 6, 7, 8, 9, 10, 11, 12, 13
    hm = lambda h: k.c("head_of_row", P, h, h + 1)
    group = lambda t, g: t[:, 4 * g:4 * g + 4].rearrange("p b h t -> p (b h t)")

    with st, nc.Block() as block:
        k.dec_const = b["dec_table"]

        @block.sync
        def _(sp):
            sp.dma_start(b["page_table"][:, :], io["page_table"].rearrange("b (o p) -> o (b p)", o=1)).then_inc(s["ptab_loaded"], 16)
            sp.dma_start(b["dec_table"][:, :], io["table"][:, SPLIT:TABLE_W]).then_inc(s["dtab_loaded"], 16)
            sp.dma_start(b["w_cmp"][0:HD], io["nsa_w_ck"][0].rearrange("p d e -> d p e")).then_inc(s["wcd_loaded"], 16)
            sp.dma_start(b["w_cmp"][HD:P], io["nsa_w_cv"][0].rearrange("p d e -> d p e")).then_inc(s["wcd_loaded"], 16)
            sp.wait_ge(s["ptab_loaded"], 16)
            for n in range(NP):
                page = sp.value_load(b["page_table"][0:1, n:n + 1], min_val=0, max_val=io["cache_nsa"].shape[1] - 1)
                sp.dma_start(b["pages"][:, n, :], io["cache_nsa"][0, bass.ds(page, 1)].rearrange("o p r d -> (o p) (r d)")).then_inc(s["pages_loaded"], 16)
                sp.dma_start(b["fox_pages"][:, n, :], io["cache_fox_kv"][0, bass.ds(page, 1)].rearrange("o p r h d -> (o p) (r h d)")).then_inc(s["fox_loaded"], 16)
                sp.dma_start(b["logf_pages"][:, n, :], io["cache_fox_logf"][0, bass.ds(page, 1)].rearrange("o p h -> (o p) h")).then_inc(s["logf_loaded"], 16)
            sp.dma_start(b["win_pages"][:, :, :], io["cache_nsa_win"].rearrange("x b (n p) r d -> p (x b n) (r d)", p=P)).then_inc(s["win_loaded"], 16)
            with nc.allow_non_contiguous_dma(reason="small states"):
                for kt in range(2):
                    for hh in range(2):
                        h = 2 * kt + hh
                        sp.dma_start(b["mem"][hh * HD:(hh + 1) * HD, kt, :, 0:HD], io["state_mlstm_c"][0, :, h].rearrange("b d e -> d b e")).then_inc(s["mem_loaded"], 16)
                        sp.dma_start(b["mem"][hh * HD:(hh + 1) * HD, kt, :, HD], io["state_mlstm_n"][0, :, h].rearrange("b d -> d b")).then_inc(s["mem_loaded"], 16)
                sp.dma_start(b["m_bh"][:, :], io["state_mlstm_m"][0]).then_inc(s["mem_loaded"], 16)
                sp.dma_start(b["m_hb"][:, :], io["state_mlstm_m"][0].rearrange("b h -> h b")).then_inc(s["mem_loaded"], 16)
                sp.dma_start(b["norm_wd"][:, :], io["mlstm_norm_w"][0].partition_broadcast(P)).then_inc(s["nwd_loaded"], 16)
                sp.wait_ge(s["res_copied"], G)
                sp.dma_start(k.br_dram.rearrange("p (c t) -> p c t", c=6)[:, :, SEQ:T], b["br_d"][:, :, :]).then_inc(s["dec_stored"], 16)
                sp.wait_ge(s["mem_done"], 2 * 2 * DB)
                for kt in range(2):
                    for hh in range(2):
                        h = 2 * kt + hh
                        sp.dma_start(io["s_mlstm_c"][0, :, h].rearrange("b d e -> d b e"), b["mem_new"][hh * HD:(hh + 1) * HD, kt, :, 0:HD]).then_inc(s["dec_stored"], 16)
                        sp.dma_start(io["s_mlstm_n"][0, :, h].rearrange("b d -> d b"), b["mem_new"][hh * HD:(hh + 1) * HD, kt, :, HD]).then_inc(s["dec_stored"], 16)
                sp.dma_start(io["s_mlstm_m"][0].rearrange("b h -> h b"), b["m_new"][:, :]).then_inc(s["dec_stored"], 16)
            sp.wait_ge(s["dec_stored"], 16 * 10)

        @block.tensor
        def _(pe):
            for n, (kind, p0) in enumerate(tj):
                if n == 0:
                    pe.wait_ge(s["pages_loaded"], 16 * NP)
                if n == 8:
                    pe.wait_ge(s["fox_loaded"], 16 * NP)
                if n == 16:
                    pe.wait_ge(s["win_loaded"], 16)
                if n >= 8:
                    pe.wait_ge(s[turn_sem(n - 8)[0]], turn_sem(n - 8)[1])
                for x in range(4):
                    pg = p0 + x
                    src = {"kcv": b["pages"][:, pg, 0:P], "ksel": b["pages"][:, pg, P:2 * P], "kwin": b["win_pages"][:, pg, :],
                           "fk0": b["fox_pages"][:, pg, 0:P], "fk1": b["fox_pages"][:, pg, P:2 * P]}[kind]
                    mm = nc.tensor.transpose(k.ps[n % 8][:, x * P:(x + 1) * P], src, k.c("ident"))
                mm.then_inc(s["d_turned"], 1)
            pe.wait_ge(s["d_act_copied"], len(tj) // 2)
            pe.wait_ge(s["d_dve_copied"], len(tj) // 2)
            pe.wait_ge(s["wcd_loaded"], 32)
            for p in range(BLK):
                nc.tensor.matmul(k.ps[6][0:HD, 0:DB * DCB], b["w_cmp"][0:HD, p, :], b["kcv_t"][0:HD, p:NP * P:BLK], start=(p == 0), stop=(p == BLK - 1))
            for p in range(BLK):
                mm = nc.tensor.matmul(k.ps[7][0:DB * DCB, 0:HD], b["kcv_t"][HD:P, p:NP * P:BLK], b["w_cmp"][HD:P, p, :], start=(p == 0), stop=(p == BLK - 1))
            mm.then_inc(s["kcd_mm"], 1)
            pe.wait_ge(s["kcd_done"], 2)
            pe.wait_ge(s["q_ready"], 3 * H)
            pe.wait_ge(s["x_ready"], 4)
            pe.wait_ge(s["mem_loaded"], 16 * 10)
            past = lambda bb, n=0: slice(bb * PAST + n * P, bb * PAST + (n + 1) * P)
            for g in range(G):
                if g:
                    pe.wait_ge(s["res_copied"], g)
                nc.tensor.matmul(s_at["cmp"], group(b["q_n"], g), b["kc_d"][:, :], start=True, stop=True).then_inc(s["d_scores"], 1)
                for kind, key in (("sel", "ksel"), ("win", "kwin")):
                    for x in range(4):
                        bb = 4 * g + x
                        nc.tensor.matmul(s_at[kind][32 * x:32 * x + 32, 0:PAST], b["q_n"][:, bb].rearrange("p h t -> p (h t)"),
                                         b[key + "_t"][:, bb * PAST:(bb + 1) * PAST], start=True, stop=True, tile_position=(0, 32 * x))
                    nc.tensor.matmul(s_at[kind][:, PAST:W], group(b["q_n"], g), td[key][0:HD, :], start=True, stop=True).then_inc(s["d_scores"], 1)
                for x in range(4):
                    bb = 4 * g + x
                    q = [b["q_f"][:, kt, bb].rearrange("p h t -> p (h t)") for kt in range(2)]
                    lf = [b["logf_rows"][:, bb * NPG + n].rearrange("p h t -> p (h t)") for n in range(NPG)]
                    new = b["x_fox"][:, bb].rearrange("p h t -> p (h t)")
                    for n in range(NPG):
                        out = s_at["fox"][32 * x:32 * x + 32, n * P:(n + 1) * P]
                        terms = [(q[0], b["fk_t"][:, 0, past(bb, n)]), (q[1], b["fk_t"][:, 1, past(bb, n)]), (lf[n], k.c("after"))]
                        terms += [(lf[m], k.c("ones")) for m in range(n + 1, NPG)] + [(new, k.c("ones", ND))]
                        for y, (lhs, rhs) in enumerate(terms):
                            nc.tensor.matmul(out, lhs, rhs, start=(y == 0), stop=(y == len(terms) - 1), tile_position=(0, 32 * x))
                terms = [(group(b["q_f"][:, kt], g), td["fk"][:, kt, :]) for kt in range(2)] + [(group(b["x_fox"], g), k.c("dec_after", ND))]
                for y, (lhs, rhs) in enumerate(terms):
                    mm = nc.tensor.matmul(s_at["fox"][:, PAST:W], lhs, rhs, start=(y == 0), stop=(y == 2))
                mm.then_inc(s["d_scores"], 1)
                for y, (lhs, rhs) in enumerate([(group(b["x_ml"], g), k.c("dec_after", ND)), (group(b["x_in"], g), k.c("ident", ND, 0, ND))]):
                    nc.tensor.matmul(k.ps[3][:, 0:ND], lhs, rhs, start=(y == 0), stop=(y == 1))
                for kt in range(2):
                    nc.tensor.matmul(k.ps[3][:, ND:2 * ND], group(b["q_m"][:, kt], g), td["mk"][:, kt, :], start=(kt == 0), stop=(kt == 1))
                nc.tensor.matmul(k.ps[3][:, 128:129], group(b["x_ml"], g), k.c("ones", ND, 0, 1), start=True, stop=True)
                nc.tensor.matmul(k.ps[3][:, 132:136], k.c("batch_to_row", DB, g * P, (g + 1) * P), b["m_bh"][:, :], start=True, stop=True)
                nc.tensor.matmul(k.ps[3][:, 136:148], k.c("row_of_token", ND, g * P, (g + 1) * P), zd[0:ND, 0, Z_NG:Z_NG + 12], start=True, stop=True).then_inc(s["d_ml_mm"], 1)
                nc.tensor.matmul(k.ps[4][:, 0:BW], k.c("row_of_token", ND, g * P, (g + 1) * P), zd[0:ND, 0, Z_MO:Z_MO + BW], start=True, stop=True).then_inc(s["o_mm"], 1)
                for n, kind in enumerate(KINDS):
                    m = g * NK + n
                    pe.wait_ge(s["d_exp"], m + 1)
                    if m >= 1:
                        pe.wait_ge(s["d_pcopied"], m)
                    if kind == "cmp":
                        mm = nc.tensor.transpose(k.ps[5][0:32, 0:P], b["probs"][:, m % 2, 0:32], k.c("ident"))
                    else:
                        for x in range(3):
                            w = min(P, W - x * P)
                            mm = nc.tensor.transpose(k.ps[5][0:w, x * P:(x + 1) * P], b["probs"][:, m % 2, x * P:x * P + w], k.c("ident"))
                    mm.then_inc(s["d_ptrn"], 1)
                    pe.wait_ge(s["d_pcopied"], m + 1)
                    c0, c1 = v_at[kind]
                    if kind == "cmp":
                        mm = nc.tensor.matmul(k.ps[6][:, c0:c1], b["probs_t"][0:32, 0, :], b["vc_d"][:, :], start=True, stop=True)
                    for x in range(4 if kind != "cmp" else 0):
                        bb = 4 * g + x
                        for y in range(3):
                            if y < 2:
                                lhs = b["probs_t"][:, y, 32 * x:32 * x + 32]
                                rhs = {"sel": b["pages"][:, bb * NPG + y, 3 * HD:4 * HD], "win": b["win_pages"][:, bb * NPG + y, HD:2 * HD],
                                       "fox": b["fox_pages"][:, bb * NPG + y, BW:2 * BW]}[kind]
                            else:
                                lhs = b["probs_t"][0:ND, 2, 32 * x:32 * x + 32]
                                cz, wz = {"sel": (Z_VS, HD), "win": (Z_VW, HD), "fox": (Z_FV, BW)}[kind]
                                rhs = zd[0:ND, 0, cz:cz + wz]
                            mm = nc.tensor.matmul(k.ps[6][32 * x:32 * x + 32, c0:c1], lhs, rhs, start=(y == 0), stop=(y == 2), tile_position=(0, 32 * x))
                    mm.then_inc(s["d_pv"], 1)
                for x in range(4):
                    bb = 4 * g + x
                    for kt in range(2):
                        nc.tensor.matmul(k.ps[7][32 * x:32 * x + 32, 264:264 + VW1], b["q_m"][:, kt, bb].rearrange("p h t -> p (h t)"), b["mem"][:, kt, bb, :],
                                         start=(kt == 0), stop=(kt == 1), tile_position=(0, 32 * x))
                pe.wait_ge(s["ml_weighted"], g + 1)
                nc.tensor.transpose(k.ps[5][0:ND, 3 * P:4 * P], b["ml_w"][:, :], k.c("ident")).then_inc(s["ml_wturned"], 1)
                pe.wait_ge(s["ml_wcopied"], g + 1)
                nc.tensor.matmul(k.ps[7][:, 0:H * VW1], b["ml_wt"][:, :], zd[0:ND, 0, Z_MV:Z_MV + H * VW1], start=True, stop=True).then_inc(s["ml_pv"], 1)
                pe.wait_ge(s["res_done"], 3 * (g + 1))
                for x in range(3):
                    mm = nc.tensor.transpose(k.ps[1][0:HD, x * P:(x + 1) * P], b["res"][:, x, :], k.c("ident"))
                mm.then_inc(s["res_turned"], 1)
            pe.wait_ge(s["res_copied"], G)
            nc.tensor.matmul(k.ps[0][0:ND, 0:H], k.c("dec_after", ND), a["sc"][0:ND, PT, 4:8], start=True, stop=True)
            nc.tensor.transpose(k.ps[0][0:H, 64:64 + ND], a["sc"][0:ND, PT, 4:8], k.c("ident", ND, 0, ND)).then_inc(s["st_mm"], 1)
            pe.wait_ge(s["st_dve"], 2)
            nc.tensor.transpose(k.ps[0][0:H, 128:128 + ND], b["tok_g"][:, :], k.c("ident", ND, 0, ND)).then_inc(s["st_mm"], 1)
            pe.wait_ge(s["st_act"], 2)
            nc.tensor.transpose(k.ps[0][0:ND, 192:192 + H], b["ws_rows"][:, :], k.c("ident", H, 0, H))
            for kt in range(2):
                mm = nc.tensor.matmul(k.ps[0][:, 256 + 8 * kt:264 + 8 * kt], k.c("head_rows", H, kt * P, (kt + 1) * P), b["decay"][:, :], start=True, stop=True)
            mm.then_inc(s["st_mm"], 1)
            n = 0
            for bb in range(DB):
                pe.wait_ge(s["v_own_done"], bb + 1)
                for kt in range(2):
                    if n >= 4:
                        pe.wait_ge(s["mem_done"], 2 * (n - 3))
                    nc.tensor.matmul(k.ps[1 + n % 4][:, 0:2 * VW1], b["k_w"][:, kt * P:(kt + 1) * P], b["v_own"][:, bb % 2, kt * 2 * VW1:(kt + 1) * 2 * VW1],
                                     start=True, stop=True).then_inc(s["st_up"], 1)
                    n += 1

        def copy_turned(eng, copy, scaled, par):
            for n, (kind, p0) in enumerate(tj):
                if n % 2 != par:
                    continue
                eng.wait_ge(s["d_turned"], n + 1)
                r = HD if kind in ("ksel", "kwin") else P
                dst, src = turned_place(kind, p0)[0:r], k.ps[n % 8][0:r, :]
                (copy(dst, src) if kind == "kcv" else scaled(dst, src)).then_inc(s[turn_sem(n)[0]], 1)

        @block.scalar
        def _(act):
            copy_turned(act, nc.scalar.copy, lambda d, x: nc.scalar.mul(d, x, SCALE), 0)
            for g in range(G):
                for n, kind in enumerate(KINDS):
                    m = g * NK + n
                    w = DB * DCB if kind == "cmp" else W
                    act.wait_ge(s["d_negmax"], m + 1)
                    row = b["probs"][:, m % 2, 0:w]
                    nc.scalar.activation(row, row, ACT.Exp, bias=b["row"][:, R_NEG:R_NEG + 1], accum_out=b["row"][:, R_SUM:R_SUM + 1]).then_inc(s["d_exp"], 1)
                    act.wait_ge(s["d_ptrn"], m + 1)
                    if m >= 1:
                        act.wait_ge(s["d_pv"], m)
                    if kind == "cmp":
                        nc.scalar.copy(b["probs_t"][0:32, 0, :], k.ps[5][0:32, 0:P]).then_inc(s["d_pcopied"], 1)
                    else:
                        nc.scalar.copy(b["probs_t"][:, 0:2, :], k.ps[5][:, 0:2 * P].rearrange("p (x r) -> p x r", x=2))
                        nc.scalar.copy(b["probs_t"][0:ND, 2, :], k.ps[5][0:ND, 2 * P:3 * P]).then_inc(s["d_pcopied"], 1)
                act.wait_ge(s["am_row"], g + 1)
                nc.scalar.activation(b["ml_d"][:, :], b["ml_d"][:, :], ACT.Exp, bias=rowc(R_NM))
                nc.scalar.activation(rowc(R_INT), rowc(R_AM), ACT.Exp)
                nc.scalar.activation(rowc(R_ENM), rowc(R_NM), ACT.Exp).then_inc(s["ml_exp"], 1)
                act.wait_ge(s["ml_wturned"], g + 1)
                nc.scalar.copy(b["ml_wt"][:, :], k.ps[5][0:ND, 3 * P:4 * P]).then_inc(s["ml_wcopied"], 1)
                act.wait_ge(s["res_turned"], g + 1)
                for x in range(3):
                    for h in range(H):
                        src = k.ps[1][0:HD, x * P:(x + 1) * P].rearrange("p (b h t) -> p b h t", b=4, h=H)[:, :, h, :]
                        dst = b["br_d"][(h % 2) * HD:(h % 2 + 1) * HD, 2 * x + h // 2, g * 32:(g + 1) * 32].rearrange("p (b t) -> p b t", b=4)
                        ins = nc.scalar.copy(dst, src)
                ins.then_inc(s["res_copied"], 1)
            act.wait_ge(s["st_dve"], 6)
            nc.scalar.activation(b["decay"][:, :], b["decay"][:, :], ACT.Exp).then_inc(s["st_act"], 1)
            nc.scalar.activation(b["ws_rows"][:, :], b["ws_rows"][:, :], ACT.Exp).then_inc(s["st_act"], 1)

        @block.gpsimd
        def _(pool):
            for g in range(G):
                pool.wait_ge(s["drs_ve"], g + 1)
                nc.gpsimd.tensor_tensor(rowc(R_RSTD), rowc(R_VE), k.c("minus_half", P, 0, 1), ALU.pow).then_inc(s["drs"], 1)

        @block.vector
        def _(dve):
            nc.vector.memset(b["q_f"][:, :, :, :, :], 0.0).then_inc(s["zeroed"], 1)
            nc.vector.memset(b["q_m"][:, :, :, :, :], 0.0).then_inc(s["zeroed"], 1)
            dve.wait_ge(s["zeroed"], 2)
            for h in range(H):
                hr, kt = (h % 2) * HD, h // 2
                part = lambda n: td[n][hr:hr + HD, kt, :].rearrange("p (b t) -> p b t", b=DB)
                nc.vector.tensor_copy(b["q_n"][:, :, h, :], part("nq")).then_inc(s["q_ready"], 1)
                nc.vector.tensor_copy(b["q_f"][hr:hr + HD, kt, :, h, :], part("fq")).then_inc(s["q_ready"], 1)
                nc.vector.tensor_copy(b["q_m"][hr:hr + HD, kt, :, h, :], part("mq")).then_inc(s["q_ready"], 1)
            dve.wait_ge(s["dtab_loaded"], 16)
            rows4 = lambda name: k.c(name, ND).rearrange("p (b h t) -> p b h t", b=DB, h=H)
            for dst, name, c in (("x_fox", "upto_row", 8), ("x_ml", "upto_row", 4), ("x_in", "batch_of_row", 0)):
                nc.vector.tensor_tensor(b[dst][:, :, :, :], rows4(name), a["sc"][0:ND, PT, c:c + H].unsqueeze(1).unsqueeze(3).to_broadcast([ND, DB, H, DT]), ALU.mult).then_inc(s["x_ready"], 1)
            dve.wait_ge(s["logf_loaded"], 16 * NP)
            nc.vector.tensor_copy(b["logf_rows"][:, :, :, :], b["logf_pages"][:, :, :].unsqueeze(3).to_broadcast([P, NP, H, DT])).then_inc(s["x_ready"], 1)
            dve.wait_ge(s["nwd_loaded"], 16)
            nacc = 0
            for h in range(H):
                src = b["norm_wd"][:, h * HD:(h + 1) * HD]
                if h == 0:
                    nc.vector.tensor_scalar(b["norm_row"][:, :], src, hm(0), None, ALU.mult).then_inc(s["nw_acc"], 1)
                else:
                    dve.wait_ge(s["nw_acc"], h)
                    nc.vector.scalar_tensor_tensor(b["norm_row"][:, :], src, hm(h), b["norm_row"][:, :], ALU.mult, ALU.add).then_inc(s["nw_acc"], 1)
            copy_turned(dve, nc.vector.tensor_copy, lambda d, x: nc.vector.tensor_scalar(d, x, SCALE, None, ALU.mult), 1)
            dve.wait_ge(s["kcd_mm"], 1)
            nc.vector.tensor_scalar(b["kc_d"][:, :], k.ps[6][0:HD, 0:DB * DCB], SCALE, None, ALU.mult).then_inc(s["kcd_done"], 1)
            nc.vector.tensor_copy(b["vc_d"][:, :], k.ps[7][0:DB * DCB, 0:HD]).then_inc(s["kcd_done"], 1)
            acc = [0]

            def chain(ins):
                acc[0] += 1
                ins.then_inc(s["acc"], 1)
                dve.wait_ge(s["acc"], acc[0])

            for g in range(G):
                dve.wait_ge(s["d_ml_mm"], g + 1)
                chain(nc.vector.tensor_copy(b["gates"][:, :], k.ps[3][:, 136:148]))
                for h in range(H):
                    src = b["gates"][:, 3 * h:3 * h + 3]
                    if h == 0:
                        chain(nc.vector.tensor_scalar(b["gate3"][:, :], src, hm(0), None, ALU.mult))
                    else:
                        chain(nc.vector.scalar_tensor_tensor(b["gate3"][:, :], src, hm(h), b["gate3"][:, :], ALU.mult, ALU.add))
                for n, kind in enumerate(KINDS):
                    m = g * NK + n
                    w = DB * DCB if kind == "cmp" else W
                    dve.wait_ge(s["d_scores"], m + 1)
                    if m >= 2:
                        dve.wait_ge(s["d_ptrn"], m - 1)
                    bias = k.c(bias_of[kind], P, g * w, (g + 1) * w)
                    chain(nc.vector.tensor_tensor_reduce(b["probs"][:, m % 2, 0:w], s_at[kind], bias, 1.0, -3e38, ALU.add, ALU.max, rowc(R_MAX)))
                    nc.vector.tensor_scalar(rowc(R_NEG), rowc(R_MAX), -1.0, None, ALU.mult).then_inc(s["d_negmax"], 1)
                    dve.wait_ge(s["d_exp"], m + 1)
                    chain(nc.vector.tensor_scalar(rowc(R_DEN), rowc(R_SUM), TINY, None, ALU.max))
                    chain(nc.vector.reciprocal(rowc(R_DEN), rowc(R_DEN)))
                    if kind != "fox":
                        chain(nc.vector.tensor_tensor(rowc(R_DEN), rowc(R_DEN), b["gate3"][:, n:n + 1], ALU.mult))
                    dve.wait_ge(s["d_pv"], m + 1)
                    c0, c1 = v_at[kind]
                    pv = k.ps[6][:, c0:c1]
                    if kind == "cmp":
                        chain(nc.vector.tensor_scalar(b["res"][:, 0, :], pv, rowc(R_DEN), None, ALU.mult))
                    elif kind != "fox":
                        ins = nc.vector.scalar_tensor_tensor(b["res"][:, 0, :], pv, rowc(R_DEN), b["res"][:, 0, :], ALU.mult, ALU.add)
                        if kind == "sel":
                            chain(ins)
                        else:
                            ins.then_inc(s["res_done"], 1)
                    else:
                        chain(nc.vector.tensor_scalar(b["res"][:, 2, :], pv[:, 0:HD], hm(0), None, ALU.mult))
                        for h in range(1, H):
                            chain(nc.vector.scalar_tensor_tensor(b["res"][:, 2, :], pv[:, h * HD:(h + 1) * HD], hm(h), b["res"][:, 2, :], ALU.mult, ALU.add))
                        nc.vector.tensor_scalar(b["res"][:, 2, :], b["res"][:, 2, :], rowc(R_DEN), None, ALU.mult).then_inc(s["res_done"], 1)
                chain(nc.vector.tensor_tensor_reduce(b["ml_d"][:, :], k.ps[3][:, 0:ND], k.c("dec_mask", P, g * ND, (g + 1) * ND), 1.0, -3e38, ALU.add, ALU.max, rowc(R_MLMAX)))
                chain(nc.vector.tensor_tensor_reduce(b["gates"][:, 0:H], k.ps[3][:, 132:136], k.c("head_of_row"), 1.0, 0.0, ALU.mult, ALU.add, rowc(R_A)))
                chain(nc.vector.tensor_tensor(rowc(R_A), rowc(R_A), k.ps[3][:, 128:129], ALU.add))
                chain(nc.vector.tensor_tensor(rowc(R_MT), rowc(R_A), rowc(R_MLMAX), ALU.max))
                chain(nc.vector.tensor_scalar(rowc(R_NM), rowc(R_MT), -1.0, None, ALU.mult))
                nc.vector.tensor_tensor(rowc(R_AM), rowc(R_A), rowc(R_MT), ALU.subtract).then_inc(s["am_row"], 1)
                dve.wait_ge(s["ml_exp"], g + 1)
                nc.vector.tensor_tensor(b["ml_w"][:, :], k.ps[3][:, ND:2 * ND], b["ml_d"][:, :], ALU.mult).then_inc(s["ml_weighted"], 1)
                dve.wait_ge(s["o_mm"], g + 1)
                for h in range(H):
                    src = k.ps[4][:, h * HD:(h + 1) * HD]
                    chain(nc.vector.tensor_scalar(b["o_row"][:, :], src, hm(0), None, ALU.mult) if h == 0 else
                          nc.vector.scalar_tensor_tensor(b["o_row"][:, :], src, hm(h), b["o_row"][:, :], ALU.mult, ALU.add))
                dve.wait_ge(s["ml_pv"], g + 1)
                chain(nc.vector.tensor_scalar(b["num"][:, :], k.ps[7][:, 264:264 + VW1], rowc(R_INT), None, ALU.mult))
                for h in range(H):
                    chain(nc.vector.scalar_tensor_tensor(b["num"][:, :], k.ps[7][:, h * VW1:(h + 1) * VW1], hm(h), b["num"][:, :], ALU.mult, ALU.add))
                chain(nc.vector.tensor_scalar(rowc(R_DEN), b["num"][:, HD:VW1], -1.0, None, ALU.mult))
                chain(nc.vector.scalar_tensor_tensor(rowc(R_DEN), b["num"][:, HD:VW1], rowc(R_ENM), rowc(R_DEN), ALU.max, ALU.max))
                chain(nc.vector.reciprocal(rowc(R_DEN), rowc(R_DEN)))
                y = b["res"][:, 1, :]
                chain(nc.vector.scalar_tensor_tensor(y, b["num"][:, 0:HD], rowc(R_DEN), b["o_row"][:, :], ALU.mult, ALU.mult))
                chain(nc.vector.bn_stats(b["stat"][:, :], y))
                chain(nc.vector.bn_aggr(b["mv"][:, :], b["stat"][:, :]))
                nc.vector.tensor_scalar(rowc(R_VE), b["mv"][:, 1:2], EPS, None, ALU.add).then_inc(s["drs_ve"], 1)
                dve.wait_ge(s["drs"], g + 1)
                chain(nc.vector.tensor_scalar(y, y, b["mv"][:, 0:1], rowc(R_RSTD), ALU.subtract, ALU.mult))
                nc.vector.tensor_tensor(y, y, b["norm_row"][:, :], ALU.mult).then_inc(s["res_done"], 1)
                if g + 1 < G:
                    dve.wait_ge(s["res_turned"], g + 1)
            dve.wait_ge(s["st_mm"], 1)
            nc.vector.tensor_tensor(b["tok_g"][:, :], k.ps[0][0:ND, 0:H], a["sc"][0:ND, PT, 0:4], ALU.add).then_inc(s["st_dve"], 1)
            nc.vector.tensor_reduce(b["bl"][:, :], k.ps[0][0:H, 64:64 + ND].rearrange("p (b t) -> p b t", b=DB), AX.X, ALU.add).then_inc(s["st_dve"], 1)
            dve.wait_ge(s["st_dve"], 2)
            chain(nc.vector.tensor_tensor(b["bl"][:, :], b["bl"][:, :], b["m_hb"][:, :], ALU.add))
            dve.wait_ge(s["st_mm"], 2)
            grow = k.ps[0][0:H, 128:128 + ND].rearrange("p (b t) -> p b t", b=DB)
            nc.vector.tensor_reduce(b["gmax"][:, :], grow, AX.X, ALU.max).then_inc(s["st_dve"], 1)
            dve.wait_ge(s["st_dve"], 3)
            nc.vector.tensor_tensor(b["m_new"][:, :], b["bl"][:, :], b["gmax"][:, :], ALU.max).then_inc(s["st_dve"], 1)
            dve.wait_ge(s["st_dve"], 4)
            nc.vector.tensor_tensor(b["decay"][:, :], b["bl"][:, :], b["m_new"][:, :], ALU.subtract).then_inc(s["st_dve"], 1)
            nc.vector.tensor_tensor(b["ws_rows"][:, :].rearrange("p (b t) -> p b t", b=DB), grow, b["m_new"][:, :].unsqueeze(2).to_broadcast([H, DB, DT]), ALU.subtract).then_inc(s["st_dve"], 1)
            dve.wait_ge(s["st_mm"], 3)
            chain(nc.vector.tensor_scalar(b["ws_tok"][:, :], k.ps[0][0:ND, 192:192 + H], SCALE, None, ALU.mult))
            chain(nc.vector.tensor_copy(b["decay_col"][:, :, :], k.ps[0][:, 256:272].rearrange("p (k b) -> p k b", k=2)))
            chain(nc.vector.tensor_tensor(b["k_w"][:, :].rearrange("p (h d) -> p h d", h=H), zd[0:ND, 0, Z_MK:Z_MK + BW].rearrange("p (h d) -> p h d", h=H),
                                          b["ws_tok"][:, :].unsqueeze(2).to_broadcast([ND, H, HD]), ALU.mult))
            for bb in range(DB + 1):
                if bb < DB:
                    if bb >= 2:
                        dve.wait_ge(s["st_up"], 2 * (bb - 1))
                    nc.vector.tensor_scalar(b["v_own"][:, bb % 2, :], zd[0:ND, 0, Z_MV:Z_MV + H * VW1], k.c("batch_of_token", ND, bb, bb + 1), None, ALU.mult).then_inc(s["v_own_done"], 1)
                if bb >= 1:
                    for kt in range(2):
                        n = 2 * (bb - 1) + kt
                        dve.wait_ge(s["st_up"], n + 1)
                        for half in range(2):
                            r = slice(half * HD, (half + 1) * HD)
                            nc.vector.scalar_tensor_tensor(b["mem_new"][r, kt, bb - 1, :], b["mem"][r, kt, bb - 1, :], b["decay_col"][r, kt, bb - 1:bb],
                                                           k.ps[1 + n % 4][r, half * VW1:(half + 1) * VW1], ALU.mult, ALU.add).then_inc(s["mem_done"], 1)


def merge_branches(k, y):
    nc, io = k.nc, k.io
    UNITS = 3 * len(NCH)
    RING = 3
    st, b, s = phase(k, "merge", dict(xt2=[P, KD, T], br_all=[P, 6, T], gate_w=[P, 2, KD, 3, P], branch_w=[P, 2, 3, 2, P], bias_g=[P, 3, KD], bias_now=[P, 2, 3],
                              sig=[P, RING, 512]),
                     ["xt2_loaded", "br_loaded", "bg_loaded", "bias_copied", "gp_mm", "sig_done", "gp_read", "bank_free"] + [f"mw_loaded{i}" for i in range(2)])
    with st, nc.Block() as block:
        @block.sync
        def _(sp):
            def load(dt, slot):
                for m in range(3):
                    sp.dma_start(b["gate_w"][:, slot, :, m, :], io["w_in"][0].rearrange("(k p) n -> p k n", p=P)[:, :, bass.ds(dt * P + (C_GM + m * D), P)]).then_inc(s[f"mw_loaded{slot}"], 16)
                    sp.dma_start(b["branch_w"][:, slot, m], io["w_branch"][0, m].rearrange("(k p) n -> p k n", p=P)[:, :, bass.ds(dt * P, P)]).then_inc(s[f"mw_loaded{slot}"], 16)
            load(0, 0)
            for kk in range(KD):
                sp.dma_start(b["xt2"][:, kk, :], k.xt_dram[:, kk * T:(kk + 1) * T]).then_inc(s["xt2_loaded"], 16)
            sp.dma_start(b["br_all"][:, :, :].rearrange("p c t -> p (c t)"), k.br_dram).then_inc(s["br_loaded"], 16)
            with nc.allow_non_contiguous_dma(reason="bias columns"):
                sp.dma_start(b["bias_g"][:, :, :], io["b_in"][0, C_GM:NIN].rearrange("(m k p) -> p m k", m=3, p=P)).then_inc(s["bg_loaded"], 16)
            load(1, 1)
            with sp.Fori(0, KD // 2 - 1) as r:
                for x in range(2):
                    sp.wait_ge(s["gp_mm"], r * (2 * UNITS) + (x + 1) * UNITS)
                    load(r * 2 + (2 + x), x)

        @block.tensor
        def _(pe):
            pe.wait_ge(s["xt2_loaded"], 16 * KD)
            pe.wait_ge(s["br_loaded"], 16)
            with pe.Fori(0, KD // 2) as r:
                for x in range(2):
                    pe.wait_ge(s[f"mw_loaded{x}"], r * 96 + 96)
                    for m in range(3):
                        for n, (a0, w) in enumerate(NCH):
                            l = x * UNITS + m * 3 + n
                            pe.wait_ge(s["bank_free"], r * (2 * UNITS) + (l + 1))
                            for kk in range(KD):
                                nc.tensor.matmul(k.ps[l % RING][:, 0:w], b["gate_w"][:, x, kk, m, :], b["xt2"][:, kk, a0:a0 + w], start=(kk == 0), stop=(kk == KD - 1))
                            for kk in range(2):
                                mm = nc.tensor.matmul(k.ps[4 + l % RING][:, 0:w], b["branch_w"][:, x, m, kk, :], b["br_all"][:, 2 * m + kk, a0:a0 + w], start=(kk == 0), stop=(kk == 1))
                            mm.then_inc(s["gp_mm"], 1)

        @block.scalar
        def _(act):
            act.wait_ge(s["bg_loaded"], 16)
            with act.Fori(0, KD // 2) as r:
                for x in range(2):
                    nc.scalar.copy(b["bias_now"][:, x, :], b["bias_g"][:, :, bass.ds(r * 2 + x, 1)].rearrange("p m o -> p (m o)")).then_inc(s["bias_copied"], 1)
                    act.wait_ge(s["bias_copied"], r * 2 + (x + 1))
                    for m in range(3):
                        for n, (a0, w) in enumerate(NCH):
                            l = x * UNITS + m * 3 + n
                            act.wait_ge(s["gp_mm"], r * (2 * UNITS) + (l + 1))
                            act.wait_ge(s["bank_free"], r * (2 * UNITS) + (l + 1))
                            nc.scalar.activation(b["sig"][:, l % RING, 0:w], k.ps[l % RING][:, 0:w], ACT.Sigmoid,
                                                 bias=b["bias_now"][:, x, m:m + 1]).then_inc(s["sig_done"], 1)

        @block.vector
        def _(dve):
            nc.vector.memset(b["sig"][:, 0, 0:1], 0.0).then_inc(s["bank_free"], RING)
            with dve.Fori(0, KD // 2) as r:
                for x in range(2):
                    for m in range(3):
                        for n, (a0, w) in enumerate(NCH):
                            l = x * UNITS + m * 3 + n
                            dve.wait_ge(s["sig_done"], r * (2 * UNITS) + (l + 1))
                            sig, prod = b["sig"][:, l % RING, 0:w], k.ps[4 + l % RING][:, 0:w]
                            dst = y[:, bass.ds(r * 2 + x, 1), a0:a0 + w].rearrange("p o t -> p (o t)")
                            if m == 0:
                                nc.vector.tensor_tensor(dst, sig, prod, ALU.mult).then_inc(s["bank_free"], 1)
                            else:
                                nc.vector.tensor_tensor(sig, sig, prod, ALU.mult).then_inc(s["gp_read"], 1)
                                dve.wait_ge(s["gp_read"], r * (12) + (x * 6 + (m - 1) * 3 + n + 1))
                                nc.vector.tensor_tensor(dst, dst, sig, ALU.add).then_inc(s["bank_free"], 1)


def mix_out_norm(k, y, x1t, acc):
    nc, io = k.nc, k.io
    XB, TB = 4, 4
    st, b, s = phase(k, "mix", dict(w_o=[P, KD, D], x_res=[P, XB, D], lw=[P, D], lb=[P, D], lwc=[P, KD], lbc=[P, KD],
                              stats1=[P, 12], mv1=[P, NT, 2], ve1=[P, NT], rstd1=[P, NT]),
                     ["wo_loaded", "ln1_par", "mix_mm", "res_added", "st1", "mv1_done", "ve1_done", "rs1", "xh1", "x1_psum", "x1_done", "par_scaled", "acc_mul", "acc_done"]
                     + [f"xr_loaded{i}" for i in range(XB)])
    groups = [(0, 4), (4, 4), (8, 1)]
    with st, nc.Block() as block:
        @block.sync
        def _(sp):
            def load(t):
                sp.dma_start(b["x_res"][0:rows(t), t % XB, :], k.xn_dram[t * P:t * P + rows(t), :]).then_inc(s[f"xr_loaded{t % XB}"], 16)
            for kk in range(KD):
                sp.dma_start(b["w_o"][:, kk, :], io["w_out"][0, kk * P:(kk + 1) * P, :]).then_inc(s["wo_loaded"], 16)
            for t in range(XB):
                load(t)
            sp.dma_start(b["lw"][:, :], io["ln1_w"][0].partition_broadcast(P)).then_inc(s["ln1_par"], 16)
            sp.dma_start(b["lb"][:, :], io["ln1_b"][0].partition_broadcast(P)).then_inc(s["ln1_par"], 16)
            with nc.allow_non_contiguous_dma(reason="1024 values to columns"):
                sp.dma_start(b["lwc"][:, :], io["ln1_w"][0].rearrange("(k p) -> p k", p=P)).then_inc(s["ln1_par"], 16)
                sp.dma_start(b["lbc"][:, :], io["ln1_b"][0].rearrange("(k p) -> p k", p=P)).then_inc(s["ln1_par"], 16)
            for t in range(XB, NT):
                sp.wait_ge(s["acc_done"], t - XB + 1)
                sp.wait_ge(s["x1_psum"], KD * ((t - XB) // 4 + 1))
                load(t)

        @block.tensor
        def _(pe):
            pe.wait_ge(s["wo_loaded"], 16 * KD)
            n = 0

            def turn_group(g):
                nonlocal n
                t0, cnt = groups[g]
                pe.wait_ge(s["xh1"], t0 + cnt)
                for kk in range(KD):
                    if n >= 4:
                        pe.wait_ge(s["x1_done"], n - 3)
                    for j in range(cnt):
                        r = rows(t0 + j)
                        mm = nc.tensor.transpose(k.ps[4 + n % 4][:, j * P:j * P + r], b["x_res"][0:r, (t0 + j) % XB, kk * P:(kk + 1) * P], k.c("ident", r, 0, r))
                    mm.then_inc(s["x1_psum"], 1)
                    n += 1

            for t in range(NT):
                r = rows(t)
                if t >= 2:
                    pe.wait_ge(s["res_added"], t - 1)
                for half in range(2):
                    for kk in range(KD):
                        mm = nc.tensor.matmul(k.ps[2 * (t % 2) + half][0:r, :], y[:, kk, t * P:t * P + r], b["w_o"][:, kk, half * 512:(half + 1) * 512],
                                              start=(kk == 0), stop=(kk == KD - 1))
                mm.then_inc(s["mix_mm"], 1)
                if t in (4, 8):
                    turn_group(t // 4 - 1)
            turn_group(2)

        @block.vector
        def _(dve):
            def statistics(t):
                r = rows(t)
                x = b["x_res"][0:r, t % XB, :]
                dve.wait_ge(s[f"xr_loaded{t % XB}"], 16 * (t // XB + 1))
                dve.wait_ge(s["mix_mm"], t + 1)
                mix = k.psum[0:r, 2 * (t % 2):2 * (t % 2) + 2, :].rearrange("p b c -> p (b c)")
                nc.vector.scalar_tensor_tensor(x, x, ALPHA, mix, ALU.mult, ALU.add).then_inc(s["res_added"], 1)
                dve.wait_ge(s["res_added"], t + 1)
                nc.vector.bn_stats(b["stats1"][0:r, 0:6], x[:, 0:512]).then_inc(s["st1"], 1)
                nc.vector.bn_stats(b["stats1"][0:r, 6:12], x[:, 512:1024]).then_inc(s["st1"], 1)
                dve.wait_ge(s["st1"], 2 * t + 2)
                nc.vector.bn_aggr(b["mv1"][0:r, t, :], b["stats1"][0:r, :]).then_inc(s["mv1_done"], 1)
                dve.wait_ge(s["mv1_done"], t + 1)
                nc.vector.tensor_scalar(b["ve1"][0:r, t:t + 1], b["mv1"][0:r, t, 1:2], EPS, None, ALU.add).then_inc(s["ve1_done"], 1)

            def normalise(t):
                r = rows(t)
                x = b["x_res"][0:r, t % XB, :]
                dve.wait_ge(s["rs1"], t + 1)
                nc.vector.tensor_scalar(x, x, b["mv1"][0:r, t, 0:1], b["rstd1"][0:r, t:t + 1], ALU.subtract, ALU.mult).then_inc(s["xh1"], 1)

            for t in range(NT):
                statistics(t)
                if t in (3, 7, 8):
                    if t != 8:
                        normalise(t - 1)
                        normalise(t)
                    else:
                        normalise(t)
                elif t % 4 != 0:
                    normalise(t - 1)

        @block.gpsimd
        def _(pool):
            pool.wait_ge(s["ln1_par"], 64)
            for w in (b["lw"], b["lb"]):
                nc.gpsimd.tensor_scalar(w[:, :], w[:, :], ALPHA, None, ALU.mult).then_inc(s["par_scaled"], 1)
            pool.wait_ge(s["par_scaled"], 2)

            def root(t):
                r = rows(t)
                pool.wait_ge(s["ve1_done"], t + 1)
                nc.gpsimd.tensor_tensor(b["rstd1"][0:r, t:t + 1], b["ve1"][0:r, t:t + 1], k.c("minus_half", r, 0, 1), ALU.pow).then_inc(s["rs1"], 1)

            root(0)
            for t in range(NT):
                if t % 4 != 3 and t + 1 < NT:
                    root(t + 1)
                r = rows(t)
                pool.wait_ge(s["xh1"], t + 1)
                nc.gpsimd.tensor_tensor(acc[0:r, t, :], b["x_res"][0:r, t % XB, :], b["lw"][0:r, :], ALU.mult).then_inc(s["acc_mul"], 1)
                pool.wait_ge(s["acc_mul"], t + 1)
                nc.gpsimd.tensor_tensor(acc[0:r, t, :], acc[0:r, t, :], b["lb"][0:r, :], ALU.add).then_inc(s["acc_done"], 1)
                if t % 4 == 3:
                    root(t + 1)

        @block.scalar
        def _(act):
            act.wait_ge(s["ln1_par"], 64)
            n = 0
            for t0, cnt in groups:
                w = sum(rows(t0 + j) for j in range(cnt))
                for kk in range(KD):
                    act.wait_ge(s["x1_psum"], n + 1)
                    nc.scalar.activation(x1t[:, kk, t0 * P:t0 * P + w], k.ps[4 + n % 4][:, 0:w], ACT.Identity,
                                         bias=b["lbc"][:, kk:kk + 1], scale=b["lwc"][:, kk:kk + 1]).then_inc(s["x1_done"], 1)
                    n += 1


def route(k, x1t, gate):
    nc, io = k.nc, k.io
    NL = GROUPS + NE
    st, b, s = phase(k, "route", dict(w_r=[P, KD, NL], bias_r=[P, NL], logit=[P, NT, NL], top=[P, NT, 4], hot_g=[P, NT, GROUPS], hot1=[P, NT, PER], hot2=[P, NT, PER],
                              left=[P, NT, 1], le=[P, NT, PER], le2=[P, NT, PER], prod=[P, NT, GROUPS, PER], eg=[P, NT, GROUPS]),
                     ["r_loaded", "logit_mm", "r_chain", "r_exp", "r_args"])
    with st, nc.Block() as block:
        @block.sync
        def _(sp):
            with nc.allow_non_contiguous_dma(reason="narrow router weights"):
                sp.dma_start(b["w_r"][:, :, 0:GROUPS], io["moe_w_group"][0].rearrange("(k p) n -> p k n", p=P)).then_inc(s["r_loaded"], 16)
                sp.dma_start(b["w_r"][:, :, GROUPS:NL], io["moe_w_expert"][0].rearrange("(k p) n -> p k n", p=P)).then_inc(s["r_loaded"], 16)
                sp.dma_start(b["bias_r"][:, 0:GROUPS], io["moe_b_group"][0].partition_broadcast(P)).then_inc(s["r_loaded"], 16)
                sp.dma_start(b["bias_r"][:, GROUPS:NL], io["moe_b_expert"][0].partition_broadcast(P)).then_inc(s["r_loaded"], 16)

        @block.tensor
        def _(pe):
            pe.wait_ge(s["r_loaded"], 64)
            for t in range(NT):
                r = rows(t)
                if t == 8:
                    pe.wait_ge(s["r_chain"], 2)
                for kk in range(KD):
                    mm = nc.tensor.matmul(k.ps[t % 8][0:r, 32 * (t // 8):32 * (t // 8) + NL], x1t[:, kk, t * P:t * P + r], b["w_r"][:, kk, :], start=(kk == 0), stop=(kk == KD - 1))
                mm.then_inc(s["logit_mm"], 1)

        @block.scalar
        def _(act):
            act.wait_ge(s["r_args"], 1)
            nc.scalar.activation(b["eg"][:, :, :], b["eg"][:, :, :], ACT.Exp)
            nc.scalar.activation(b["top"][:, :, 2], b["top"][:, :, 2], ACT.Exp).then_inc(s["r_exp"], 1)

        @block.vector
        def _(dve):
            count = [0]

            def chain(ins):
                count[0] += 1
                ins.then_inc(s["r_chain"], 1)
                dve.wait_ge(s["r_chain"], count[0])

            def first_max(hot, val, mx, n):
                chain(nc.vector.tensor_reduce(mx, val, AX.X, ALU.max))
                chain(nc.vector.tensor_tensor(hot, val, mx.unsqueeze(2).to_broadcast([P, NT, n]), ALU.is_equal))
                chain(nc.vector.memset(b["left"][:, :, :], 1.0))
                for j in range(n):
                    chain(nc.vector.tensor_tensor(hot[:, :, j:j + 1], hot[:, :, j:j + 1], b["left"][:, :, :], ALU.mult))
                    chain(nc.vector.tensor_tensor(b["left"][:, :, :], b["left"][:, :, :], hot[:, :, j:j + 1], ALU.subtract))

            chain(nc.vector.memset(b["logit"][:, :, :], 0.0))
            dve.wait_ge(s["r_loaded"], 64)
            for t in range(NT):
                r = rows(t)
                dve.wait_ge(s["logit_mm"], t + 1)
                chain(nc.vector.tensor_tensor(b["logit"][0:r, t, :], k.ps[t % 8][0:r, 32 * (t // 8):32 * (t // 8) + NL], b["bias_r"][0:r, :], ALU.add))
            top = b["top"]
            lg = b["logit"][:, :, 0:GROUPS]
            first_max(b["hot_g"][:, :, :], lg, top[:, :, 0], GROUPS)
            chain(nc.vector.tensor_tensor(b["eg"][:, :, :], lg, top[:, :, 0:1].to_broadcast([P, NT, GROUPS]), ALU.subtract))
            for t in range(NT):
                chain(nc.vector.tensor_tensor(b["prod"][:, t], b["logit"][:, t, GROUPS:NL].rearrange("p (g j) -> p g j", g=GROUPS),
                                              b["hot_g"][:, t, :].unsqueeze(2).to_broadcast([P, GROUPS, PER]), ALU.mult))
            chain(nc.vector.tensor_reduce(b["le"][:, :, :], b["prod"][:, :, :, :].rearrange("p t g j -> p t j g"), AX.X, ALU.add))
            first_max(b["hot1"][:, :, :], b["le"][:, :, :], top[:, :, 1], PER)
            chain(nc.vector.scalar_tensor_tensor(b["le2"][:, :, :], b["hot1"][:, :, :], NEG, b["le"][:, :, :], ALU.mult, ALU.add))
            first_max(b["hot2"][:, :, :], b["le2"][:, :, :], top[:, :, 2], PER)
            nc.vector.tensor_tensor(top[:, :, 2], top[:, :, 2], top[:, :, 1], ALU.subtract).then_inc(s["r_args"], 1)
            dve.wait_ge(s["r_exp"], 1)
            chain(nc.vector.tensor_reduce(top[:, :, 0], b["eg"][:, :, :], AX.X, ALU.add))
            chain(nc.vector.tensor_scalar(top[:, :, 3], top[:, :, 2], 1.0, None, ALU.add))
            chain(nc.vector.tensor_tensor(top[:, :, 0], top[:, :, 0], top[:, :, 3], ALU.mult))
            chain(nc.vector.reciprocal(top[:, :, 0], top[:, :, 0]))
            chain(nc.vector.tensor_tensor(b["hot2"][:, :, :], b["hot2"][:, :, :], top[:, :, 2:3].to_broadcast([P, NT, PER]), ALU.mult))
            chain(nc.vector.tensor_tensor(b["hot1"][:, :, :], b["hot1"][:, :, :], b["hot2"][:, :, :], ALU.add))
            chain(nc.vector.tensor_tensor(b["hot1"][:, :, :], b["hot1"][:, :, :], top[:, :, 0:1].to_broadcast([P, NT, PER]), ALU.mult))
            for t in range(NT):
                nc.vector.tensor_tensor(gate[:, t], b["hot_g"][:, t, :].unsqueeze(2).to_broadcast([P, GROUPS, PER]),
                                        b["hot1"][:, t, :].unsqueeze(1).to_broadcast([P, GROUPS, PER]), ALU.mult)


def experts(k, x1t, gate, acc):
    nc, io = k.nc, k.io
    UU = 2 * len(NCH)
    DU = 2 * NT
    st, b, s = phase(k, "moe", dict(wg=[P, 2, KD, FE], wu=[P, 2, KD, FE], wd=[P, 2, 2, D], sg=[P, 2, 512], hid=[P, 2, 2, T]),
                     ["up_mm", "sg_done", "silu_done", "hid_done", "down_mm", "down_read"] + [f"wgu_loaded{i}" for i in range(2)] + [f"wd_loaded{i}" for i in range(2)])

    def up(eng, e, x, f):
        for fh in range(2):
            for n in range(len(NCH)):
                f(fh * len(NCH) + n, fh, n)

    with st, nc.Block() as block:
        @block.sync
        def _(sp):
            def load(e, x, first):
                sl = bass.ds(e, 1)
                if not first:
                    sp.wait_ge(s["up_mm"], (e - 1) * UU)
                sp.dma_start(b["wg"][:, x], io["moe_w_gate"][0, sl].rearrange("o (k p) f -> p (o k) f", p=P)).then_inc(s[f"wgu_loaded{x}"], 16)
                sp.dma_start(b["wu"][:, x], io["moe_w_up"][0, sl].rearrange("o (k p) f -> p (o k) f", p=P)).then_inc(s[f"wgu_loaded{x}"], 16)
                if not first:
                    sp.wait_ge(s["down_mm"], (e - 1) * DU)
                sp.dma_start(b["wd"][:, x], io["moe_w_down"][0, sl].rearrange("o (c p) d -> p (o c) d", p=P)).then_inc(s[f"wd_loaded{x}"], 16)
            load(0, 0, True)
            load(1, 1, True)
            with sp.Fori(1, NE // 2) as r:
                for x in range(2):
                    load(r * 2 + x, x, False)

        @block.tensor
        def _(pe):
            def ups(e, x, r, first):
                pe.wait_ge(s[f"wgu_loaded{x}"], r * 32 + 32)
                for u in range(UU):
                    fh, (a0, w) = u // len(NCH), NCH[u % len(NCH)]
                    if not (first and u < 2):
                        pe.wait_ge(s["hid_done"], e * UU + (u - 1))
                    for bank, wt in ((u % 2, b["wg"]), (2 + u % 2, b["wu"])):
                        for kk in range(KD):
                            mm = nc.tensor.matmul(k.ps[bank][:, 0:w], wt[:, x, kk, fh * P:(fh + 1) * P], x1t[:, kk, a0:a0 + w], start=(kk == 0), stop=(kk == KD - 1))
                    mm.then_inc(s["up_mm"], 1)

            def downs(e, x, r, first):
                pe.wait_ge(s[f"wd_loaded{x}"], r * 16 + 16)
                pe.wait_ge(s["hid_done"], (e + 1) * UU)
                for q in range(DU):
                    t, half = q // 2, q % 2
                    rr = rows(t)
                    g = (x * DU + q) % 4
                    if not (first and q < 4):
                        pe.wait_ge(s["down_read"], e * DU + (q - 3))
                    for c in range(2):
                        mm = nc.tensor.matmul(k.ps[4 + g][0:rr, :], b["hid"][:, x, c, t * P:t * P + rr], b["wd"][:, x, c, half * 512:(half + 1) * 512], start=(c == 0), stop=(c == 1))
                    mm.then_inc(s["down_mm"], 1)

            ups(0, 0, 0, True)
            ups(1, 1, 0, False)
            downs(0, 0, 0, True)
            with pe.Fori(1, NE // 2) as r:
                ups(r * 2, 0, r, False)
                downs(r * 2 - 1, 1, r - 1, False)
                ups(r * 2 + 1, 1, r, False)
                downs(r * 2, 0, r, False)
            downs(NE - 1, 1, NE // 2 - 1, False)

        @block.scalar
        def _(act):
            def sigmoids(e, first):
                for u in range(UU):
                    w = NCH[u % len(NCH)][1]
                    act.wait_ge(s["up_mm"], e * UU + (u + 1))
                    if not (first and u < 2):
                        act.wait_ge(s["hid_done"], e * UU + (u - 1))
                    nc.scalar.activation(b["sg"][:, u % 2, 0:w], k.ps[u % 2][:, 0:w], ACT.Sigmoid).then_inc(s["sg_done"], 1)
            sigmoids(0, True)
            with act.Fori(1, NE) as e:
                sigmoids(e, False)

        @block.vector
        def _(dve):
            def hidden(e, x, first):
                for u in range(UU):
                    fh, (a0, w) = u // len(NCH), NCH[u % len(NCH)]
                    dve.wait_ge(s["sg_done"], e * UU + (u + 1))
                    sg = b["sg"][:, u % 2, 0:w]
                    nc.vector.tensor_tensor(sg, sg, k.ps[u % 2][:, 0:w], ALU.mult).then_inc(s["silu_done"], 1)
                    dve.wait_ge(s["silu_done"], e * UU + (u + 1))
                    if u == 0 and not first:
                        dve.wait_ge(s["down_mm"], (e - 1) * DU)
                    nc.vector.tensor_tensor(b["hid"][:, x, fh, a0:a0 + w], sg, k.ps[2 + u % 2][:, 0:w], ALU.mult).then_inc(s["hid_done"], 1)

            def add(e, x):
                for q in range(DU):
                    t, half = q // 2, q % 2
                    rr = rows(t)
                    dve.wait_ge(s["down_mm"], e * DU + (q + 1))
                    dst = acc[0:rr, t, half * 512:(half + 1) * 512]
                    wgt = gate[0:rr, t].rearrange("p g j -> p (g j)")[:, bass.ds(e, 1)]
                    nc.vector.scalar_tensor_tensor(dst, k.ps[4 + (x * DU + q) % 4][0:rr, :], wgt, dst, ALU.mult, ALU.add).then_inc(s["down_read"], 1)

            hidden(0, 0, True)
            hidden(1, 1, True)
            add(0, 0)
            with dve.Fori(1, NE // 2) as r:
                hidden(r * 2, 0, False)
                add(r * 2 - 1, 1)
                hidden(r * 2 + 1, 1, False)
                add(r * 2, 0)
            add(NE - 1, 1)


def final_norm(k, acc):
    nc, io = k.nc, k.io
    st, b, s = phase(k, "final", dict(l2w=[P, D], l2b=[P, D], stats2=[P, NT, 12], mv2=[P, NT, 2], ve2=[P, NT], rstd2=[P, NT]),
                     ["ln2_par", "st2", "mv2_done", "ve2_done", "rs2", "xh2", "y_mul", "y_done", "y_stored"])
    with st, nc.Block() as block:
        @block.sync
        def _(sp):
            sp.dma_start(b["l2w"][:, :], io["ln2_w"][0].partition_broadcast(P)).then_inc(s["ln2_par"], 16)
            sp.dma_start(b["l2b"][:, :], io["ln2_b"][0].partition_broadcast(P)).then_inc(s["ln2_par"], 16)
            for t in range(NT):
                sp.wait_ge(s["y_done"], t + 1)
                dst = io["y_prompt"][0, t * P:(t + 1) * P, :] if t < PT else io["y_sample"].rearrange("b t d -> (b t) d")
                sp.dma_start(dst, acc[0:rows(t), t, :]).then_inc(s["y_stored"], 16)
            sp.wait_ge(s["y_stored"], 16 * NT)

        @block.vector
        def _(dve):
            for t in range(NT):
                r = rows(t)
                for half in range(2):
                    nc.vector.bn_stats(b["stats2"][0:r, t, 6 * half:6 * half + 6], acc[0:r, t, 512 * half:512 * half + 512]).then_inc(s["st2"], 1)
            dve.wait_ge(s["st2"], 2 * NT)
            for t in range(NT):
                nc.vector.bn_aggr(b["mv2"][0:rows(t), t, :], b["stats2"][0:rows(t), t, :]).then_inc(s["mv2_done"], 1)
            dve.wait_ge(s["mv2_done"], NT)
            for r, t0, t1 in ((P, 0, PT), (ND, PT, NT)):
                nc.vector.tensor_scalar(b["ve2"][0:r, t0:t1], b["mv2"][0:r, t0:t1, 1], EPS, None, ALU.add).then_inc(s["ve2_done"], 1)
            dve.wait_ge(s["ln2_par"], 32)
            dve.wait_ge(s["rs2"], 2)
            for t in range(NT):
                r = rows(t)
                x = acc[0:r, t, :]
                nc.vector.tensor_scalar(x, x, b["mv2"][0:r, t, 0:1], b["rstd2"][0:r, t:t + 1], ALU.subtract, ALU.mult).then_inc(s["xh2"], 1)
                dve.wait_ge(s["xh2"], t + 1)
                nc.vector.tensor_tensor(x, x, b["l2w"][0:r, :], ALU.mult).then_inc(s["y_mul"], 1)

        @block.gpsimd
        def _(pool):
            pool.wait_ge(s["ve2_done"], 2)
            for r, t0, t1 in ((P, 0, PT), (ND, PT, NT)):
                nc.gpsimd.tensor_tensor(b["rstd2"][0:r, t0:t1], b["ve2"][0:r, t0:t1], k.c("minus_half", r, 0, t1 - t0), ALU.pow).then_inc(s["rs2"], 1)
            for t in range(NT):
                r = rows(t)
                pool.wait_ge(s["y_mul"], t + 1)
                nc.gpsimd.tensor_tensor(acc[0:r, t, :], acc[0:r, t, :], b["l2b"][0:r, :], ALU.add).then_inc(s["y_done"], 1)


def build(nc, io):
    with ExitStack() as stack:
        k = Core(nc, stack, io)

        def left(st, name, shape):
            return st.enter_context(nc.sbuf_tensor(name, shape, F32))

        zd = left(stack, "z_dec", [P, 1, ZW])
        td = {n: left(stack, f"new_{n}_t", [P, 2, ND]) for n in ("nq", "mq", "fq", "mk", "fk")}
        td |= {n: left(stack, f"new_{n}_t", [P, ND]) for n in ("kcv", "ksel", "kwin")}
        a = {"sc": left(stack, "token_scalars", [P, NT, 12])}
        right_kcv, right_xt = ExitStack(), ExitStack()
        kcv = right_kcv.enter_context(nc.sbuf_tensor("kcv_t_p", [P, SEQ], F32, side="right"))
        xt = right_xt.enter_context(nc.sbuf_tensor("x_t", [P, KD, T], F32, side="right"))
        normalise_input(k, xt)
        with ExitStack() as att:
            z = left(att, "z", [P, PT, ZW])
            tb = {n: left(att, f"{n}_t", [P, 2, SEQ]) for n in ("nq", "mq", "fq", "mk", "fk")}
            tb |= {n: left(att, f"{n}_t", [P, SEQ]) for n in ("ksel", "kwin")}
            tb["kcv"] = kcv
            project(k, xt, z, tb, zd, td)
            right_xt.close()
            log_sigmoid_and_gates(k, z, zd, a)
            a |= {"u": left(att, "u", [P, PT, H]), "exp_neg_m": left(att, "exp_neg_m", [P, PT, H]), "cm": left(att, "neg_cm", [P, H, SEQ]),
                  "fneg": left(att, "neg_f_rows", [P, H, SEQ]), "kc": left(att, "kc", [P, 32]), "vc": left(att, "vc", [P, BW])}
            prompt_setup(k, z, tb, a)
            right_kcv.close()
            prompt_attention(k, z, tb, a)
        nc.clear_and_free_semaphores(k.used)
        nc.all_engine_barrier()
        decode_mixers(k, zd, td, a)
        with ExitStack() as ys:
            y = ys.enter_context(nc.sbuf_tensor("y_t", [P, KD, T], F32, side="right"))
            merge_branches(k, y)
            acc, x1t = left(stack, "acc", [P, NT, D]), left(stack, "x1_t", [P, KD, T])
            gate = left(stack, "gate", [P, NT, GROUPS, PER])
            mix_out_norm(k, y, x1t, acc)
        route(k, x1t, gate)
        experts(k, x1t, gate, acc)
        final_norm(k, acc)


INS = ["x_prompt", "x_sample", "cache_nsa", "cache_nsa_win", "cache_fox_kv", "cache_fox_logf", "state_mlstm_c", "state_mlstm_n",
       "state_mlstm_m", "page_table", "ln_in_w", "ln_in_b", "w_in", "b_in", "nsa_w_ck", "nsa_w_cv", "mlstm_norm_w", "w_branch", "w_out",
       "ln1_w", "ln1_b", "moe_w_group", "moe_b_group", "moe_w_expert", "moe_b_expert", "moe_w_gate", "moe_w_up", "moe_w_down", "ln2_w", "ln2_b"]
OUTS = [("y_prompt", (1, SEQ, D)), ("y_sample", (DB, DT, D)), ("p_nsa_rows", (1, 1, SEQ, 4, HD)), ("p_nsa_win", (1, 1, WIN, 2, HD)),
        ("p_fox_kv", (1, 1, SEQ, 2, H, HD)), ("p_fox_logf", (1, 1, SEQ, H)), ("p_mlstm_c", (1, 1, H, HD, HD)), ("p_mlstm_n", (1, 1, H, HD)),
        ("p_mlstm_m", (1, 1, H)), ("s_nsa_rows", (1, DB, DT, 4, HD)), ("s_nsa_win", (1, DB, PAST, 2, HD)), ("s_fox_kv", (1, DB, DT, 2, H, HD)),
        ("s_fox_logf", (1, DB, DT, H)), ("s_mlstm_c", (1, DB, H, HD, HD)), ("s_mlstm_n", (1, DB, H, HD)), ("s_mlstm_m", (1, DB, H))]


def kernel(**inputs):
    import concourse.bacc as bacc
    from concourse.bass_utils import run_bass_kernel_spmd

    nc = bacc.Bacc("TRN2", target_bir_lowering=False, num_devices=1)
    arrays = {f"in_{n}": np.ascontiguousarray(inputs[n]) for n in INS}
    arrays |= {"in_table": TABLE, "in_alibi": ALIBI}
    io = {n[3:]: nc.dram_tensor(n, a.shape, mybir.dt.from_np(a.dtype), kind="ExternalInput").ap() for n, a in arrays.items()}
    io |= {n: nc.dram_tensor(f"out_{n}", shape, F32, kind="ExternalOutput").ap() for n, shape in OUTS}
    build(nc, io)
    r = run_bass_kernel_spmd(nc, [arrays], core_ids=[0])
    return tuple(r.results[0][f"out_{n}"] for n, _ in OUTS)
```

```python
from contextlib import ExitStack

import numpy as np
import concourse.bass as bass
from concourse import mybir

F32 = mybir.dt.float32
I32 = mybir.dt.int32
ALU = mybir.AluOpType
ACT = mybir.ActivationFunctionType
AX = mybir.AxisListType

P = 128
D = 1024
KD = D // P
SEQ, DB, DT = 1024, 8, 8
PT = SEQ // P
ND = DB * DT
NT = PT + 1
T = SEQ + ND
H, HD = 4, 64
BW = H * HD
BLK = 64
NCB = SEQ // BLK
PAST = 256
PAGE = 128
NPG = PAST // PAGE
DCB = PAST // BLK
WIN = 512
SCALE = HD ** -0.5
EPS = 1e-5
TINY = 1e-30
NEG = -1e30
FLOOR = -1e20
ALPHA = 2.0 ** 0.25
NE, FE = 16, 256
GROUPS, PER = 4, 4
CAP = 192
ROUNDS = -(-T // CAP)
SLOTS = ROUNDS * CAP
SLOPES = [2.0 ** (-8.0 * (h + 1) / H) for h in range(H)]

C_NQ, C_NKV, C_MQ, C_MK, C_MV, C_MO, C_FQ, C_FK, C_FV, C_GM = 0, 256, 652, 908, 1164, 1420, 1684, 1940, 2196, 2456
NIN = C_GM + 3 * D
Z_KC, Z_VC, Z_KS, Z_VS, Z_KW, Z_VW, Z_NG = 0, 64, 128, 192, 256, 320, 384
Z_MK = 396
Z_MV = 652
VW1 = HD + 1
Z_MO = Z_MV + H * VW1
Z_MI = Z_MO + BW
Z_MF = Z_MI + H
Z_FK = Z_MF + H
Z_FV = Z_FK + BW
Z_FF = Z_FV + BW
ZW = Z_FF + H
CHUNKS = [(True, C_NQ, 256, 0), (False, 256, 256, 0), (False, 512, 140, 256),
          (True, C_MQ, 256, 1), (False, C_MK, 256, Z_MK), (False, C_MV, 256, Z_MV), (False, C_MO, 264, Z_MO),
          (True, C_FQ, 256, 2), (False, C_FK, 256, Z_FK), (False, C_FV, 260, Z_FV)]
CW = 264
NCH = [(0, 512), (512, 512), (1024, ND)]


def rows(t):
    return P if t < PT else ND


def const_tables():
    p = np.arange(P)
    c = np.arange(P)
    out, at, cols = {}, {}, 0

    def put(name, a):
        nonlocal cols
        a = np.asarray(a, np.float32)
        full = np.zeros((P, a.shape[1]), np.float32)
        full[:a.shape[0]] = a
        out[name], at[name] = full, (cols, cols + a.shape[1])
        cols += a.shape[1]

    put("ident", np.eye(P))
    put("ones", np.ones((P, P)))
    put("minus_half", np.full((P, 16), -0.5))
    put("upto", p[:, None] <= c[None, :])
    put("after", p[:, None] > c[None, :])
    put("mask_future", np.where(c[None, :] > p[:, None], NEG, 0.0))
    put("mask_future_t", np.where(p[:, None] > c[None, :], NEG, 0.0))
    put("mask_window", np.where(c[None, :] <= p[:, None], NEG, 0.0))
    cb = np.full((P, PT, H, 32), NEG)
    for i in range(PT):
        for h in range(H):
            for j in range(NCB):
                dist = i * P + p - (j * BLK + BLK - 1)
                cb[:, i, h, j] = np.where(dist >= 0, -SLOPES[h] * dist, NEG)
    put("cmp_bias", cb.reshape(P, -1))
    token = np.arange(NT)[None, :] * P + p[:, None]
    put("slot_entry", np.stack([token, 2 * token, token, 2 * token + 1], axis=-1).reshape(P, -1))
    put("slot_base", np.broadcast_to(np.arange(NE)[None, :] * SLOTS - 1, (P, NE)))
    put("head_bcast", np.repeat(np.eye(H), P, axis=1))
    split = cols
    b4, hh, tt = p // 32, (p // 8) % 4, p % 8
    slope = np.array(SLOPES)[hh]
    sb = np.zeros((P, 2, PAST + ND))
    cd = np.zeros((P, 2, DB * DCB))
    fb = np.zeros((P, 2, PAST + ND))
    mn = np.zeros((P, 2, ND))
    k = np.arange(PAST)
    n = np.arange(ND)
    for g in range(2):
        b = 4 * g + b4
        sb[:, g, :PAST] = -slope[:, None] * (PAST + tt[:, None] - k[None, :])
        own = (n[None, :] // DT == b[:, None]) & (n[None, :] % DT <= tt[:, None])
        sb[:, g, PAST:] = np.where(own, -slope[:, None] * (tt[:, None] - n[None, :] % DT), NEG)
        mn[:, g] = np.where(own, 0.0, NEG)
        j = np.arange(DB * DCB)
        dist = PAST + tt[:, None] - (j[None, :] % DCB * BLK + BLK - 1)
        fb[:, g, PAST:] = mn[:, g]
        cd[:, g] = np.where(j[None, :] // DCB == b[:, None], -slope[:, None] * dist, NEG)
    put("dec_bias", sb.reshape(P, -1))
    put("dec_fox_bias", fb.reshape(P, -1))
    put("dec_cmp_bias", cd.reshape(P, -1))
    put("dec_mask", mn.reshape(P, -1))
    put("head_of_row", hh[:, None] == np.arange(H)[None, :])
    bn, tn = n // DT, n % DT
    brow = np.concatenate([b4, 4 + b4])
    trow = np.concatenate([tt, tt])
    put("row_of_token", (bn[:, None] == brow) & (tn[:, None] == trow))
    put("upto_row", (bn[:, None] == brow) & (tn[:, None] <= trow))
    put("batch_of_row", bn[:, None] == brow)
    put("dec_after", (bn[:, None] == bn[None, :]) & (tn[:, None] > tn[None, :]))
    put("batch_of_token", bn[:, None] == np.arange(DB)[None, :])
    put("batch_to_row", np.arange(DB)[:, None] == brow)
    put("head_rows", np.arange(H)[:, None] == np.arange(BW)[None, :] // HD)
    table = np.concatenate([out[n] for n in out], axis=1)
    dist = (PT - 1) * P + p[:, None] - np.arange(SEQ)[None, :]
    alibi = np.stack([np.where(dist >= 0, -s * dist, NEG) for s in SLOPES], axis=1).astype(np.float32)
    return np.ascontiguousarray(table), at, split, np.ascontiguousarray(alibi)


TABLE, TABLE_AT, SPLIT, ALIBI = const_tables()
EMPTY_SLOTS = np.stack([np.zeros(NE * SLOTS), 2 * T + np.arange(NE * SLOTS) % CAP], axis=1).astype(np.int32)
TABLE_W = TABLE.shape[1]


class Core:

    def __init__(self, nc, stack, io):
        self.nc, self.io, self.used = nc, io, []
        self.const = stack.enter_context(nc.sbuf_tensor("const", [P, SPLIT], F32))
        self.dec_const = None
        self.psum = stack.enter_context(nc.psum_tensor("psum", [P, 8, 512], F32))
        self.ps = [self.psum[:, i, :] for i in range(8)]
        self.xn_dram = nc.dram_tensor("xn_scratch", [NT * P, D], F32).ap()
        self.xt_dram = nc.dram_tensor("xt_scratch", [P, KD * T], F32).ap()
        self.x1_dram = nc.dram_tensor("x1_scratch", [T, D], F32).ap()
        self.y_dram = nc.dram_tensor("expert_rows", [2 * T + CAP, D], F32).ap()
        self.idx_dram = nc.dram_tensor("slot_tokens", [NE * SLOTS, 2], I32).ap()
        self.br_dram = nc.dram_tensor("branch_scratch", [P, 6 * T], F32).ap()

    def c(self, name, n=P, lo=0, hi=None):
        a, b = TABLE_AT[name]
        if a >= SPLIT:
            return self.dec_const[0:n, a - SPLIT + lo:(b - SPLIT if hi is None else a - SPLIT + hi)]
        return self.const[0:n, a + lo:(b if hi is None else a + hi)]


INDICES = ("page_table", "idx_all", "idx_from", "idx_to", "slot", "entry")


def phase(k, tag, sbs, sems):
    nc, st = k.nc, ExitStack()
    b = {n: st.enter_context(nc.sbuf_tensor(f"{tag}_{n}", shape, I32 if n in INDICES else F32)) for n, shape in sbs.items()}
    s = {n: nc.alloc_semaphore(f"{tag}_{n}") for n in sems}
    k.used += s.values()
    return st, b, s


def normalise_input(k, xt):
    nc, io = k.nc, k.io
    XB = NT
    st, b, s = phase(k, "ln_in", dict(
        x_in=[P, XB, D], ln_w=[P, D], ln_b=[P, D], lnw_col=[P, KD], lnb_col=[P, KD], x_norm=[P, 2, D],
        stats=[P, 12], mean_var=[P, NT, 2], var_eps=[P, NT], rstd=[P, NT]),
        ["const_loaded", "lnin_par", "stats_done", "mv_done", "ve_done", "rstd_done", "xhat_done", "xt_psum", "xt_done",
         "xscaled", "xnorm_done"] + [f"x_loaded{i}" for i in range(XB)] + [f"xnorm_stored{i}" for i in range(2)])
    groups = [(0, 4), (4, 4), (8, 1)]
    src = lambda t: io["x_prompt"][0, t * P:(t + 1) * P, :] if t < PT else io["x_sample"].rearrange("b t d -> (b t) d")
    with st, nc.Block() as block:
        @block.sync
        def _(sp):
            def load(t):
                sp.dma_start(b["x_in"][0:rows(t), t % XB, :], src(t)).then_inc(s[f"x_loaded{t % XB}"], 16)
            load(0)
            sp.dma_start(k.const[:, :], io["table"][:, 0:SPLIT]).then_inc(s["const_loaded"], 16)
            for t in range(1, 4):
                load(t)
            with nc.allow_non_contiguous_dma(reason="1024 values to columns"):
                sp.dma_start(b["lnw_col"][:, :], io["ln_in_w"].rearrange("(k p) -> p k", p=P)).then_inc(s["lnin_par"], 16)
                sp.dma_start(b["lnb_col"][:, :], io["ln_in_b"].rearrange("(k p) -> p k", p=P)).then_inc(s["lnin_par"], 16)
            sp.dma_start(b["ln_w"][:, :], io["ln_in_w"].partition_broadcast(P)).then_inc(s["lnin_par"], 16)
            sp.dma_start(b["ln_b"][:, :], io["ln_in_b"].partition_broadcast(P)).then_inc(s["lnin_par"], 16)
            for t in range(4, NT):
                load(t)
            for t in range(NT):
                sp.wait_ge(s["xnorm_done"], t + 1)
                sp.dma_start(k.xn_dram[t * P:t * P + rows(t), :], b["x_norm"][0:rows(t), t % 2, :]).then_inc(s[f"xnorm_stored{t % 2}"], 16)
            sp.wait_ge(s["xnorm_stored0"], 16 * ((NT + 1) // 2))
            sp.wait_ge(s["xnorm_stored1"], 16 * (NT // 2))

        @block.vector
        def _(dve):
            def statistics(t):
                r = rows(t)
                x = b["x_in"][0:r, t % XB, :]
                dve.wait_ge(s[f"x_loaded{t % XB}"], 16 * (t // XB + 1))
                nc.vector.bn_stats(b["stats"][0:r, 0:6], x[:, 0:512]).then_inc(s["stats_done"], 1)
                nc.vector.bn_stats(b["stats"][0:r, 6:12], x[:, 512:1024]).then_inc(s["stats_done"], 1)
                dve.wait_ge(s["stats_done"], 2 * t + 2)
                nc.vector.bn_aggr(b["mean_var"][0:r, t, :], b["stats"][0:r, :]).then_inc(s["mv_done"], 1)
                dve.wait_ge(s["mv_done"], t + 1)
                nc.vector.tensor_scalar(b["var_eps"][0:r, t:t + 1], b["mean_var"][0:r, t, 1:2], EPS, None, ALU.add).then_inc(s["ve_done"], 1)

            statistics(0)
            for t in range(NT):
                if t + 1 < NT:
                    statistics(t + 1)
                r = rows(t)
                x = b["x_in"][0:r, t % XB, :]
                dve.wait_ge(s["rstd_done"], t + 1)
                nc.vector.tensor_scalar(x, x, b["mean_var"][0:r, t, 0:1], b["rstd"][0:r, t:t + 1], ALU.subtract, ALU.mult).then_inc(s["xhat_done"], 1)

        @block.gpsimd
        def _(pool):
            pool.wait_ge(s["lnin_par"], 64)
            pool.wait_ge(s["const_loaded"], 16)

            def root(t):
                r = rows(t)
                pool.wait_ge(s["ve_done"], t + 1)
                nc.gpsimd.tensor_tensor(b["rstd"][0:r, t:t + 1], b["var_eps"][0:r, t:t + 1], k.c("minus_half", r, 0, 1), ALU.pow).then_inc(s["rstd_done"], 1)

            root(0)
            for t in range(NT):
                if t + 1 < NT:
                    root(t + 1)
                r = rows(t)
                xn = b["x_norm"][0:r, t % 2, :]
                pool.wait_ge(s["xhat_done"], t + 1)
                if t >= 2:
                    pool.wait_ge(s[f"xnorm_stored{t % 2}"], 16 * (t // 2))
                nc.gpsimd.tensor_tensor(xn, b["x_in"][0:r, t % XB, :], b["ln_w"][0:r, :], ALU.mult).then_inc(s["xscaled"], 1)
                pool.wait_ge(s["xscaled"], t + 1)
                nc.gpsimd.tensor_tensor(xn, xn, b["ln_b"][0:r, :], ALU.add).then_inc(s["xnorm_done"], 1)

        @block.tensor
        def _(pe):
            pe.wait_ge(s["const_loaded"], 16)
            n = 0
            for t0, cnt in groups:
                pe.wait_ge(s["xhat_done"], t0 + cnt)
                for kk in range(KD):
                    if n >= 8:
                        pe.wait_ge(s["xt_done"], n - 7)
                    for j in range(cnt):
                        r = rows(t0 + j)
                        mm = nc.tensor.transpose(k.ps[n % 8][:, j * P:j * P + r], b["x_in"][0:r, (t0 + j) % XB, kk * P:(kk + 1) * P], k.c("ident", r, 0, r))
                    mm.then_inc(s["xt_psum"], 1)
                    n += 1

        @block.scalar
        def _(act):
            act.wait_ge(s["lnin_par"], 64)
            n = 0
            for t0, cnt in groups:
                w = sum(rows(t0 + j) for j in range(cnt))
                for kk in range(KD):
                    act.wait_ge(s["xt_psum"], n + 1)
                    nc.scalar.activation(xt[:, kk, t0 * P:t0 * P + w], k.ps[n % 8][:, 0:w], ACT.Identity,
                                         bias=b["lnb_col"][:, kk:kk + 1], scale=b["lnw_col"][:, kk:kk + 1]).then_inc(s["xt_done"], 1)
                    n += 1


def project(k, xt, z, tb, zd, td):
    nc, io = k.nc, k.io
    nchunk = len(CHUNKS)
    st, b, s = phase(k, "proj", dict(
        w_chunk=[P, 2, KD, CW], bias_z=[P, C_GM], bias_q=[P, 6]),
        ["bias_loaded", "mm_done", "feat_done", "tok_done", "turned", "turn_copied", "pj_stored"] + [f"w_loaded{i}" for i in range(2)])
    units = []
    for ci, (feat, c0, w, _) in enumerate(CHUNKS):
        if feat:
            units += [(ci, blk, n) for blk in range(2) for n in range(3)]
        else:
            units += [(ci, -1, t) for t in range(NT)]
    last = {ci: max(u for u, x in enumerate(units) if x[0] == ci) for ci in range(nchunk)}
    evac = []
    cf = ct = 0
    for ci, blk, n in units:
        if CHUNKS[ci][0]:
            cf += 1
            evac.append(("feat_done", cf))
        else:
            ct += 1
            evac.append(("tok_done", ct))
    MB = 6
    turns = [("kcv", Z_KC), ("ksel", Z_KS), ("kwin", Z_KW), ("mk0", Z_MK), ("mk1", Z_MK + P), ("fk0", Z_FK), ("fk1", Z_FK + P)]
    tgroups = [(0, 4), (4, 4), (8, 1)]

    def zz(t, c0, c1):
        return z[:, t, c0:c1] if t < PT else zd[0:ND, 0, c0:c1]

    with st, nc.Block() as block:
        @block.sync
        def _(sp):
            def load(ci):
                _, c0, w, _ = CHUNKS[ci]
                if ci >= 2:
                    sp.wait_ge(s["mm_done"], last[ci - 2] + 1)
                sp.dma_start(b["w_chunk"][:, ci % 2, :, 0:w], io["w_in"][0].rearrange("(k p) n -> p k n", p=P)[:, :, c0:c0 + w]).then_inc(s[f"w_loaded{ci % 2}"], 16)
            load(0)
            with nc.allow_non_contiguous_dma(reason="bias columns"):
                for j, c0 in enumerate((C_NQ, C_MQ, C_FQ)):
                    sp.dma_start(b["bias_q"][:, 2 * j:2 * j + 2], io["b_in"][0, c0:c0 + 256].rearrange("(k p) -> p k", p=P)).then_inc(s["bias_loaded"], 16)
            sp.dma_start(b["bias_z"][:, :], io["b_in"][0, 0:C_GM].partition_broadcast(P)).then_inc(s["bias_loaded"], 16)
            for ci in range(1, nchunk):
                load(ci)
            sp.dma_start(k.xt_dram, xt[:, :, :].rearrange("p k t -> p (k t)")).then_inc(s["pj_stored"], 16)
            sp.wait_ge(s["tok_done"], ct)
            tok = lambda c0, c1, a=0, e=PT: z[:, a:e, c0:c1]
            dec = lambda c0, c1: zd[0:ND, 0, c0:c1]
            n = 1
            sp.dma_start(io["p_nsa_rows"].rearrange("x y (t p) r d -> (x y p) t (r d)", p=P), tok(0, 256)).then_inc(s["pj_stored"], 16)
            sp.dma_start(io["p_nsa_win"].rearrange("x y (t p) r d -> (x y p) t (r d)", p=P), tok(Z_KW, Z_KW + 128, 4, 8)).then_inc(s["pj_stored"], 16)
            sp.dma_start(io["p_fox_kv"].rearrange("x y (t p) r h d -> (x y p) t (r h d)", p=P), tok(Z_FK, Z_FK + 512)).then_inc(s["pj_stored"], 16)
            sp.dma_start(io["s_nsa_rows"].rearrange("x b t r d -> (x b t) (r d)"), dec(0, 256)).then_inc(s["pj_stored"], 16)
            sp.dma_start(io["s_fox_kv"].rearrange("x b t r h d -> (x b t) (r h d)"), dec(Z_FK, Z_FK + 512)).then_inc(s["pj_stored"], 16)
            n += 5
            win = io["s_nsa_win"].rearrange("x b c r d -> (x b) c (r d)")
            sp.dma_start(win[:, 0:PAST - DT, :], io["cache_nsa_win"].rearrange("x b c r d -> (x b) c (r d)")[:, DT:PAST, :]).then_inc(s["pj_stored"], 16)
            n += 1
            for bb in range(DB):
                sp.dma_start(win[bb, PAST - DT:PAST, :], zd[bb * DT:(bb + 1) * DT, 0, Z_KW:Z_KW + 128]).then_inc(s["pj_stored"], 16)
                n += 1
            sp.wait_ge(s["pj_stored"], 16 * n)

        @block.tensor
        def _(pe):
            for u, (ci, blk, n) in enumerate(units):
                w = CHUNKS[ci][2]
                if u == 0 or units[u - 1][0] != ci:
                    pe.wait_ge(s[f"w_loaded{ci % 2}"], 16 * (ci // 2 + 1))
                if u >= MB:
                    pe.wait_ge(s[evac[u - MB][0]], evac[u - MB][1])
                for kk in range(KD):
                    if blk >= 0:
                        a, m = NCH[n]
                        mm = nc.tensor.matmul(k.ps[u % MB][:, 0:m], b["w_chunk"][:, ci % 2, kk, blk * P:(blk + 1) * P], xt[:, kk, a:a + m],
                                              start=(kk == 0), stop=(kk == KD - 1))
                    else:
                        r = rows(n)
                        mm = nc.tensor.matmul(k.ps[u % MB][0:r, 0:w], xt[:, kk, n * P:n * P + r], b["w_chunk"][:, ci % 2, kk, 0:w],
                                              start=(kk == 0), stop=(kk == KD - 1))
                mm.then_inc(s["mm_done"], 1)
            pe.wait_ge(s["tok_done"], ct)
            n = 0
            for name, c0 in turns:
                for t0, cnt in tgroups:
                    if n >= 2:
                        pe.wait_ge(s["turn_copied"], n - 1)
                    for j in range(cnt):
                        r = rows(t0 + j)
                        mm = nc.tensor.transpose(k.ps[6 + n % 2][:, j * P:j * P + r], zz(t0 + j, c0, c0 + P), k.c("ident", r, 0, r))
                    mm.then_inc(s["turned"], 1)
                    n += 1

        @block.vector
        def _(dve):
            dve.wait_ge(s["bias_loaded"], 64)
            for u, (ci, blk, t) in enumerate(units):
                feat, c0, w, z0 = CHUNKS[ci]
                if feat:
                    continue
                r = rows(t)
                dve.wait_ge(s["mm_done"], u + 1)
                src, bias, dst = k.ps[u % MB][0:r, 0:w], b["bias_z"][0:r, c0:c0 + w], zz(t, z0, z0 + w)
                if c0 == C_MV:
                    src, bias = (a.rearrange("p (h d) -> p h d", h=H) for a in (src, bias))
                    dst = zz(t, z0, z0 + H * VW1).rearrange("p (h d) -> p h d", h=H)[:, :, 0:HD]
                nc.vector.tensor_tensor(dst, src, bias, ALU.add).then_inc(s["tok_done"], 1)

        @block.gpsimd
        def _(pool):
            for x in (z[:, :, Z_MV:Z_MV + H * VW1], zd[:, :, Z_MV:Z_MV + H * VW1]):
                nc.gpsimd.memset(x.rearrange("p t (h d) -> p t h d", h=H)[:, :, :, HD:VW1], 1.0)

        @block.scalar
        def _(act):
            act.wait_ge(s["bias_loaded"], 64)
            for u, (ci, blk, n) in enumerate(units):
                feat, c0, w, which = CHUNKS[ci]
                if not feat:
                    continue
                a, m = NCH[n]
                act.wait_ge(s["mm_done"], u + 1)
                name = ("nq", "mq", "fq")[which]
                dst = tb[name][:, blk, a:a + m] if n < 2 else td[name][:, blk, :]
                nc.scalar.activation(dst, k.ps[u % MB][:, 0:m], ACT.Identity, bias=b["bias_q"][:, 2 * which + blk:2 * which + blk + 1]).then_inc(s["feat_done"], 1)
            n = 0
            for name, c0 in turns:
                for t0, cnt in tgroups:
                    w = sum(rows(t0 + j) for j in range(cnt))
                    act.wait_ge(s["turned"], n + 1)
                    src = k.ps[6 + n % 2]
                    dst, a = (tb, t0 * P) if t0 < PT else (td, 0)
                    if name == "kcv" and t0 >= PT:
                        nc.scalar.copy(dst["kcv"][:, 0:w], src[:, 0:w]).then_inc(s["turn_copied"], 1)
                    elif name in ("ksel", "kwin"):
                        nc.scalar.mul(dst[name][0:HD, a:a + w], src[0:HD, 0:w], SCALE)
                        nc.scalar.mul(dst[name][HD:P, a:a + w], src[0:HD, 0:w], SCALE).then_inc(s["turn_copied"], 1)
                    elif name == "kcv":
                        nc.scalar.copy(dst[name][:, a:a + w], src[:, 0:w]).then_inc(s["turn_copied"], 1)
                    else:
                        nc.scalar.mul(dst[name[:2]][:, int(name[2]), a:a + w], src[:, 0:w], SCALE).then_inc(s["turn_copied"], 1)
                    n += 1


def log_sigmoid_and_gates(k, z, zd, a):
    nc, io = k.nc, k.io
    st, b, s = phase(k, "gates", dict(neg=[P, NT, 8], neg_abs=[P, NT, 8], softplus=[P, NT, 8], least=[P, NT, 8]),
                     ["neg_done", "na_done", "e_done", "sp_done", "least_done", "sc_done", "gate_exp", "gate_one", "gate_done", "logf_stored"])
    parts = [(P, 0, PT), (ND, PT, NT)]
    zz = lambda t0, c0, c1: z[:, :, c0:c1] if t0 < PT else zd[0:ND, :, c0:c1]
    with st, nc.Block() as block:
        @block.vector
        def _(dve):
            for r, t0, t1 in parts:
                for j, c0 in enumerate((Z_MF, Z_FF)):
                    x = zz(t0, c0, c0 + H)
                    nc.vector.tensor_scalar(b["neg"][0:r, t0:t1, 4 * j:4 * j + 4], x, -1.0, None, ALU.mult).then_inc(s["neg_done"], 1)
                    nc.vector.tensor_scalar(b["least"][0:r, t0:t1, 4 * j:4 * j + 4], x, 0.0, None, ALU.min).then_inc(s["least_done"], 1)
                nc.vector.tensor_copy(a["sc"][0:r, t0:t1, 0:4], zz(t0, Z_MI, Z_MI + H))
            dve.wait_ge(s["least_done"], 4)
            dve.wait_ge(s["neg_done"], 4)
            for r, t0, t1 in parts:
                for j, c0 in enumerate((Z_MF, Z_FF)):
                    c = slice(4 * j, 4 * j + 4)
                    nc.vector.tensor_tensor(b["neg_abs"][0:r, t0:t1, c], zz(t0, c0, c0 + H), b["neg"][0:r, t0:t1, c], ALU.min).then_inc(s["na_done"], 1)
            dve.wait_ge(s["sp_done"], 2)
            for r, t0, t1 in parts:
                nc.vector.tensor_tensor(a["sc"][0:r, t0:t1, 4:12], b["least"][0:r, t0:t1, :], b["softplus"][0:r, t0:t1, :], ALU.subtract).then_inc(s["sc_done"], 1)
            n = 0
            for c0, w in ((Z_NG, 12), (Z_MO, BW)):
                for r, t0, t1 in parts:
                    x = zz(t0, c0, c0 + w)
                    n += 1
                    dve.wait_ge(s["gate_exp"], n)
                    nc.vector.tensor_scalar(x, x, 1.0, None, ALU.add).then_inc(s["gate_one"], 1)
                    dve.wait_ge(s["gate_one"], n)
                    nc.vector.reciprocal(x, x).then_inc(s["gate_done"], 1)

        @block.scalar
        def _(act):
            act.wait_ge(s["na_done"], 4)
            for r, t0, t1 in parts:
                nc.scalar.activation(b["neg_abs"][0:r, t0:t1, :], b["neg_abs"][0:r, t0:t1, :], ACT.Exp).then_inc(s["e_done"], 1)
            act.wait_ge(s["e_done"], 2)
            for r, t0, t1 in parts:
                nc.scalar.activation(b["softplus"][0:r, t0:t1, :], b["neg_abs"][0:r, t0:t1, :], ACT.Ln, bias=1.0).then_inc(s["sp_done"], 1)
            for c0, w in ((Z_NG, 12), (Z_MO, BW)):
                for r, t0, t1 in parts:
                    x = zz(t0, c0, c0 + w)
                    nc.scalar.activation(x, x, ACT.Exp, scale=-1.0).then_inc(s["gate_exp"], 1)

        @block.sync
        def _(sp):
            sp.wait_ge(s["sc_done"], 2)
            sp.dma_start(io["p_fox_logf"].rearrange("x y (t p) h -> (x y p) t h", p=P), a["sc"][:, 0:PT, 8:12]).then_inc(s["logf_stored"], 16)
            sp.dma_start(io["s_fox_logf"].rearrange("x b t h -> (x b t) h"), a["sc"][0:ND, PT, 8:12]).then_inc(s["logf_stored"], 16)
            sp.wait_ge(s["logf_stored"], 32)


def prompt_setup(k, z, tb, a):
    nc, io = k.nc, k.io
    st, b, s = phase(k, "setup", dict(
        sums=[P, PT, 8], neg_f=[P, PT, H], u_rows=[H, SEQ], f_rows=[H, SEQ], cm_rows=[H, SEQ], m_tok=[P, PT, H],
        w_state=[P, PT, H], w_cmp=[P, BLK, HD], state=[HD, H, VW1]),
        ["sums_mm", "sums_done", "u_done", "f_done", "rows_mm", "rows_done", "cm_done", "bc_mm", "bc_done", "cmt_mm", "m_done",
         "ws_arg", "ws_exp", "ws_done", "kw_done", "state_mm", "state_done", "wc_loaded", "kc_mm", "vc_mm", "cmp_zero",
         "setup_stored"])
    sc = a["sc"]
    with st, nc.Block() as block:
        @block.sync
        def _(sp):
            sp.dma_start(b["w_cmp"][0:HD], io["nsa_w_ck"][0].rearrange("p d e -> d p e")).then_inc(s["wc_loaded"], 16)
            sp.dma_start(b["w_cmp"][HD:P], io["nsa_w_cv"][0].rearrange("p d e -> d p e")).then_inc(s["wc_loaded"], 16)
            sp.wait_ge(s["m_done"], 1)
            sp.dma_start(io["p_mlstm_m"].rearrange("x y h -> (x y) h"), b["m_tok"][P - 1:P, PT - 1, :]).then_inc(s["setup_stored"], 16)
            sp.wait_ge(s["state_done"], H)
            sp.dma_start(io["p_mlstm_c"].rearrange("x y h d e -> (x y d) h e"), b["state"][:, :, 0:HD]).then_inc(s["setup_stored"], 16)
            with nc.allow_non_contiguous_dma(reason="the normaliser is a column of the state"):
                sp.dma_start(io["p_mlstm_n"].rearrange("x y h d -> (x y d) h"), b["state"][:, :, HD]).then_inc(s["setup_stored"], 16)
            sp.wait_ge(s["setup_stored"], 48)

        @block.tensor
        def _(pe):
            for i in range(PT):
                for j in range(i + 1):
                    lhs = k.c("upto") if j == 0 else k.c("ones")
                    rhs = sc[:, i if j == 0 else j - 1, 4:12]
                    mm = nc.tensor.matmul(k.ps[0][:, 8 * i:8 * i + 8], lhs, rhs, start=(j == 0), stop=(j == i))
            mm.then_inc(s["sums_mm"], 1)
            pe.wait_ge(s["wc_loaded"], 32)
            for p in range(BLK):
                mm = nc.tensor.matmul(k.ps[6][0:HD, 0:NCB], b["w_cmp"][0:HD, p, :], tb["kcv"][0:HD, p:SEQ:BLK], start=(p == 0), stop=(p == BLK - 1))
            mm.then_inc(s["kc_mm"], 1)
            for p in range(BLK):
                mm = nc.tensor.matmul(k.ps[7][0:NCB, 0:HD], tb["kcv"][HD:P, p:SEQ:BLK], b["w_cmp"][HD:P, p, :], start=(p == 0), stop=(p == BLK - 1))
            mm.then_inc(s["vc_mm"], 1)
            pe.wait_ge(s["u_done"], 1)
            pe.wait_ge(s["f_done"], 1)
            for n, src in enumerate((a["u"], b["neg_f"])):
                for i in range(PT):
                    mm = nc.tensor.transpose(k.ps[1 + 2 * n + i // 4][0:H, i % 4 * P:i % 4 * P + P], src[:, i, :], k.c("ident"))
                mm.then_inc(s["rows_mm"], 1)
            pe.wait_ge(s["cm_done"], 1)
            for i in range(PT):
                mm = nc.tensor.transpose(k.ps[5][:, 4 * i:4 * i + 4], b["cm_rows"][:, i * P:(i + 1) * P], k.c("ident", H, 0, H))
            mm.then_inc(s["cmt_mm"], 1)
            pe.wait_ge(s["rows_done"], 4)
            n = 0
            for src in (b["cm_rows"], b["f_rows"]):
                for h in range(H):
                    for half in range(2):
                        if n >= 4:
                            pe.wait_ge(s["bc_done"], n - 3)
                        nc.tensor.matmul(k.ps[1 + n % 4][:, :], k.c("head_bcast", H, h * P, (h + 1) * P), src[:, half * 512:(half + 1) * 512],
                                         start=True, stop=True).then_inc(s["bc_mm"], 1)
                        n += 1
            pe.wait_ge(s["kw_done"], PT)
            for h in range(H):
                if h == 0:
                    pe.wait_ge(s["sums_done"], 1)
                if h == 1:
                    pe.wait_ge(s["m_done"], 1)
                bank = k.ps[(0, 5)[h % 2]]
                if h >= 2:
                    pe.wait_ge(s["state_done"], h - 1)
                for j in range(PT):
                    mm = nc.tensor.matmul(bank[0:HD, 0:VW1], z[:, j, Z_MK + h * HD:Z_MK + (h + 1) * HD],
                                          z[:, j, Z_MV + h * VW1:Z_MV + (h + 1) * VW1], start=(j == 0), stop=(j == PT - 1))
                mm.then_inc(s["state_mm"], 1)

        @block.vector
        def _(dve):
            dve.wait_ge(s["sums_mm"], 1)
            nc.vector.tensor_copy(b["sums"][:, :, :], k.ps[0][:, 0:64].rearrange("p (t c) -> p t c", t=PT)).then_inc(s["sums_done"], 1)
            dve.wait_ge(s["sums_done"], 1)
            nc.vector.tensor_tensor(a["u"][:, :, :], sc[:, 0:PT, 0:4], b["sums"][:, :, 0:4], ALU.subtract).then_inc(s["u_done"], 1)
            nc.vector.tensor_scalar(b["neg_f"][:, :, :], b["sums"][:, :, 4:8], -1.0, None, ALU.mult).then_inc(s["f_done"], 1)
            nc.vector.memset(a["kc"][:, :], 0.0).then_inc(s["cmp_zero"], 1)
            nc.vector.memset(a["vc"][:, :], 0.0).then_inc(s["cmp_zero"], 1)
            dve.wait_ge(s["cmp_zero"], 2)
            dve.wait_ge(s["kc_mm"], 1)
            dve.wait_ge(s["vc_mm"], 1)
            for half in range(2):
                nc.vector.tensor_scalar(a["kc"][half * HD:(half + 1) * HD, 0:NCB], k.ps[6][0:HD, 0:NCB], SCALE, None, ALU.mult)
            for h in range(H):
                nc.vector.tensor_copy(a["vc"][32 * h:32 * h + NCB, h * HD:(h + 1) * HD], k.ps[7][0:NCB, 0:HD])
            dve.wait_ge(s["rows_mm"], 2)
            for n, dst in enumerate((b["u_rows"], b["f_rows"])):
                for half in range(2):
                    nc.vector.tensor_copy(dst[:, half * 512:(half + 1) * 512], k.ps[1 + 2 * n + half][0:H, :]).then_inc(s["rows_done"], 1)
            dve.wait_ge(s["rows_done"], 2)
            nc.vector.tensor_tensor_scan(b["cm_rows"][:, :], b["u_rows"][:, :], b["u_rows"][:, :], 0.0, ALU.max, ALU.max).then_inc(s["cm_done"], 1)
            dve.wait_ge(s["cmt_mm"], 1)
            nc.vector.tensor_tensor(b["m_tok"][:, :, :], k.ps[5][:, 0:32].rearrange("p (t c) -> p t c", t=PT), b["sums"][:, :, 0:4], ALU.add).then_inc(s["m_done"], 1)
            dve.wait_ge(s["bc_done"], 8)
            nc.vector.tensor_tensor(b["w_state"][:, :, :], a["u"][:, :, :],
                                    a["cm"][:, :, SEQ - 1].unsqueeze(1).to_broadcast([P, PT, H]), ALU.add).then_inc(s["ws_arg"], 1)
            dve.wait_ge(s["ws_exp"], 1)
            nc.vector.tensor_scalar(b["w_state"][:, :, :], b["w_state"][:, :, :], SCALE, None, ALU.mult).then_inc(s["ws_done"], 1)
            dve.wait_ge(s["ws_done"], 1)
            for j in range(PT):
                kk = z[:, j, Z_MK:Z_MK + BW].rearrange("p (h d) -> p h d", h=H)
                nc.vector.tensor_tensor(kk, kk, b["w_state"][:, j, :].unsqueeze(2).to_broadcast([P, H, HD]), ALU.mult).then_inc(s["kw_done"], 1)
            for h in range(H):
                dve.wait_ge(s["state_mm"], h + 1)
                nc.vector.tensor_copy(b["state"][:, h, :], k.ps[(0, 5)[h % 2]][0:HD, 0:VW1]).then_inc(s["state_done"], 1)

        @block.scalar
        def _(act):
            n = 0
            for sign, dst in ((-1.0, a["cm"]), (1.0, a["fneg"])):
                for h in range(H):
                    for half in range(2):
                        act.wait_ge(s["bc_mm"], n + 1)
                        nc.scalar.mul(dst[:, h, half * 512:(half + 1) * 512], k.ps[1 + n % 4][:, :], sign).then_inc(s["bc_done"], 1)
                        n += 1
                        if n == 8:
                            act.wait_ge(s["ws_arg"], 1)
                            nc.scalar.activation(b["w_state"][:, :, :], b["w_state"][:, :, :], ACT.Exp).then_inc(s["ws_exp"], 1)
            act.wait_ge(s["m_done"], 1)
            nc.scalar.activation(a["exp_neg_m"][:, :, :], b["m_tok"][:, :, :], ACT.Exp, scale=-1.0)


def prompt_attention(k, z, tb, a):
    nc, io = k.nc, k.io
    TURN_AT, VALUES_AT = 2, 3
    SB, PB, RS = 3, 3, 8
    st, b, s = phase(k, "attn", dict(
        scores=[P, SB, SEQ], probs_t=[P, PB, SEQ], alibi=[P, H, SEQ], neg_max=[P, SB], row_max=[P, SB], row_sum=[P, RS], gate=[P, 2],
        br=[P, 2, 3 * BW], br_t=[P, 6, P], cmp_s=[P, H, 32], cmp_t=[P, P], cmp_max=[P, H], cmp_sum=[P, H],
        ml_stats=[P, H, 6], ml_mv=[P, H, 2], ml_ve=[P, H], ml_rstd=[P, H], norm_w=[P, BW]),
        ["alibi_loaded", "scores_mm", "biased", "max_negated", "exped", "masked", "weighted", "turned", "turn_copied", "pv_mm",
         "den_neg", "sum_floor", "sum_inv", "gated", "out_done", "cmp_even", "cmp_mm", "cmp_biased", "cmp_max_done", "cmp_floor", "cmp_shift", "cmp_exp",
         "cmp_sum_done", "cmp_sum_floor", "cmp_inv", "cmp_gate", "cmp_p", "cmp_turned", "cmp_copied", "cmp_pv", "cmp_out",
         "ml_stat", "ml_agg", "ml_ve_done", "ml_rs", "ml_normed", "tile_done", "br_turned", "br_copied", "br_stored"])
    KINDS = ["fox", "ml", "sel", "win"]
    units = [(kind, h, i) for i in range(PT) for kind in KINDS for h in range(H)]
    PER_TILE = len(KINDS) * H
    N = len(units)

    def nblk(u):
        kind, h, i = units[u]
        return min(i + 1, WIN // P + 1) if kind == "win" else i + 1

    def first(u):
        return units[u][2] + 1 - nblk(u)

    halves = []
    for u in range(N):
        if units[u][0] != "ml":
            halves += [(u, x, min(4, nblk(u) - x)) for x in range(0, nblk(u), 4)]
    upto_half = lambda u: sum(1 for x in halves if x[0] <= u)
    ml_upto = lambda u: sum(1 for x in units[:u + 1] if x[0] == "ml")
    sm_upto = lambda u: u + 1 - ml_upto(u)
    hrow = lambda h: (h % 2) * HD

    ring, ring_at = [], {}

    def use(key, sem, value):
        ring_at[key] = len(ring)
        ring.append((sem, value))

    for v in range(N + VALUES_AT):
        if TURN_AT <= v:
            for q, x in enumerate(halves):
                if x[0] == v - TURN_AT:
                    use(("half", q), "turn_copied", q + 1)
        i, x = v // PER_TILE, v % PER_TILE
        if i < PT:
            if x == 0:
                use(("cmp_s", i), "cmp_biased", i + 1)
            if x == 5:
                use(("cmp_t", i), "cmp_copied", i + 1)
            if x == 8:
                use(("cmp_v", i), "cmp_out", i + 1)
            if i >= 1 and x in (6, 8):
                use(("br", 2 * (i - 1) + (x - 6) // 2), "br_copied", 2 * (i - 1) + (x - 6) // 2 + 1)
    for r in range(2):
        use(("br", 2 * (PT - 1) + r), "br_copied", 2 * (PT - 1) + r + 1)

    def bank_of(key):
        return k.ps[4 + ring_at[key] % 2]

    def bank_free(pe, key):
        n = ring_at[key]
        if n >= 2:
            pe.wait_ge(s[ring[n - 2][0]], ring[n - 2][1])
        return k.ps[4 + n % 2]

    with st, nc.Block() as block:
        @block.sync
        def _(sp):
            sp.dma_start(b["alibi"][:, :, :], io["alibi"]).then_inc(s["alibi_loaded"], 16)
            sp.dma_start(b["norm_w"][:, :], io["mlstm_norm_w"][0].partition_broadcast(P)).then_inc(s["alibi_loaded"], 16)
            for i in range(PT):
                sp.wait_ge(s["br_copied"], 2 * (i + 1))
                sp.dma_start(k.br_dram.rearrange("p (c t) -> p c t", c=6)[:, :, i * P:(i + 1) * P], b["br_t"][:, :, :]).then_inc(s["br_stored"], 16)
            sp.wait_ge(s["br_stored"], 16 * PT)

        @block.tensor
        def _(pe):
            def scores(u):
                kind, h, i = units[u]
                if u >= 2:
                    pe.wait_ge(s["biased"], u - 1)
                    if units[u - 2][0] == "ml":
                        pe.wait_ge(s["weighted"], ml_upto(u - 2))
                bank = k.ps[2 * (u % 2):2 * (u % 2) + 2]
                hr, nb, f = hrow(h), nblk(u), first(u)
                if kind == "ml":
                    q = tb["mq"][hr:hr + HD, h // 2, i * P:(i + 1) * P]
                    for x in range(nb):
                        mm = nc.tensor.matmul(bank[x // 4][:, x % 4 * P:x % 4 * P + P], tb["mk"][hr:hr + HD, h // 2, x * P:(x + 1) * P], q, start=True, stop=True)
                else:
                    q = tb["fq" if kind == "fox" else "nq"][hr:hr + HD, h // 2, i * P:(i + 1) * P]
                    key = tb["fk"][hr:hr + HD, h // 2] if kind == "fox" else tb["k" + kind][hr:hr + HD]
                    masks = {nb - 1: "mask_future"} if kind == "fox" else {0: "mask_window"} if kind == "win" and nb > WIN // P else {}
                    x = 0
                    while x < nb:
                        e = x + 1
                        while x not in masks and e < nb and e not in masks and e % 4:
                            e += 1
                        out = bank[x // 4][:, x % 4 * P:(x % 4 + e - x) * P]
                        mm = nc.tensor.matmul(out, q, key[:, (f + x) * P:(f + e) * P], start=True, stop=x not in masks)
                        if x in masks:
                            mm = nc.tensor.matmul(out, k.c("ident"), k.c(masks[x]), start=False, stop=True)
                        x = e
                mm.then_inc(s["scores_mm"], 1)

            def turn(u):
                if units[u][0] == "ml":
                    return
                pe.wait_ge(s["exped"], u + 1)
                for q, (uu, x, w) in enumerate(halves):
                    if uu != u:
                        continue
                    bank = bank_free(pe, ("half", q))
                    for y in range(w):
                        mm = nc.tensor.transpose(bank[:, y * P:(y + 1) * P], b["scores"][:, u % SB, (x + y) * P:(x + y + 1) * P], k.c("ident"))
                    mm.then_inc(s["turned"], 1)

            def values(u):
                kind, h, i = units[u]
                if kind == "ml":
                    pe.wait_ge(s["weighted"], ml_upto(u))
                else:
                    pe.wait_ge(s["turn_copied"], upto_half(u))
                if u >= 2:
                    pe.wait_ge(s["out_done"], u - 1)
                c0 = {"ml": Z_MV + h * VW1, "fox": Z_FV + h // 2 * P, "sel": Z_VS, "win": Z_VW}[kind]
                w = P
                for x in range(nblk(u)):
                    mm = nc.tensor.matmul(k.ps[6 + u % 2][:, 0:w], b["probs_t"][:, u % PB, x * P:(x + 1) * P], z[:, first(u) + x, c0:c0 + w],
                                          start=(x == 0), stop=(x == nblk(u) - 1))
                mm.then_inc(s["pv_mm"], 1)

            def cmp_scores(i):
                bank = bank_free(pe, ("cmp_s", i))
                for h in (0, 2, 1, 3):
                    hr = hrow(h)
                    if h == 1:
                        mm.then_inc(s["cmp_even"], 1)
                        pe.wait_ge(s["cmp_even"], i + 1)
                    mm = nc.tensor.matmul(bank[:, 32 * h:32 * h + 32], tb["nq"][hr:hr + HD, h // 2, i * P:(i + 1) * P], a["kc"][hr:hr + HD, :], start=True, stop=True)
                mm.then_inc(s["cmp_mm"], 1)

            def cmp_turn(i):
                pe.wait_ge(s["cmp_p"], i + 1)
                nc.tensor.transpose(bank_free(pe, ("cmp_t", i))[:, 0:P], b["cmp_s"][:, :, :].rearrange("p h j -> p (h j)"), k.c("ident")).then_inc(s["cmp_turned"], 1)

            def cmp_values(i):
                pe.wait_ge(s["cmp_copied"], i + 1)
                nc.tensor.matmul(bank_free(pe, ("cmp_v", i))[:, 0:BW], b["cmp_t"][:, :], a["vc"][:, :], start=True, stop=True).then_inc(s["cmp_pv"], 1)

            def branch_turn(i, r):
                if r == 0:
                    pe.wait_ge(s["tile_done"], i + 1)
                bank = bank_free(pe, ("br", 2 * i + r))
                for x in range(4 if r == 0 else 2):
                    mm = nc.tensor.transpose(bank[:, x * P:(x + 1) * P], b["br"][:, i % 2, (4 * r + x) * P:(4 * r + x + 1) * P], k.c("ident"))
                mm.then_inc(s["br_turned"], 1)

            for v in range(N + VALUES_AT):
                if v < N:
                    scores(v)
                if TURN_AT <= v < N + TURN_AT:
                    turn(v - TURN_AT)
                if v >= VALUES_AT:
                    values(v - VALUES_AT)
                i, x = v // PER_TILE, v % PER_TILE
                if i < PT:
                    if x == 0:
                        cmp_scores(i)
                    if x == 5:
                        cmp_turn(i)
                    if x == 8:
                        cmp_values(i)
                if i >= 1 and x in (6, 8) and i < PT:
                    branch_turn(i - 1, (x - 6) // 2)
            for r in range(2):
                branch_turn(PT - 1, r)

        @block.vector
        def _(dve):
            def bias(u):
                kind, h, i = units[u]
                w, f = nblk(u) * P, first(u)
                dve.wait_ge(s["scores_mm"], u + 1)
                if u >= SB:
                    if units[u - SB][0] == "ml":
                        dve.wait_ge(s["weighted"], ml_upto(u - SB))
                    else:
                        dve.wait_ge(s["turned"], upto_half(u - SB))
                dst = b["scores"][:, u % SB, 0:w]
                if kind == "ml":
                    nc.vector.tensor_tensor(dst.rearrange("p (j q) -> p j q", q=P), a["cm"][:, h, i * P:(i + 1) * P].unsqueeze(1).to_broadcast([P, nblk(u), P]),
                                            a["u"][:, 0:nblk(u), h:h + 1].to_broadcast([P, nblk(u), P]), ALU.add).then_inc(s["masked"], 1)
                    dve.wait_ge(s["masked"], ml_upto(u))
                    last = b["scores"][:, u % SB, w - P:w]
                    nc.vector.tensor_tensor(last, last, k.c("mask_future_t"), ALU.add).then_inc(s["biased"], 1)
                    return
                mx = b["row_max"][:, u % SB:u % SB + 1]
                if kind == "fox":
                    add = a["fneg"][:, h, 0:w]
                else:
                    add = b["alibi"][:, h, SEQ - w:SEQ]
                src = k.psum[:, 2 * (u % 2):2 * (u % 2) + 2, :].rearrange("p b c -> p (b c)")[:, 0:w]
                nc.vector.tensor_tensor_reduce(dst, src, add, 1.0, -3e38, ALU.add, ALU.max, mx).then_inc(s["biased"], 1)
                dve.wait_ge(s["biased"], u + 1)
                nc.vector.tensor_scalar(b["neg_max"][:, u % SB:u % SB + 1], mx, -1.0, None, ALU.mult).then_inc(s["max_negated"], 1)

            def weight(u):
                if units[u][0] != "ml":
                    return
                w = nblk(u) * P
                dve.wait_ge(s["exped"], u + 1)
                if u >= PB:
                    dve.wait_ge(s["pv_mm"], u - PB + 1)
                src = k.psum[:, 2 * (u % 2):2 * (u % 2) + 2, :].rearrange("p b c -> p (b c)")[:, 0:w]
                nc.vector.tensor_tensor(b["probs_t"][:, u % PB, 0:w], src, b["scores"][:, u % SB, 0:w], ALU.mult).then_inc(s["weighted"], 1)

            def output(u):
                kind, h, i = units[u]
                sl = slice(u % RS, u % RS + 1)
                if kind == "ml":
                    dve.wait_ge(s["pv_mm"], u + 1)
                    den = k.ps[6 + u % 2][:, HD:VW1]
                    nc.vector.tensor_scalar(b["row_sum"][:, sl], den, -1.0, None, ALU.mult).then_inc(s["den_neg"], 1)
                    dve.wait_ge(s["den_neg"], ml_upto(u))
                    nc.vector.scalar_tensor_tensor(b["row_sum"][:, sl], den, a["exp_neg_m"][:, i, h:h + 1], b["row_sum"][:, sl], ALU.max, ALU.max).then_inc(s["sum_floor"], 1)
                else:
                    dve.wait_ge(s["exped"], u + 1)
                    nc.vector.tensor_scalar(b["row_sum"][:, sl], b["row_sum"][:, sl], TINY, None, ALU.max).then_inc(s["sum_floor"], 1)
                dve.wait_ge(s["sum_floor"], u + 1)
                nc.vector.reciprocal(b["row_sum"][:, sl], b["row_sum"][:, sl]).then_inc(s["sum_inv"], 1)
                dve.wait_ge(s["sum_inv"], u + 1)
                dve.wait_ge(s["pv_mm"], u + 1)
                v0 = h % 2 * HD if kind == "fox" else 0
                pv = k.ps[6 + u % 2][:, v0:v0 + HD]
                r = b["row_sum"][:, sl]
                if kind == "ml":
                    nc.vector.scalar_tensor_tensor(b["br"][:, i % 2, BW + h * HD:BW + (h + 1) * HD], pv, r, z[:, i, Z_MO + h * HD:Z_MO + (h + 1) * HD], ALU.mult, ALU.mult).then_inc(s["out_done"], 1)
                elif kind == "fox":
                    if h == 0 and i >= 2:
                        dve.wait_ge(s["br_turned"], 2 * (i - 1))
                    nc.vector.tensor_scalar(b["br"][:, i % 2, 2 * BW + h * HD:2 * BW + (h + 1) * HD], pv, r, None, ALU.mult).then_inc(s["out_done"], 1)
                else:
                    g = Z_NG + 3 * h + (1 if kind == "sel" else 2)
                    nc.vector.tensor_tensor(b["gate"][:, u % 2:u % 2 + 1], r, z[:, i, g:g + 1], ALU.mult).then_inc(s["gated"], 1)
                    dve.wait_ge(s["gated"], sum(1 for x in units[:u + 1] if x[0] in ("sel", "win")))
                    dst = b["br"][:, i % 2, h * HD:(h + 1) * HD]
                    dve.wait_ge(s["cmp_out"], i + 1)
                    if kind == "win":
                        dve.wait_ge(s["out_done"], u - H + 1)
                    nc.vector.scalar_tensor_tensor(dst, pv, b["gate"][:, u % 2:u % 2 + 1], dst, ALU.mult, ALU.add).then_inc(s["out_done"], 1)

            def cmp_weights(i, step):
                cs = b["cmp_s"]
                bc = lambda t: t[:, :].unsqueeze(2).to_broadcast([P, H, 32])
                if step == 0:
                    dve.wait_ge(s["cmp_mm"], i + 1)
                    if i >= 1:
                        dve.wait_ge(s["cmp_turned"], i)
                    nc.vector.tensor_tensor(cs[:, :, :], bank_of(("cmp_s", i))[:, 0:P].rearrange("p (h j) -> p h j", h=H),
                                            k.c("cmp_bias", P, i * P, (i + 1) * P).rearrange("p (h j) -> p h j", h=H), ALU.add).then_inc(s["cmp_biased"], 1)
                    dve.wait_ge(s["cmp_biased"], i + 1)
                    nc.vector.tensor_reduce(b["cmp_max"][:, :], cs[:, :, :], AX.X, ALU.max).then_inc(s["cmp_max_done"], 1)
                    dve.wait_ge(s["cmp_max_done"], i + 1)
                    nc.vector.tensor_scalar(b["cmp_max"][:, :], b["cmp_max"][:, :], FLOOR, None, ALU.max).then_inc(s["cmp_floor"], 1)
                    dve.wait_ge(s["cmp_floor"], i + 1)
                    nc.vector.tensor_tensor(cs[:, :, :], cs[:, :, :], bc(b["cmp_max"]), ALU.subtract).then_inc(s["cmp_shift"], 1)
                else:
                    dve.wait_ge(s["cmp_exp"], i + 1)
                    nc.vector.tensor_reduce(b["cmp_sum"][:, :], cs[:, :, :], AX.X, ALU.add).then_inc(s["cmp_sum_done"], 1)
                    dve.wait_ge(s["cmp_sum_done"], i + 1)
                    nc.vector.tensor_scalar(b["cmp_sum"][:, :], b["cmp_sum"][:, :], TINY, None, ALU.max).then_inc(s["cmp_sum_floor"], 1)
                    dve.wait_ge(s["cmp_sum_floor"], i + 1)
                    nc.vector.reciprocal(b["cmp_sum"][:, :], b["cmp_sum"][:, :]).then_inc(s["cmp_inv"], 1)
                    dve.wait_ge(s["cmp_inv"], i + 1)
                    nc.vector.tensor_tensor(b["cmp_sum"][:, :], b["cmp_sum"][:, :], z[:, i, Z_NG:Z_NG + 3 * H:3], ALU.mult).then_inc(s["cmp_gate"], 1)
                    dve.wait_ge(s["cmp_gate"], i + 1)
                    nc.vector.tensor_tensor(cs[:, :, :], cs[:, :, :], bc(b["cmp_sum"]), ALU.mult).then_inc(s["cmp_p"], 1)

            def cmp_output(i):
                dve.wait_ge(s["cmp_pv"], i + 1)
                if i >= 2:
                    dve.wait_ge(s["br_turned"], 2 * (i - 1))
                nc.vector.tensor_copy(b["br"][:, i % 2, 0:BW], bank_of(("cmp_v", i))[:, 0:BW]).then_inc(s["cmp_out"], 1)

            def mlstm_norm(i):
                dve.wait_ge(s["out_done"], i * PER_TILE + 2 * H)
                y = b["br"][:, i % 2, BW:2 * BW].rearrange("p (h d) -> p h d", h=H)
                for h in range(H):
                    nc.vector.bn_stats(b["ml_stats"][:, h, :], y[:, h, :]).then_inc(s["ml_stat"], 1)
                dve.wait_ge(s["ml_stat"], H * (i + 1))
                for h in range(H):
                    nc.vector.bn_aggr(b["ml_mv"][:, h, :], b["ml_stats"][:, h, :]).then_inc(s["ml_agg"], 1)
                dve.wait_ge(s["ml_agg"], H * (i + 1))
                nc.vector.tensor_scalar(b["ml_ve"][:, :], b["ml_mv"][:, :, 1], EPS, None, ALU.add).then_inc(s["ml_ve_done"], 1)
                dve.wait_ge(s["ml_rs"], i + 1)
                for h in range(H):
                    nc.vector.tensor_scalar(y[:, h, :], y[:, h, :], b["ml_mv"][:, h, 0:1], b["ml_rstd"][:, h:h + 1], ALU.subtract, ALU.mult).then_inc(s["ml_normed"], 1)
                dve.wait_ge(s["ml_normed"], H * (i + 1))
                yy = b["br"][:, i % 2, BW:2 * BW]
                nc.vector.tensor_tensor(yy, yy, b["norm_w"][:, :], ALU.mult).then_inc(s["tile_done"], 1)

            dve.wait_ge(s["alibi_loaded"], 32)
            for v in range(N + VALUES_AT):
                i, x = v // PER_TILE, v % PER_TILE
                if i < PT:
                    if x == 1:
                        cmp_weights(i, 0)
                    if x == 3:
                        cmp_weights(i, 1)
                    if x == 9:
                        cmp_output(i)
                if v < N:
                    bias(v)
                if 1 <= v <= N:
                    weight(v - 1)
                if v >= VALUES_AT:
                    output(v - VALUES_AT)
                    if (v - VALUES_AT) % PER_TILE == PER_TILE - 1:
                        mlstm_norm((v - VALUES_AT) // PER_TILE)

        @block.gpsimd
        def _(pool):
            for i in range(PT):
                pool.wait_ge(s["ml_ve_done"], i + 1)
                nc.gpsimd.tensor_tensor(b["ml_rstd"][:, :], b["ml_ve"][:, :], k.c("minus_half", P, 0, H), ALU.pow).then_inc(s["ml_rs"], 1)

        @block.scalar
        def _(act):
            def exponent(u):
                w = nblk(u) * P
                row = b["scores"][:, u % SB, 0:w]
                if units[u][0] == "ml":
                    act.wait_ge(s["biased"], u + 1)
                    nc.scalar.activation(row, row, ACT.Exp).then_inc(s["exped"], 1)
                else:
                    act.wait_ge(s["max_negated"], sm_upto(u))
                    if u >= RS:
                        act.wait_ge(s["out_done"], u - RS + 1)
                    nc.scalar.activation(row, row, ACT.Exp, bias=b["neg_max"][:, u % SB:u % SB + 1], accum_out=b["row_sum"][:, u % RS:u % RS + 1]).then_inc(s["exped"], 1)

            def copy_turned(u):
                if u >= PB:
                    act.wait_ge(s["pv_mm"], u - PB + 1)
                for q, (uu, x, w) in enumerate(halves):
                    if uu == u:
                        act.wait_ge(s["turned"], q + 1)
                        nc.scalar.copy(b["probs_t"][:, u % PB, x * P:(x + w) * P], bank_of(("half", q))[:, 0:w * P]).then_inc(s["turn_copied"], 1)

            def branch_copy(i, r):
                act.wait_ge(s["br_turned"], 2 * i + r + 1)
                if i >= 1 and r == 0:
                    act.wait_ge(s["br_stored"], 16 * i)
                w = 4 if r == 0 else 2
                nc.scalar.copy(b["br_t"][:, 4 * r:4 * r + w, :], bank_of(("br", 2 * i + r))[:, 0:w * P].rearrange("p (c t) -> p c t", c=w)).then_inc(s["br_copied"], 1)

            for v in range(N + VALUES_AT):
                i, x = v // PER_TILE, v % PER_TILE
                if i < PT and x == 6:
                    act.wait_ge(s["cmp_turned"], i + 1)
                    if i >= 1:
                        act.wait_ge(s["cmp_pv"], i)
                    nc.scalar.copy(b["cmp_t"][:, :], bank_of(("cmp_t", i))[:, 0:P]).then_inc(s["cmp_copied"], 1)
                if 1 <= i < PT and x in (7, 9):
                    branch_copy(i - 1, (x - 7) // 2)
                if TURN_AT <= v < N + TURN_AT and units[v - TURN_AT][0] != "ml":
                    copy_turned(v - TURN_AT)
                if v < N:
                    exponent(v)
                if i < PT and x == 1:
                    act.wait_ge(s["cmp_shift"], i + 1)
                    nc.scalar.activation(b["cmp_s"][:, :, :], b["cmp_s"][:, :, :], ACT.Exp).then_inc(s["cmp_exp"], 1)
            for r in range(2):
                branch_copy(PT - 1, r)


def decode_mixers(k, zd, td, a):
    nc, io = k.nc, k.io
    G, NP = 2, DB * NPG
    W = PAST + ND
    st, b, s = phase(k, "dec", dict(
        page_table=[1, NP], dec_table=[P, TABLE_W - SPLIT], pages=[P, NP, 4 * HD], fox_pages=[P, NP, 2 * BW], logf_pages=[P, NP, H], win_pages=[P, NP, 2 * HD],
        kcv_t=[P, NP * P], ksel_t=[HD, NP * P], kwin_t=[HD, NP * P], fk_t=[P, 2, NP * P], w_cmp=[P, BLK, HD],
        q_n=[HD, DB, H, DT], q_f=[P, 2, DB, H, DT], q_m=[P, 2, DB, H, DT],
        logf_rows=[P, NP, H, DT], x_fox=[ND, DB, H, DT], x_ml=[ND, DB, H, DT], x_in=[ND, DB, H, DT],
        kc_d=[HD, DB * DCB], vc_d=[DB * DCB, HD], probs=[P, 2, W], probs_t=[P, 3, P],
        row=[P, 16], gates=[P, 3 * H], gate3=[P, 3], gate_tmp=[P, 3 * H], ml_d=[P, ND], ml_w=[P, ND], ml_wt=[ND, P],
        mem=[P, 2, DB, VW1], mem_new=[P, 2, DB, VW1], m_bh=[DB, H], m_hb=[H, DB],
        norm_wd=[P, BW], norm_row=[P, HD], num=[P, VW1], o_row=[P, HD], stat=[P, 6], mv=[P, 2], res=[P, 3, HD], br_d=[P, 6, ND],
        tok_g=[ND, H], g_rows=[H, ND], lf_rows=[H, ND], bl=[H, DB], gmax=[H, DB], m_new=[H, DB], decay=[H, DB], ws_rows=[H, ND],
        ws_tok=[ND, H], k_w=[ND, BW], v_own=[ND, 2, H * VW1], decay_col=[P, 2, DB]),
        ["dtab_loaded", "ptab_loaded", "pages_loaded", "fox_loaded", "logf_loaded", "win_loaded", "wcd_loaded", "mem_loaded", "nwd_loaded",
         "d_turned", "d_act_copied", "d_dve_copied", "zeroed", "q_ready", "x_ready", "kcd_mm", "kcd_done", "d_scores", "d_negmax",
         "d_exp", "d_ptrn", "d_pcopied", "d_pv", "d_ml_mm", 
         "am_row", "ml_exp", "ml_weighted", "ml_wturned", "ml_wcopied", "ml_pv", "acc",
         "drs_ve", "drs", "res_done", "res_turned", "res_copied", "nw_acc", "o_mm",
         "st_mm", "st_dve", "st_act", "st_up", "v_own_done", "mem_done", "dec_stored"])
    tj = [(kind, p0) for kind in ("kcv", "ksel", "fk0", "fk1", "kwin") for p0 in range(0, NP, 4)]
    turn_sem = lambda n: ("d_act_copied" if n % 2 == 0 else "d_dve_copied", n // 2 + 1)

    def turned_place(kind, p0):
        c = slice(p0 * P, (p0 + 4) * P)
        return {"kcv": b["kcv_t"][:, c], "ksel": b["ksel_t"][:, c], "kwin": b["kwin_t"][:, c], "fk0": b["fk_t"][:, 0, c], "fk1": b["fk_t"][:, 1, c]}[kind]

    KINDS = ["cmp", "sel", "win", "fox"]
    NK = len(KINDS)
    s_at = {"cmp": k.ps[3][:, 160:192], "sel": k.ps[0][:, 0:W], "win": k.ps[1][:, 0:W], "fox": k.ps[2][:, 0:W]}
    v_at = {"cmp": (384, 448), "sel": (0, 64), "win": (64, 128), "fox": (128, 384)}
    bias_of = {"cmp": "dec_cmp_bias", "sel": "dec_bias", "win": "dec_bias", "fox": "dec_fox_bias"}
    rowc = lambda x, n=1: b["row"][:, x:x + n]
    R_MAX, R_NEG, R_SUM, R_A, R_MT, R_NM, R_AM, R_INT, R_ENM, R_DEN, R_RSTD, R_MLMAX, R_VE = 0, 1, 2, 4, 5, 6, 7, 8, 9, 10, 11, 12, 13
    hm = lambda h: k.c("head_of_row", P, h, h + 1)
    group = lambda t, g: t[:, 4 * g:4 * g + 4].rearrange("p b h t -> p (b h t)")

    with st, nc.Block() as block:
        k.dec_const = b["dec_table"]

        @block.sync
        def _(sp):
            sp.dma_start(b["page_table"][:, :], io["page_table"].rearrange("b (o p) -> o (b p)", o=1)).then_inc(s["ptab_loaded"], 16)
            sp.dma_start(b["dec_table"][:, :], io["table"][:, SPLIT:TABLE_W]).then_inc(s["dtab_loaded"], 16)
            sp.dma_start(b["w_cmp"][0:HD], io["nsa_w_ck"][0].rearrange("p d e -> d p e")).then_inc(s["wcd_loaded"], 16)
            sp.dma_start(b["w_cmp"][HD:P], io["nsa_w_cv"][0].rearrange("p d e -> d p e")).then_inc(s["wcd_loaded"], 16)
            sp.wait_ge(s["ptab_loaded"], 16)
            for n in range(NP):
                page = sp.value_load(b["page_table"][0:1, n:n + 1], min_val=0, max_val=io["cache_nsa"].shape[1] - 1)
                sp.dma_start(b["pages"][:, n, :], io["cache_nsa"][0, bass.ds(page, 1)].rearrange("o p r d -> (o p) (r d)")).then_inc(s["pages_loaded"], 16)
                sp.dma_start(b["fox_pages"][:, n, :], io["cache_fox_kv"][0, bass.ds(page, 1)].rearrange("o p r h d -> (o p) (r h d)")).then_inc(s["fox_loaded"], 16)
                sp.dma_start(b["logf_pages"][:, n, :], io["cache_fox_logf"][0, bass.ds(page, 1)].rearrange("o p h -> (o p) h")).then_inc(s["logf_loaded"], 16)
            sp.dma_start(b["win_pages"][:, :, :], io["cache_nsa_win"].rearrange("x b (n p) r d -> p (x b n) (r d)", p=P)).then_inc(s["win_loaded"], 16)
            with nc.allow_non_contiguous_dma(reason="small states"):
                for kt in range(2):
                    for hh in range(2):
                        h = 2 * kt + hh
                        sp.dma_start(b["mem"][hh * HD:(hh + 1) * HD, kt, :, 0:HD], io["state_mlstm_c"][0, :, h].rearrange("b d e -> d b e")).then_inc(s["mem_loaded"], 16)
                        sp.dma_start(b["mem"][hh * HD:(hh + 1) * HD, kt, :, HD], io["state_mlstm_n"][0, :, h].rearrange("b d -> d b")).then_inc(s["mem_loaded"], 16)
                sp.dma_start(b["m_bh"][:, :], io["state_mlstm_m"][0]).then_inc(s["mem_loaded"], 16)
                sp.dma_start(b["m_hb"][:, :], io["state_mlstm_m"][0].rearrange("b h -> h b")).then_inc(s["mem_loaded"], 16)
                sp.dma_start(b["norm_wd"][:, :], io["mlstm_norm_w"][0].partition_broadcast(P)).then_inc(s["nwd_loaded"], 16)
                sp.wait_ge(s["res_copied"], G)
                sp.dma_start(k.br_dram.rearrange("p (c t) -> p c t", c=6)[:, :, SEQ:T], b["br_d"][:, :, :]).then_inc(s["dec_stored"], 16)
                sp.wait_ge(s["mem_done"], 2 * 2 * DB)
                for kt in range(2):
                    for hh in range(2):
                        h = 2 * kt + hh
                        sp.dma_start(io["s_mlstm_c"][0, :, h].rearrange("b d e -> d b e"), b["mem_new"][hh * HD:(hh + 1) * HD, kt, :, 0:HD]).then_inc(s["dec_stored"], 16)
                        sp.dma_start(io["s_mlstm_n"][0, :, h].rearrange("b d -> d b"), b["mem_new"][hh * HD:(hh + 1) * HD, kt, :, HD]).then_inc(s["dec_stored"], 16)
                sp.dma_start(io["s_mlstm_m"][0].rearrange("b h -> h b"), b["m_new"][:, :]).then_inc(s["dec_stored"], 16)
            sp.wait_ge(s["dec_stored"], 16 * 10)

        @block.tensor
        def _(pe):
            for n, (kind, p0) in enumerate(tj):
                if n == 0:
                    pe.wait_ge(s["pages_loaded"], 16 * NP)
                if n == 8:
                    pe.wait_ge(s["fox_loaded"], 16 * NP)
                if n == 16:
                    pe.wait_ge(s["win_loaded"], 16)
                if n >= 8:
                    pe.wait_ge(s[turn_sem(n - 8)[0]], turn_sem(n - 8)[1])
                for x in range(4):
                    pg = p0 + x
                    src = {"kcv": b["pages"][:, pg, 0:P], "ksel": b["pages"][:, pg, P:2 * P], "kwin": b["win_pages"][:, pg, :],
                           "fk0": b["fox_pages"][:, pg, 0:P], "fk1": b["fox_pages"][:, pg, P:2 * P]}[kind]
                    mm = nc.tensor.transpose(k.ps[n % 8][:, x * P:(x + 1) * P], src, k.c("ident"))
                mm.then_inc(s["d_turned"], 1)
            pe.wait_ge(s["d_act_copied"], len(tj) // 2)
            pe.wait_ge(s["d_dve_copied"], len(tj) // 2)
            pe.wait_ge(s["wcd_loaded"], 32)
            for p in range(BLK):
                nc.tensor.matmul(k.ps[6][0:HD, 0:DB * DCB], b["w_cmp"][0:HD, p, :], b["kcv_t"][0:HD, p:NP * P:BLK], start=(p == 0), stop=(p == BLK - 1))
            for p in range(BLK):
                mm = nc.tensor.matmul(k.ps[7][0:DB * DCB, 0:HD], b["kcv_t"][HD:P, p:NP * P:BLK], b["w_cmp"][HD:P, p, :], start=(p == 0), stop=(p == BLK - 1))
            mm.then_inc(s["kcd_mm"], 1)
            pe.wait_ge(s["kcd_done"], 2)
            pe.wait_ge(s["q_ready"], 3 * H)
            pe.wait_ge(s["x_ready"], 4)
            pe.wait_ge(s["mem_loaded"], 16 * 10)
            past = lambda bb, n=0: slice(bb * PAST + n * P, bb * PAST + (n + 1) * P)
            for g in range(G):
                if g:
                    pe.wait_ge(s["res_copied"], g)
                nc.tensor.matmul(s_at["cmp"], group(b["q_n"], g), b["kc_d"][:, :], start=True, stop=True).then_inc(s["d_scores"], 1)
                for kind, key in (("sel", "ksel"), ("win", "kwin")):
                    for x in range(4):
                        bb = 4 * g + x
                        nc.tensor.matmul(s_at[kind][32 * x:32 * x + 32, 0:PAST], b["q_n"][:, bb].rearrange("p h t -> p (h t)"),
                                         b[key + "_t"][:, bb * PAST:(bb + 1) * PAST], start=True, stop=True, tile_position=(0, 32 * x))
                    nc.tensor.matmul(s_at[kind][:, PAST:W], group(b["q_n"], g), td[key][0:HD, :], start=True, stop=True).then_inc(s["d_scores"], 1)
                for x in range(4):
                    bb = 4 * g + x
                    q = [b["q_f"][:, kt, bb].rearrange("p h t -> p (h t)") for kt in range(2)]
                    lf = [b["logf_rows"][:, bb * NPG + n].rearrange("p h t -> p (h t)") for n in range(NPG)]
                    new = b["x_fox"][:, bb].rearrange("p h t -> p (h t)")
                    for n in range(NPG):
                        out = s_at["fox"][32 * x:32 * x + 32, n * P:(n + 1) * P]
                        terms = [(q[0], b["fk_t"][:, 0, past(bb, n)]), (q[1], b["fk_t"][:, 1, past(bb, n)]), (lf[n], k.c("after"))]
                        terms += [(lf[m], k.c("ones")) for m in range(n + 1, NPG)] + [(new, k.c("ones", ND))]
                        for y, (lhs, rhs) in enumerate(terms):
                            nc.tensor.matmul(out, lhs, rhs, start=(y == 0), stop=(y == len(terms) - 1), tile_position=(0, 32 * x))
                terms = [(group(b["q_f"][:, kt], g), td["fk"][:, kt, :]) for kt in range(2)] + [(group(b["x_fox"], g), k.c("dec_after", ND))]
                for y, (lhs, rhs) in enumerate(terms):
                    mm = nc.tensor.matmul(s_at["fox"][:, PAST:W], lhs, rhs, start=(y == 0), stop=(y == 2))
                mm.then_inc(s["d_scores"], 1)
                for y, (lhs, rhs) in enumerate([(group(b["x_ml"], g), k.c("dec_after", ND)), (group(b["x_in"], g), k.c("ident", ND, 0, ND))]):
                    nc.tensor.matmul(k.ps[3][:, 0:ND], lhs, rhs, start=(y == 0), stop=(y == 1))
                for kt in range(2):
                    nc.tensor.matmul(k.ps[3][:, ND:2 * ND], group(b["q_m"][:, kt], g), td["mk"][:, kt, :], start=(kt == 0), stop=(kt == 1))
                nc.tensor.matmul(k.ps[3][:, 128:129], group(b["x_ml"], g), k.c("ones", ND, 0, 1), start=True, stop=True)
                nc.tensor.matmul(k.ps[3][:, 132:136], k.c("batch_to_row", DB, g * P, (g + 1) * P), b["m_bh"][:, :], start=True, stop=True)
                nc.tensor.matmul(k.ps[3][:, 136:148], k.c("row_of_token", ND, g * P, (g + 1) * P), zd[0:ND, 0, Z_NG:Z_NG + 12], start=True, stop=True).then_inc(s["d_ml_mm"], 1)
                nc.tensor.matmul(k.ps[4][:, 0:BW], k.c("row_of_token", ND, g * P, (g + 1) * P), zd[0:ND, 0, Z_MO:Z_MO + BW], start=True, stop=True).then_inc(s["o_mm"], 1)
                for n, kind in enumerate(KINDS):
                    m = g * NK + n
                    pe.wait_ge(s["d_exp"], m + 1)
                    if m >= 1:
                        pe.wait_ge(s["d_pcopied"], m)
                    if kind == "cmp":
                        mm = nc.tensor.transpose(k.ps[5][0:32, 0:P], b["probs"][:, m % 2, 0:32], k.c("ident"))
                    else:
                        for x in range(3):
                            w = min(P, W - x * P)
                            mm = nc.tensor.transpose(k.ps[5][0:w, x * P:(x + 1) * P], b["probs"][:, m % 2, x * P:x * P + w], k.c("ident"))
                    mm.then_inc(s["d_ptrn"], 1)
                    pe.wait_ge(s["d_pcopied"], m + 1)
                    c0, c1 = v_at[kind]
                    if kind == "cmp":
                        mm = nc.tensor.matmul(k.ps[6][:, c0:c1], b["probs_t"][0:32, 0, :], b["vc_d"][:, :], start=True, stop=True)
                    for x in range(4 if kind != "cmp" else 0):
                        bb = 4 * g + x
                        for y in range(3):
                            if y < 2:
                                lhs = b["probs_t"][:, y, 32 * x:32 * x + 32]
                                rhs = {"sel": b["pages"][:, bb * NPG + y, 3 * HD:4 * HD], "win": b["win_pages"][:, bb * NPG + y, HD:2 * HD],
                                       "fox": b["fox_pages"][:, bb * NPG + y, BW:2 * BW]}[kind]
                            else:
                                lhs = b["probs_t"][0:ND, 2, 32 * x:32 * x + 32]
                                cz, wz = {"sel": (Z_VS, HD), "win": (Z_VW, HD), "fox": (Z_FV, BW)}[kind]
                                rhs = zd[0:ND, 0, cz:cz + wz]
                            mm = nc.tensor.matmul(k.ps[6][32 * x:32 * x + 32, c0:c1], lhs, rhs, start=(y == 0), stop=(y == 2), tile_position=(0, 32 * x))
                    mm.then_inc(s["d_pv"], 1)
                for x in range(4):
                    bb = 4 * g + x
                    for kt in range(2):
                        nc.tensor.matmul(k.ps[7][32 * x:32 * x + 32, 264:264 + VW1], b["q_m"][:, kt, bb].rearrange("p h t -> p (h t)"), b["mem"][:, kt, bb, :],
                                         start=(kt == 0), stop=(kt == 1), tile_position=(0, 32 * x))
                pe.wait_ge(s["ml_weighted"], g + 1)
                nc.tensor.transpose(k.ps[5][0:ND, 3 * P:4 * P], b["ml_w"][:, :], k.c("ident")).then_inc(s["ml_wturned"], 1)
                pe.wait_ge(s["ml_wcopied"], g + 1)
                nc.tensor.matmul(k.ps[7][:, 0:H * VW1], b["ml_wt"][:, :], zd[0:ND, 0, Z_MV:Z_MV + H * VW1], start=True, stop=True).then_inc(s["ml_pv"], 1)
                pe.wait_ge(s["res_done"], 3 * (g + 1))
                for x in range(3):
                    mm = nc.tensor.transpose(k.ps[1][0:HD, x * P:(x + 1) * P], b["res"][:, x, :], k.c("ident"))
                mm.then_inc(s["res_turned"], 1)
            pe.wait_ge(s["res_copied"], G)
            nc.tensor.matmul(k.ps[0][0:ND, 0:H], k.c("dec_after", ND), a["sc"][0:ND, PT, 4:8], start=True, stop=True)
            nc.tensor.transpose(k.ps[0][0:H, 64:64 + ND], a["sc"][0:ND, PT, 4:8], k.c("ident", ND, 0, ND)).then_inc(s["st_mm"], 1)
            pe.wait_ge(s["st_dve"], 2)
            nc.tensor.transpose(k.ps[0][0:H, 128:128 + ND], b["tok_g"][:, :], k.c("ident", ND, 0, ND)).then_inc(s["st_mm"], 1)
            pe.wait_ge(s["st_act"], 2)
            nc.tensor.transpose(k.ps[0][0:ND, 192:192 + H], b["ws_rows"][:, :], k.c("ident", H, 0, H))
            for kt in range(2):
                mm = nc.tensor.matmul(k.ps[0][:, 256 + 8 * kt:264 + 8 * kt], k.c("head_rows", H, kt * P, (kt + 1) * P), b["decay"][:, :], start=True, stop=True)
            mm.then_inc(s["st_mm"], 1)
            n = 0
            for bb in range(DB):
                pe.wait_ge(s["v_own_done"], bb + 1)
                for kt in range(2):
                    if n >= 4:
                        pe.wait_ge(s["mem_done"], 2 * (n - 3))
                    nc.tensor.matmul(k.ps[1 + n % 4][:, 0:2 * VW1], b["k_w"][:, kt * P:(kt + 1) * P], b["v_own"][:, bb % 2, kt * 2 * VW1:(kt + 1) * 2 * VW1],
                                     start=True, stop=True).then_inc(s["st_up"], 1)
                    n += 1

        def copy_turned(eng, copy, scaled, par):
            for n, (kind, p0) in enumerate(tj):
                if n % 2 != par:
                    continue
                eng.wait_ge(s["d_turned"], n + 1)
                r = HD if kind in ("ksel", "kwin") else P
                dst, src = turned_place(kind, p0)[0:r], k.ps[n % 8][0:r, :]
                (copy(dst, src) if kind == "kcv" else scaled(dst, src)).then_inc(s[turn_sem(n)[0]], 1)

        @block.scalar
        def _(act):
            copy_turned(act, nc.scalar.copy, lambda d, x: nc.scalar.mul(d, x, SCALE), 0)
            for g in range(G):
                for n, kind in enumerate(KINDS):
                    m = g * NK + n
                    w = DB * DCB if kind == "cmp" else W
                    act.wait_ge(s["d_negmax"], m + 1)
                    row = b["probs"][:, m % 2, 0:w]
                    nc.scalar.activation(row, row, ACT.Exp, bias=b["row"][:, R_NEG:R_NEG + 1], accum_out=b["row"][:, R_SUM:R_SUM + 1]).then_inc(s["d_exp"], 1)
                    act.wait_ge(s["d_ptrn"], m + 1)
                    if m >= 1:
                        act.wait_ge(s["d_pv"], m)
                    if kind == "cmp":
                        nc.scalar.copy(b["probs_t"][0:32, 0, :], k.ps[5][0:32, 0:P]).then_inc(s["d_pcopied"], 1)
                    else:
                        nc.scalar.copy(b["probs_t"][:, 0:2, :], k.ps[5][:, 0:2 * P].rearrange("p (x r) -> p x r", x=2))
                        nc.scalar.copy(b["probs_t"][0:ND, 2, :], k.ps[5][0:ND, 2 * P:3 * P]).then_inc(s["d_pcopied"], 1)
                act.wait_ge(s["am_row"], g + 1)
                nc.scalar.activation(b["ml_d"][:, :], b["ml_d"][:, :], ACT.Exp, bias=rowc(R_NM))
                nc.scalar.activation(rowc(R_INT), rowc(R_AM), ACT.Exp)
                nc.scalar.activation(rowc(R_ENM), rowc(R_NM), ACT.Exp).then_inc(s["ml_exp"], 1)
                act.wait_ge(s["ml_wturned"], g + 1)
                nc.scalar.copy(b["ml_wt"][:, :], k.ps[5][0:ND, 3 * P:4 * P]).then_inc(s["ml_wcopied"], 1)
                act.wait_ge(s["res_turned"], g + 1)
                for x in range(3):
                    for h in range(H):
                        src = k.ps[1][0:HD, x * P:(x + 1) * P].rearrange("p (b h t) -> p b h t", b=4, h=H)[:, :, h, :]
                        dst = b["br_d"][(h % 2) * HD:(h % 2 + 1) * HD, 2 * x + h // 2, g * 32:(g + 1) * 32].rearrange("p (b t) -> p b t", b=4)
                        ins = nc.scalar.copy(dst, src)
                ins.then_inc(s["res_copied"], 1)
            act.wait_ge(s["st_dve"], 6)
            nc.scalar.activation(b["decay"][:, :], b["decay"][:, :], ACT.Exp).then_inc(s["st_act"], 1)
            nc.scalar.activation(b["ws_rows"][:, :], b["ws_rows"][:, :], ACT.Exp).then_inc(s["st_act"], 1)

        @block.gpsimd
        def _(pool):
            for g in range(G):
                pool.wait_ge(s["drs_ve"], g + 1)
                nc.gpsimd.tensor_tensor(rowc(R_RSTD), rowc(R_VE), k.c("minus_half", P, 0, 1), ALU.pow).then_inc(s["drs"], 1)

        @block.vector
        def _(dve):
            nc.vector.memset(b["q_f"][:, :, :, :, :], 0.0).then_inc(s["zeroed"], 1)
            nc.vector.memset(b["q_m"][:, :, :, :, :], 0.0).then_inc(s["zeroed"], 1)
            dve.wait_ge(s["zeroed"], 2)
            for h in range(H):
                hr, kt = (h % 2) * HD, h // 2
                part = lambda n: td[n][hr:hr + HD, kt, :].rearrange("p (b t) -> p b t", b=DB)
                nc.vector.tensor_copy(b["q_n"][:, :, h, :], part("nq")).then_inc(s["q_ready"], 1)
                nc.vector.tensor_copy(b["q_f"][hr:hr + HD, kt, :, h, :], part("fq")).then_inc(s["q_ready"], 1)
                nc.vector.tensor_copy(b["q_m"][hr:hr + HD, kt, :, h, :], part("mq")).then_inc(s["q_ready"], 1)
            dve.wait_ge(s["dtab_loaded"], 16)
            rows4 = lambda name: k.c(name, ND).rearrange("p (b h t) -> p b h t", b=DB, h=H)
            for dst, name, c in (("x_fox", "upto_row", 8), ("x_ml", "upto_row", 4), ("x_in", "batch_of_row", 0)):
                nc.vector.tensor_tensor(b[dst][:, :, :, :], rows4(name), a["sc"][0:ND, PT, c:c + H].unsqueeze(1).unsqueeze(3).to_broadcast([ND, DB, H, DT]), ALU.mult).then_inc(s["x_ready"], 1)
            dve.wait_ge(s["logf_loaded"], 16 * NP)
            nc.vector.tensor_copy(b["logf_rows"][:, :, :, :], b["logf_pages"][:, :, :].unsqueeze(3).to_broadcast([P, NP, H, DT])).then_inc(s["x_ready"], 1)
            dve.wait_ge(s["nwd_loaded"], 16)
            nacc = 0
            for h in range(H):
                src = b["norm_wd"][:, h * HD:(h + 1) * HD]
                if h == 0:
                    nc.vector.tensor_scalar(b["norm_row"][:, :], src, hm(0), None, ALU.mult).then_inc(s["nw_acc"], 1)
                else:
                    dve.wait_ge(s["nw_acc"], h)
                    nc.vector.scalar_tensor_tensor(b["norm_row"][:, :], src, hm(h), b["norm_row"][:, :], ALU.mult, ALU.add).then_inc(s["nw_acc"], 1)
            copy_turned(dve, nc.vector.tensor_copy, lambda d, x: nc.vector.tensor_scalar(d, x, SCALE, None, ALU.mult), 1)
            dve.wait_ge(s["kcd_mm"], 1)
            nc.vector.tensor_scalar(b["kc_d"][:, :], k.ps[6][0:HD, 0:DB * DCB], SCALE, None, ALU.mult).then_inc(s["kcd_done"], 1)
            nc.vector.tensor_copy(b["vc_d"][:, :], k.ps[7][0:DB * DCB, 0:HD]).then_inc(s["kcd_done"], 1)
            acc = [0]

            def chain(ins):
                acc[0] += 1
                ins.then_inc(s["acc"], 1)
                dve.wait_ge(s["acc"], acc[0])

            for g in range(G):
                dve.wait_ge(s["d_ml_mm"], g + 1)
                chain(nc.vector.tensor_copy(b["gates"][:, :], k.ps[3][:, 136:148]))
                for h in range(H):
                    src = b["gates"][:, 3 * h:3 * h + 3]
                    if h == 0:
                        chain(nc.vector.tensor_scalar(b["gate3"][:, :], src, hm(0), None, ALU.mult))
                    else:
                        chain(nc.vector.scalar_tensor_tensor(b["gate3"][:, :], src, hm(h), b["gate3"][:, :], ALU.mult, ALU.add))
                for n, kind in enumerate(KINDS):
                    m = g * NK + n
                    w = DB * DCB if kind == "cmp" else W
                    dve.wait_ge(s["d_scores"], m + 1)
                    if m >= 2:
                        dve.wait_ge(s["d_ptrn"], m - 1)
                    bias = k.c(bias_of[kind], P, g * w, (g + 1) * w)
                    chain(nc.vector.tensor_tensor_reduce(b["probs"][:, m % 2, 0:w], s_at[kind], bias, 1.0, -3e38, ALU.add, ALU.max, rowc(R_MAX)))
                    nc.vector.tensor_scalar(rowc(R_NEG), rowc(R_MAX), -1.0, None, ALU.mult).then_inc(s["d_negmax"], 1)
                    dve.wait_ge(s["d_exp"], m + 1)
                    chain(nc.vector.tensor_scalar(rowc(R_DEN), rowc(R_SUM), TINY, None, ALU.max))
                    chain(nc.vector.reciprocal(rowc(R_DEN), rowc(R_DEN)))
                    if kind != "fox":
                        chain(nc.vector.tensor_tensor(rowc(R_DEN), rowc(R_DEN), b["gate3"][:, n:n + 1], ALU.mult))
                    dve.wait_ge(s["d_pv"], m + 1)
                    c0, c1 = v_at[kind]
                    pv = k.ps[6][:, c0:c1]
                    if kind == "cmp":
                        chain(nc.vector.tensor_scalar(b["res"][:, 0, :], pv, rowc(R_DEN), None, ALU.mult))
                    elif kind != "fox":
                        ins = nc.vector.scalar_tensor_tensor(b["res"][:, 0, :], pv, rowc(R_DEN), b["res"][:, 0, :], ALU.mult, ALU.add)
                        if kind == "sel":
                            chain(ins)
                        else:
                            ins.then_inc(s["res_done"], 1)
                    else:
                        chain(nc.vector.tensor_scalar(b["res"][:, 2, :], pv[:, 0:HD], hm(0), None, ALU.mult))
                        for h in range(1, H):
                            chain(nc.vector.scalar_tensor_tensor(b["res"][:, 2, :], pv[:, h * HD:(h + 1) * HD], hm(h), b["res"][:, 2, :], ALU.mult, ALU.add))
                        nc.vector.tensor_scalar(b["res"][:, 2, :], b["res"][:, 2, :], rowc(R_DEN), None, ALU.mult).then_inc(s["res_done"], 1)
                chain(nc.vector.tensor_tensor_reduce(b["ml_d"][:, :], k.ps[3][:, 0:ND], k.c("dec_mask", P, g * ND, (g + 1) * ND), 1.0, -3e38, ALU.add, ALU.max, rowc(R_MLMAX)))
                chain(nc.vector.tensor_tensor_reduce(b["gates"][:, 0:H], k.ps[3][:, 132:136], k.c("head_of_row"), 1.0, 0.0, ALU.mult, ALU.add, rowc(R_A)))
                chain(nc.vector.tensor_tensor(rowc(R_A), rowc(R_A), k.ps[3][:, 128:129], ALU.add))
                chain(nc.vector.tensor_tensor(rowc(R_MT), rowc(R_A), rowc(R_MLMAX), ALU.max))
                chain(nc.vector.tensor_scalar(rowc(R_NM), rowc(R_MT), -1.0, None, ALU.mult))
                nc.vector.tensor_tensor(rowc(R_AM), rowc(R_A), rowc(R_MT), ALU.subtract).then_inc(s["am_row"], 1)
                dve.wait_ge(s["ml_exp"], g + 1)
                nc.vector.tensor_tensor(b["ml_w"][:, :], k.ps[3][:, ND:2 * ND], b["ml_d"][:, :], ALU.mult).then_inc(s["ml_weighted"], 1)
                dve.wait_ge(s["o_mm"], g + 1)
                for h in range(H):
                    src = k.ps[4][:, h * HD:(h + 1) * HD]
                    chain(nc.vector.tensor_scalar(b["o_row"][:, :], src, hm(0), None, ALU.mult) if h == 0 else
                          nc.vector.scalar_tensor_tensor(b["o_row"][:, :], src, hm(h), b["o_row"][:, :], ALU.mult, ALU.add))
                dve.wait_ge(s["ml_pv"], g + 1)
                chain(nc.vector.tensor_scalar(b["num"][:, :], k.ps[7][:, 264:264 + VW1], rowc(R_INT), None, ALU.mult))
                for h in range(H):
                    chain(nc.vector.scalar_tensor_tensor(b["num"][:, :], k.ps[7][:, h * VW1:(h + 1) * VW1], hm(h), b["num"][:, :], ALU.mult, ALU.add))
                chain(nc.vector.tensor_scalar(rowc(R_DEN), b["num"][:, HD:VW1], -1.0, None, ALU.mult))
                chain(nc.vector.scalar_tensor_tensor(rowc(R_DEN), b["num"][:, HD:VW1], rowc(R_ENM), rowc(R_DEN), ALU.max, ALU.max))
                chain(nc.vector.reciprocal(rowc(R_DEN), rowc(R_DEN)))
                y = b["res"][:, 1, :]
                chain(nc.vector.scalar_tensor_tensor(y, b["num"][:, 0:HD], rowc(R_DEN), b["o_row"][:, :], ALU.mult, ALU.mult))
                chain(nc.vector.bn_stats(b["stat"][:, :], y))
                chain(nc.vector.bn_aggr(b["mv"][:, :], b["stat"][:, :]))
                nc.vector.tensor_scalar(rowc(R_VE), b["mv"][:, 1:2], EPS, None, ALU.add).then_inc(s["drs_ve"], 1)
                dve.wait_ge(s["drs"], g + 1)
                chain(nc.vector.tensor_scalar(y, y, b["mv"][:, 0:1], rowc(R_RSTD), ALU.subtract, ALU.mult))
                nc.vector.tensor_tensor(y, y, b["norm_row"][:, :], ALU.mult).then_inc(s["res_done"], 1)
                if g + 1 < G:
                    dve.wait_ge(s["res_turned"], g + 1)
            dve.wait_ge(s["st_mm"], 1)
            nc.vector.tensor_tensor(b["tok_g"][:, :], k.ps[0][0:ND, 0:H], a["sc"][0:ND, PT, 0:4], ALU.add).then_inc(s["st_dve"], 1)
            nc.vector.tensor_reduce(b["bl"][:, :], k.ps[0][0:H, 64:64 + ND].rearrange("p (b t) -> p b t", b=DB), AX.X, ALU.add).then_inc(s["st_dve"], 1)
            dve.wait_ge(s["st_dve"], 2)
            chain(nc.vector.tensor_tensor(b["bl"][:, :], b["bl"][:, :], b["m_hb"][:, :], ALU.add))
            dve.wait_ge(s["st_mm"], 2)
            grow = k.ps[0][0:H, 128:128 + ND].rearrange("p (b t) -> p b t", b=DB)
            nc.vector.tensor_reduce(b["gmax"][:, :], grow, AX.X, ALU.max).then_inc(s["st_dve"], 1)
            dve.wait_ge(s["st_dve"], 3)
            nc.vector.tensor_tensor(b["m_new"][:, :], b["bl"][:, :], b["gmax"][:, :], ALU.max).then_inc(s["st_dve"], 1)
            dve.wait_ge(s["st_dve"], 4)
            nc.vector.tensor_tensor(b["decay"][:, :], b["bl"][:, :], b["m_new"][:, :], ALU.subtract).then_inc(s["st_dve"], 1)
            nc.vector.tensor_tensor(b["ws_rows"][:, :].rearrange("p (b t) -> p b t", b=DB), grow, b["m_new"][:, :].unsqueeze(2).to_broadcast([H, DB, DT]), ALU.subtract).then_inc(s["st_dve"], 1)
            dve.wait_ge(s["st_mm"], 3)
            chain(nc.vector.tensor_scalar(b["ws_tok"][:, :], k.ps[0][0:ND, 192:192 + H], SCALE, None, ALU.mult))
            chain(nc.vector.tensor_copy(b["decay_col"][:, :, :], k.ps[0][:, 256:272].rearrange("p (k b) -> p k b", k=2)))
            chain(nc.vector.tensor_tensor(b["k_w"][:, :].rearrange("p (h d) -> p h d", h=H), zd[0:ND, 0, Z_MK:Z_MK + BW].rearrange("p (h d) -> p h d", h=H),
                                          b["ws_tok"][:, :].unsqueeze(2).to_broadcast([ND, H, HD]), ALU.mult))
            for bb in range(DB + 1):
                if bb < DB:
                    if bb >= 2:
                        dve.wait_ge(s["st_up"], 2 * (bb - 1))
                    nc.vector.tensor_scalar(b["v_own"][:, bb % 2, :], zd[0:ND, 0, Z_MV:Z_MV + H * VW1], k.c("batch_of_token", ND, bb, bb + 1), None, ALU.mult).then_inc(s["v_own_done"], 1)
                if bb >= 1:
                    for kt in range(2):
                        n = 2 * (bb - 1) + kt
                        dve.wait_ge(s["st_up"], n + 1)
                        for half in range(2):
                            r = slice(half * HD, (half + 1) * HD)
                            nc.vector.scalar_tensor_tensor(b["mem_new"][r, kt, bb - 1, :], b["mem"][r, kt, bb - 1, :], b["decay_col"][r, kt, bb - 1:bb],
                                                           k.ps[1 + n % 4][r, half * VW1:(half + 1) * VW1], ALU.mult, ALU.add).then_inc(s["mem_done"], 1)


def merge_branches(k, y):
    nc, io = k.nc, k.io
    UNITS = 3 * len(NCH)
    RING = 3
    st, b, s = phase(k, "merge", dict(xt2=[P, KD, T], br_all=[P, 6, T], gate_w=[P, 2, KD, 3, P], branch_w=[P, 2, 3, 2, P], bias_g=[P, 3, KD], bias_now=[P, 2, 3],
                              sig=[P, RING, 512]),
                     ["xt2_loaded", "br_loaded", "bg_loaded", "bias_copied", "gp_mm", "sig_done", "gp_read", "bank_free"] + [f"mw_loaded{i}" for i in range(2)])
    with st, nc.Block() as block:
        @block.sync
        def _(sp):
            def load(dt, slot):
                for m in range(3):
                    sp.dma_start(b["gate_w"][:, slot, :, m, :], io["w_in"][0].rearrange("(k p) n -> p k n", p=P)[:, :, bass.ds(dt * P + (C_GM + m * D), P)]).then_inc(s[f"mw_loaded{slot}"], 16)
                    sp.dma_start(b["branch_w"][:, slot, m], io["w_branch"][0, m].rearrange("(k p) n -> p k n", p=P)[:, :, bass.ds(dt * P, P)]).then_inc(s[f"mw_loaded{slot}"], 16)
            load(0, 0)
            for kk in range(KD):
                sp.dma_start(b["xt2"][:, kk, :], k.xt_dram[:, kk * T:(kk + 1) * T]).then_inc(s["xt2_loaded"], 16)
            sp.dma_start(b["br_all"][:, :, :].rearrange("p c t -> p (c t)"), k.br_dram).then_inc(s["br_loaded"], 16)
            with nc.allow_non_contiguous_dma(reason="bias columns"):
                sp.dma_start(b["bias_g"][:, :, :], io["b_in"][0, C_GM:NIN].rearrange("(m k p) -> p m k", m=3, p=P)).then_inc(s["bg_loaded"], 16)
            load(1, 1)
            with sp.Fori(0, KD // 2 - 1) as r:
                for x in range(2):
                    sp.wait_ge(s["gp_mm"], r * (2 * UNITS) + (x + 1) * UNITS)
                    load(r * 2 + (2 + x), x)

        @block.tensor
        def _(pe):
            pe.wait_ge(s["xt2_loaded"], 16 * KD)
            pe.wait_ge(s["br_loaded"], 16)
            with pe.Fori(0, KD // 2) as r:
                for x in range(2):
                    pe.wait_ge(s[f"mw_loaded{x}"], r * 96 + 96)
                    for m in range(3):
                        for n, (a0, w) in enumerate(NCH):
                            l = x * UNITS + m * 3 + n
                            pe.wait_ge(s["bank_free"], r * (2 * UNITS) + (l + 1))
                            for kk in range(KD):
                                nc.tensor.matmul(k.ps[l % RING][:, 0:w], b["gate_w"][:, x, kk, m, :], b["xt2"][:, kk, a0:a0 + w], start=(kk == 0), stop=(kk == KD - 1))
                            for kk in range(2):
                                mm = nc.tensor.matmul(k.ps[4 + l % RING][:, 0:w], b["branch_w"][:, x, m, kk, :], b["br_all"][:, 2 * m + kk, a0:a0 + w], start=(kk == 0), stop=(kk == 1))
                            mm.then_inc(s["gp_mm"], 1)

        @block.scalar
        def _(act):
            act.wait_ge(s["bg_loaded"], 16)
            with act.Fori(0, KD // 2) as r:
                for x in range(2):
                    nc.scalar.copy(b["bias_now"][:, x, :], b["bias_g"][:, :, bass.ds(r * 2 + x, 1)].rearrange("p m o -> p (m o)")).then_inc(s["bias_copied"], 1)
                    act.wait_ge(s["bias_copied"], r * 2 + (x + 1))
                    for m in range(3):
                        for n, (a0, w) in enumerate(NCH):
                            l = x * UNITS + m * 3 + n
                            act.wait_ge(s["gp_mm"], r * (2 * UNITS) + (l + 1))
                            act.wait_ge(s["bank_free"], r * (2 * UNITS) + (l + 1))
                            nc.scalar.activation(b["sig"][:, l % RING, 0:w], k.ps[l % RING][:, 0:w], ACT.Sigmoid,
                                                 bias=b["bias_now"][:, x, m:m + 1]).then_inc(s["sig_done"], 1)

        @block.vector
        def _(dve):
            nc.vector.memset(b["sig"][:, 0, 0:1], 0.0).then_inc(s["bank_free"], RING)
            with dve.Fori(0, KD // 2) as r:
                for x in range(2):
                    for m in range(3):
                        for n, (a0, w) in enumerate(NCH):
                            l = x * UNITS + m * 3 + n
                            dve.wait_ge(s["sig_done"], r * (2 * UNITS) + (l + 1))
                            sig, prod = b["sig"][:, l % RING, 0:w], k.ps[4 + l % RING][:, 0:w]
                            dst = y[:, bass.ds(r * 2 + x, 1), a0:a0 + w].rearrange("p o t -> p (o t)")
                            if m == 0:
                                nc.vector.tensor_tensor(dst, sig, prod, ALU.mult).then_inc(s["bank_free"], 1)
                            else:
                                nc.vector.tensor_tensor(sig, sig, prod, ALU.mult).then_inc(s["gp_read"], 1)
                                dve.wait_ge(s["gp_read"], r * (12) + (x * 6 + (m - 1) * 3 + n + 1))
                                nc.vector.tensor_tensor(dst, dst, sig, ALU.add).then_inc(s["bank_free"], 1)


def mix_out_norm(k, y, x1t, x1):
    nc, io = k.nc, k.io
    XB, TB = 4, 4
    st, b, s = phase(k, "mix", dict(w_o=[P, KD, D], x_res=[P, XB, D], lw=[P, D], lb=[P, D], lwc=[P, KD], lbc=[P, KD],
                              stats1=[P, 12], mv1=[P, NT, 2], ve1=[P, NT], rstd1=[P, NT]),
                     ["wo_loaded", "ln1_par", "mix_mm", "res_added", "st1", "mv1_done", "ve1_done", "rs1", "xh1", "x1_psum", "x1_done", "x1_mul", "x1_row_done", "x1_stored"]
                     + [f"xr_loaded{i}" for i in range(XB)])
    groups = [(0, 4), (4, 4), (8, 1)]
    with st, nc.Block() as block:
        @block.sync
        def _(sp):
            def load(t):
                sp.dma_start(b["x_res"][0:rows(t), t % XB, :], k.xn_dram[t * P:t * P + rows(t), :]).then_inc(s[f"xr_loaded{t % XB}"], 16)
            for kk in range(KD):
                sp.dma_start(b["w_o"][:, kk, :], io["w_out"][0, kk * P:(kk + 1) * P, :]).then_inc(s["wo_loaded"], 16)
            for t in range(XB):
                load(t)
            sp.dma_start(b["lw"][:, :], io["ln1_w"][0].partition_broadcast(P)).then_inc(s["ln1_par"], 16)
            sp.dma_start(b["lb"][:, :], io["ln1_b"][0].partition_broadcast(P)).then_inc(s["ln1_par"], 16)
            with nc.allow_non_contiguous_dma(reason="1024 values to columns"):
                sp.dma_start(b["lwc"][:, :], io["ln1_w"][0].rearrange("(k p) -> p k", p=P)).then_inc(s["ln1_par"], 16)
                sp.dma_start(b["lbc"][:, :], io["ln1_b"][0].rearrange("(k p) -> p k", p=P)).then_inc(s["ln1_par"], 16)
            for t in range(NT):
                sp.wait_ge(s["x1_row_done"], t + 1)
                sp.dma_start(k.x1_dram[t * P:t * P + rows(t), :], x1[0:rows(t), t, :]).then_inc(s["x1_stored"], 16)
                if t + XB >= NT:
                    continue
                sp.wait_ge(s["x1_psum"], KD * (t // 4 + 1))
                load(t + XB)
            sp.wait_ge(s["x1_stored"], 16 * NT)

        @block.tensor
        def _(pe):
            pe.wait_ge(s["wo_loaded"], 16 * KD)
            n = 0

            def turn_group(g):
                nonlocal n
                t0, cnt = groups[g]
                pe.wait_ge(s["xh1"], t0 + cnt)
                for kk in range(KD):
                    if n >= 4:
                        pe.wait_ge(s["x1_done"], n - 3)
                    for j in range(cnt):
                        r = rows(t0 + j)
                        mm = nc.tensor.transpose(k.ps[4 + n % 4][:, j * P:j * P + r], b["x_res"][0:r, (t0 + j) % XB, kk * P:(kk + 1) * P], k.c("ident", r, 0, r))
                    mm.then_inc(s["x1_psum"], 1)
                    n += 1

            for t in range(NT):
                r = rows(t)
                if t >= 2:
                    pe.wait_ge(s["res_added"], t - 1)
                for half in range(2):
                    for kk in range(KD):
                        mm = nc.tensor.matmul(k.ps[2 * (t % 2) + half][0:r, :], y[:, kk, t * P:t * P + r], b["w_o"][:, kk, half * 512:(half + 1) * 512],
                                              start=(kk == 0), stop=(kk == KD - 1))
                mm.then_inc(s["mix_mm"], 1)
                if t in (4, 8):
                    turn_group(t // 4 - 1)
            turn_group(2)

        @block.vector
        def _(dve):
            def statistics(t):
                r = rows(t)
                x = b["x_res"][0:r, t % XB, :]
                dve.wait_ge(s[f"xr_loaded{t % XB}"], 16 * (t // XB + 1))
                dve.wait_ge(s["mix_mm"], t + 1)
                mix = k.psum[0:r, 2 * (t % 2):2 * (t % 2) + 2, :].rearrange("p b c -> p (b c)")
                nc.vector.scalar_tensor_tensor(x, x, ALPHA, mix, ALU.mult, ALU.add).then_inc(s["res_added"], 1)
                dve.wait_ge(s["res_added"], t + 1)
                nc.vector.bn_stats(b["stats1"][0:r, 0:6], x[:, 0:512]).then_inc(s["st1"], 1)
                nc.vector.bn_stats(b["stats1"][0:r, 6:12], x[:, 512:1024]).then_inc(s["st1"], 1)
                dve.wait_ge(s["st1"], 2 * t + 2)
                nc.vector.bn_aggr(b["mv1"][0:r, t, :], b["stats1"][0:r, :]).then_inc(s["mv1_done"], 1)
                dve.wait_ge(s["mv1_done"], t + 1)
                nc.vector.tensor_scalar(b["ve1"][0:r, t:t + 1], b["mv1"][0:r, t, 1:2], EPS, None, ALU.add).then_inc(s["ve1_done"], 1)

            def normalise(t):
                r = rows(t)
                x = b["x_res"][0:r, t % XB, :]
                dve.wait_ge(s["rs1"], t + 1)
                nc.vector.tensor_scalar(x, x, b["mv1"][0:r, t, 0:1], b["rstd1"][0:r, t:t + 1], ALU.subtract, ALU.mult).then_inc(s["xh1"], 1)

            for t in range(NT):
                statistics(t)
                if t in (3, 7, 8):
                    if t != 8:
                        normalise(t - 1)
                        normalise(t)
                    else:
                        normalise(t)
                elif t % 4 != 0:
                    normalise(t - 1)

        @block.gpsimd
        def _(pool):
            pool.wait_ge(s["ln1_par"], 64)

            def root(t):
                r = rows(t)
                pool.wait_ge(s["ve1_done"], t + 1)
                nc.gpsimd.tensor_tensor(b["rstd1"][0:r, t:t + 1], b["ve1"][0:r, t:t + 1], k.c("minus_half", r, 0, 1), ALU.pow).then_inc(s["rs1"], 1)

            root(0)
            for t in range(NT):
                if t % 4 != 3 and t + 1 < NT:
                    root(t + 1)
                r = rows(t)
                pool.wait_ge(s["xh1"], t + 1)
                nc.gpsimd.tensor_tensor(x1[0:r, t, :], b["x_res"][0:r, t % XB, :], b["lw"][0:r, :], ALU.mult).then_inc(s["x1_mul"], 1)
                pool.wait_ge(s["x1_mul"], t + 1)
                nc.gpsimd.tensor_tensor(x1[0:r, t, :], x1[0:r, t, :], b["lb"][0:r, :], ALU.add).then_inc(s["x1_row_done"], 1)
                if t % 4 == 3:
                    root(t + 1)

        @block.scalar
        def _(act):
            act.wait_ge(s["ln1_par"], 64)
            n = 0
            for t0, cnt in groups:
                w = sum(rows(t0 + j) for j in range(cnt))
                for kk in range(KD):
                    act.wait_ge(s["x1_psum"], n + 1)
                    nc.scalar.activation(x1t[:, kk, t0 * P:t0 * P + w], k.ps[4 + n % 4][:, 0:w], ACT.Identity,
                                         bias=b["lbc"][:, kk:kk + 1], scale=b["lwc"][:, kk:kk + 1]).then_inc(s["x1_done"], 1)
                    n += 1


def route(k, x1t, weight, most):
    nc, io = k.nc, k.io
    NL = GROUPS + NE
    st, b, s = phase(k, "route", dict(w_r=[P, KD, NL], bias_r=[P, NL], logit=[P, NT, NL], top=[P, NT, 4], hot_g=[P, NT, GROUPS], hot1=[P, NT, PER], hot2=[P, NT, PER],
                              left=[P, NT, 1], le=[P, NT, PER], le2=[P, NT, PER], prod=[P, NT, GROUPS, PER], eg=[P, NT, GROUPS],
                              hit1=[P, NT, NE], hit2=[P, NT, NE], hits=[P, NT, NE], before=[P, NT + 1, NE], place=[P, NT, NE], slot_f=[P, 2, NT], most_f=[P, 1],
                              slot=[P, 2, NT], entry=[P, NT, 2, 2]),
                     ["r_loaded", "logit_mm", "r_chain", "r_exp", "r_args", "hits_done", "place_mm", "slots_done", "idx_cleared", "idx_stored"])
    with st, nc.Block() as block:
        @block.sync
        def _(sp):
            with nc.allow_non_contiguous_dma(reason="narrow router weights"):
                sp.dma_start(b["w_r"][:, :, 0:GROUPS], io["moe_w_group"][0].rearrange("(k p) n -> p k n", p=P)).then_inc(s["r_loaded"], 16)
                sp.dma_start(b["w_r"][:, :, GROUPS:NL], io["moe_w_expert"][0].rearrange("(k p) n -> p k n", p=P)).then_inc(s["r_loaded"], 16)
                sp.dma_start(b["bias_r"][:, 0:GROUPS], io["moe_b_group"][0].partition_broadcast(P)).then_inc(s["r_loaded"], 16)
                sp.dma_start(b["bias_r"][:, GROUPS:NL], io["moe_b_expert"][0].partition_broadcast(P)).then_inc(s["r_loaded"], 16)
            sp.dma_start(k.idx_dram, io["empty_slots"]).then_inc(s["idx_cleared"], 16)

        @block.gpsimd
        def _(pool):
            pool.wait_ge(s["idx_cleared"], 16)
            pool.wait_ge(s["slots_done"], 1)
            for t in range(NT):
                for i in range(2):
                    r = rows(t)
                    nc.gpsimd.indirect_dma_start(k.idx_dram, bass.IndirectOffsetOnAxis(ap=b["slot"][0:r, i, t:t + 1], axis=0), b["entry"][0:r, t, i, :], None).then_inc(s["idx_stored"], 16)
            pool.wait_ge(s["idx_stored"], 16 * 2 * NT)

        @block.tensor
        def _(pe):
            pe.wait_ge(s["r_loaded"], 64)
            for t in range(NT):
                r = rows(t)
                if t == 8:
                    pe.wait_ge(s["r_chain"], 3)
                for kk in range(KD):
                    mm = nc.tensor.matmul(k.ps[t % 8][0:r, 32 * (t // 8):32 * (t // 8) + NL], x1t[:, kk, t * P:t * P + r], b["w_r"][:, kk, :], start=(kk == 0), stop=(kk == KD - 1))
                mm.then_inc(s["logit_mm"], 1)
            pe.wait_ge(s["hits_done"], 1)
            flat = lambda a: a.rearrange("p t e -> p (t e)")
            nc.tensor.matmul(k.ps[1][:, 0:NT * NE], k.c("upto"), flat(b["hits"][:, :, :]), start=True, stop=False)
            nc.tensor.matmul(k.ps[1][:, 0:NT * NE], k.c("ones"), flat(b["before"][:, 0:NT, :]), start=False, stop=True).then_inc(s["place_mm"], 1)
            nc.tensor.matmul(k.ps[2][:, 0:NE], k.c("ones"), b["before"][:, NT, :], start=True, stop=True).then_inc(s["place_mm"], 1)

        @block.scalar
        def _(act):
            act.wait_ge(s["r_args"], 1)
            nc.scalar.activation(b["eg"][:, :, :], b["eg"][:, :, :], ACT.Exp)
            nc.scalar.activation(b["top"][:, :, 2], b["top"][:, :, 2], ACT.Exp).then_inc(s["r_exp"], 1)

        @block.vector
        def _(dve):
            count = [0]

            def chain(ins):
                count[0] += 1
                ins.then_inc(s["r_chain"], 1)
                dve.wait_ge(s["r_chain"], count[0])

            def first_max(hot, val, mx, n):
                chain(nc.vector.tensor_reduce(mx, val, AX.X, ALU.max))
                chain(nc.vector.tensor_tensor(hot, val, mx.unsqueeze(2).to_broadcast([P, NT, n]), ALU.is_equal))
                chain(nc.vector.memset(b["left"][:, :, :], 1.0))
                for j in range(n):
                    chain(nc.vector.tensor_tensor(hot[:, :, j:j + 1], hot[:, :, j:j + 1], b["left"][:, :, :], ALU.mult))
                    chain(nc.vector.tensor_tensor(b["left"][:, :, :], b["left"][:, :, :], hot[:, :, j:j + 1], ALU.subtract))

            chain(nc.vector.tensor_copy(b["entry"][:, :, :, :].rearrange("p t i c -> p (t i c)"), k.c("slot_entry")))
            chain(nc.vector.memset(b["logit"][:, :, :], 0.0))
            dve.wait_ge(s["r_loaded"], 64)
            for t in range(NT):
                r = rows(t)
                dve.wait_ge(s["logit_mm"], t + 1)
                chain(nc.vector.tensor_tensor(b["logit"][0:r, t, :], k.ps[t % 8][0:r, 32 * (t // 8):32 * (t // 8) + NL], b["bias_r"][0:r, :], ALU.add))
            top = b["top"]
            lg = b["logit"][:, :, 0:GROUPS]
            first_max(b["hot_g"][:, :, :], lg, top[:, :, 0], GROUPS)
            chain(nc.vector.memset(b["hot_g"][ND:P, PT, :], 0.0))
            chain(nc.vector.tensor_tensor(b["eg"][:, :, :], lg, top[:, :, 0:1].to_broadcast([P, NT, GROUPS]), ALU.subtract))
            for t in range(NT):
                chain(nc.vector.tensor_tensor(b["prod"][:, t], b["logit"][:, t, GROUPS:NL].rearrange("p (g j) -> p g j", g=GROUPS),
                                              b["hot_g"][:, t, :].unsqueeze(2).to_broadcast([P, GROUPS, PER]), ALU.mult))
            chain(nc.vector.tensor_reduce(b["le"][:, :, :], b["prod"][:, :, :, :].rearrange("p t g j -> p t j g"), AX.X, ALU.add))
            first_max(b["hot1"][:, :, :], b["le"][:, :, :], top[:, :, 1], PER)
            chain(nc.vector.scalar_tensor_tensor(b["le2"][:, :, :], b["hot1"][:, :, :], NEG, b["le"][:, :, :], ALU.mult, ALU.add))
            first_max(b["hot2"][:, :, :], b["le2"][:, :, :], top[:, :, 2], PER)
            nc.vector.tensor_tensor(top[:, :, 2], top[:, :, 2], top[:, :, 1], ALU.subtract).then_inc(s["r_args"], 1)
            for t in range(NT):
                for hit, hot in (("hit1", "hot1"), ("hit2", "hot2")):
                    last = nc.vector.tensor_tensor(b[hit][:, t, :].rearrange("p (g j) -> p g j", g=GROUPS), b["hot_g"][:, t, :].unsqueeze(2).to_broadcast([P, GROUPS, PER]),
                                                   b[hot][:, t, :].unsqueeze(1).to_broadcast([P, GROUPS, PER]), ALU.mult)
                    chain(last)
            chain(nc.vector.tensor_tensor(b["hits"][:, :, :], b["hit1"][:, :, :], b["hit2"][:, :, :], ALU.add))
            chain(nc.vector.memset(b["before"][:, 0, :], 0.0))
            for t in range(NT):
                last = nc.vector.tensor_tensor(b["before"][:, t + 1, :], b["before"][:, t, :], b["hits"][:, t, :], ALU.add)
                if t < NT - 1:
                    chain(last)
            last.then_inc(s["hits_done"], 1)
            dve.wait_ge(s["place_mm"], 2)
            place = b["place"]
            chain(nc.vector.tensor_tensor(place[:, :, :], k.ps[1][:, 0:NT * NE].rearrange("p (t e) -> p t e", t=NT), k.c("slot_base").unsqueeze(1).to_broadcast([P, NT, NE]), ALU.add))
            for i, hit in enumerate(("hit1", "hit2")):
                chain(nc.vector.tensor_tensor(b[hit][:, :, :], b[hit][:, :, :], place[:, :, :], ALU.mult))
                chain(nc.vector.tensor_reduce(b["slot_f"][:, i, :], b[hit][:, :, :], AX.X, ALU.add))
            chain(nc.vector.tensor_reduce(b["most_f"][:, :], k.ps[2][:, 0:NE], AX.X, ALU.max))
            chain(nc.vector.tensor_copy(most[:, :], b["most_f"][:, :]))
            nc.vector.tensor_copy(b["slot"][:, :, :], b["slot_f"][:, :, :]).then_inc(s["slots_done"], 1)
            dve.wait_ge(s["r_exp"], 1)
            chain(nc.vector.tensor_reduce(top[:, :, 0], b["eg"][:, :, :], AX.X, ALU.add))
            chain(nc.vector.tensor_scalar(top[:, :, 3], top[:, :, 2], 1.0, None, ALU.add))
            chain(nc.vector.tensor_tensor(top[:, :, 0], top[:, :, 0], top[:, :, 3], ALU.mult))
            chain(nc.vector.reciprocal(top[:, :, 0], top[:, :, 0]))
            chain(nc.vector.tensor_copy(weight[:, 0, :], top[:, :, 0]))
            chain(nc.vector.tensor_tensor(weight[:, 1, :], top[:, :, 0], top[:, :, 2], ALU.mult))


def experts(k, most):
    nc, io = k.nc, k.io
    TURN = 4
    st, b, s = phase(k, "moe", dict(wg=[P, 2, KD, FE], wu=[P, 2, KD, FE], wd=[P, 2, 2, D], idx_all=[P, 2, NE, 2], idx_from=[P, 2, 2], idx_to=[P, 2, 2], xg=[P, 2, 2, D], xgt=[P, 2, KD, CAP],
                                    sg=[P, 2, CAP], hid=[P, 2, CAP], y_out=[P, 2, 2, D]),
                     ["turned", "xt_copied", "up_mm", "sg_done", "silu_done", "hid_done", "down_mm", "y0_done", "y1_done",
                      "idx_zeroed", "idx_loaded", "idx_copied", "pool_at", "y_stored", "y_free"]
                     + [f"{n}{i}" for n in ("gathered", "wgu_loaded", "wd_loaded") for i in range(2)])
    LEAD = {"xt_copied": 2, "turned": 8, "up_mm": 4, "hid_done": 2, "down_mm": 4, "y0_done": 1, "y1_done": 1, "y_free": 2}
    parts = [(0, P), (P, CAP - P)]

    def after(name, count):
        return count + LEAD.get(name, 0)

    def all_rounds(eng, body):
        body(0)
        n = eng.value_load(most[0:1, 0:1], min_val=0, max_val=T)
        with eng.Fori(1, ROUNDS) as rnd:
            with eng.If(n > rnd * CAP):
                body(rnd)

    with st, nc.Block() as block:
        @block.sync
        def _(sp):
            for name, n in LEAD.items():
                sp.sem_inc(s[name], n)
            sp.wait_ge(s["idx_zeroed"], 1)

            def one_round(rnd):
                sp.wait_ge(s["y_free"], rnd * NE + after("y_free", 0))
                for j, (p0, n) in enumerate(parts):
                    sp.dma_start(b["idx_all"][0:n, j], k.idx_dram.rearrange("(e s) c -> s e c", e=NE)[bass.ds(rnd * CAP + p0, n)]).then_inc(s["idx_loaded"], 16)
                with sp.Fori(0, NE // 2) as i:
                    for x in range(2):
                        e, g = i * 2 + x, rnd * NE + i * 2 + x
                        sp.wait_ge(s["up_mm"], g * 2 + after("up_mm", -2))
                        for w, src in (("wg", "moe_w_gate"), ("wu", "moe_w_up")):
                            sp.dma_start(b[w][:, x], io[src][0, bass.ds(e, 1)].rearrange("o (k p) f -> p (o k) f", p=P)).then_inc(s[f"wgu_loaded{x}"], 16)
                        sp.wait_ge(s["down_mm"], g * 2 + after("down_mm", -2))
                        sp.dma_start(b["wd"][:, x], io["moe_w_down"][0, bass.ds(e, 1)].rearrange("o (c p) d -> p (o c) d", p=P)).then_inc(s[f"wd_loaded{x}"], 16)
            all_rounds(sp, one_round)

        @block.gpsimd
        def _(pool):
            nc.gpsimd.memset(b["idx_all"][:, :, :, :], 0).then_inc(s["idx_zeroed"], 1)

            def waited():
                pool.sem_inc(s["pool_at"], 1)

            def entries(buf, x, e, col, copies):
                nc.gpsimd.tensor_copy(b[buf][:, x, :], b["idx_all"][:, :, bass.ds(e, 1), col].rearrange("p j o -> p (j o)")).then_inc(s["idx_copied"], 1)
                pool.wait_ge(s["idx_copied"], copies)
                waited()

            def gather(rnd, e, x, copies):
                pool.wait_ge(s["turned"], (rnd * NE + e) * TURN + after("turned", -TURN))
                waited()
                entries("idx_from", x, e, 0, copies)
                for j, (p0, n) in enumerate(parts):
                    nc.gpsimd.indirect_dma_start(b["xg"][0:n, x, j, :], None, k.x1_dram, bass.IndirectOffsetOnAxis(ap=b["idx_from"][0:n, x, j:j + 1], axis=0)).then_inc(s[f"gathered{x}"], 16)

            def scatter(rnd, e, x, copies):
                entries("idx_to", x, e, 1, copies)
                for j, (p0, n) in enumerate(parts):
                    pool.wait_ge(s[f"y{j}_done"], rnd * NE + e + after("y0_done", 1))
                waited()
                for j, (p0, n) in enumerate(parts):
                    nc.gpsimd.indirect_dma_start(k.y_dram, bass.IndirectOffsetOnAxis(ap=b["idx_to"][0:n, x, j:j + 1], axis=0), b["y_out"][0:n, x, j, :], None).then_inc(s["y_stored"], 16)
                pool.wait_ge(s["y_stored"], (rnd * NE + e) * 32 + 32)
                pool.sem_inc(s["y_free"], 1)

            def one_round(rnd):
                C = rnd * (2 * NE)
                pool.wait_ge(s["idx_loaded"], rnd * 32 + 32)
                waited()
                gather(rnd, 0, 0, C + 1)
                gather(rnd, 1, 1, C + 2)
                with pool.Fori(0, NE // 2 - 1) as i:
                    for x in range(2):
                        gather(rnd, i * 2 + (x + 2), x, C + i * 4 + (2 * x + 3))
                        scatter(rnd, i * 2 + x, x, C + i * 4 + (2 * x + 4))
                for x in range(2):
                    scatter(rnd, NE - 2 + x, x, C + (2 * NE - 1 + x))
            all_rounds(pool, one_round)

        @block.tensor
        def _(pe):
            def turn(rnd, g, h, x):
                pe.wait_ge(s[f"gathered{x}"], h * 32 + 32)
                for q in range(TURN):
                    pe.wait_ge(s["xt_copied"], g * TURN + after("xt_copied", q - 1))
                    for kk in (2 * q, 2 * q + 1):
                        for j, (p0, n) in enumerate(parts):
                            c0 = (kk % 2) * CAP + p0
                            mm = nc.tensor.transpose(k.ps[2 + q % 2][:, c0:c0 + n], b["xg"][0:n, x, j, kk * P:(kk + 1) * P], k.c("ident", n, 0, n))
                    mm.then_inc(s["turned"], 1)

            def ups(g, h, x):
                pe.wait_ge(s[f"wgu_loaded{x}"], h * 32 + 32)
                pe.wait_ge(s["xt_copied"], g * TURN + after("xt_copied", TURN))
                for fh in range(2):
                    pe.wait_ge(s["hid_done"], g * 2 + after("hid_done", fh - 1))
                    for c0, wt in ((0, b["wg"]), (CAP, b["wu"])):
                        for kk in range(KD):
                            mm = nc.tensor.matmul(k.ps[fh][:, c0:c0 + CAP], wt[:, x, kk, fh * P:(fh + 1) * P], b["xgt"][:, x, kk, :], start=(kk == 0), stop=(kk == KD - 1))
                    mm.then_inc(s["up_mm"], 1)

            def downs(g, h, x):
                pe.wait_ge(s[f"wd_loaded{x}"], h * 16 + 16)
                pe.wait_ge(s["hid_done"], g * 2 + after("hid_done", 2))
                for j, (p0, n) in enumerate(parts):
                    pe.wait_ge(s[f"y{j}_done"], g + after("y0_done", 0))
                    for half in range(2):
                        for c in range(2):
                            mm = nc.tensor.matmul(k.ps[4 + 2 * j + half][0:n, :], b["hid"][:, c, p0:p0 + n], b["wd"][:, x, c, half * 512:(half + 1) * 512], start=(c == 0), stop=(c == 1))
                    mm.then_inc(s["down_mm"], 1)

            def one_round(rnd):
                G, HH = rnd * NE, rnd * (NE // 2)

                def pair(i, last):
                    ups(G + i * 2, HH + i, 0)
                    turn(rnd, G + i * 2 + 1, HH + i, 1)
                    downs(G + i * 2, HH + i, 0)
                    ups(G + i * 2 + 1, HH + i, 1)
                    if not last:
                        turn(rnd, G + i * 2 + 2, HH + i + 1, 0)
                    downs(G + i * 2 + 1, HH + i, 1)

                turn(rnd, G, HH, 0)
                with pe.Fori(0, NE // 2 - 1) as i:
                    pair(i, False)
                pair(NE // 2 - 1, True)
            all_rounds(pe, one_round)

        @block.scalar
        def _(act):
            def copies(g, x):
                for q in range(TURN):
                    act.wait_ge(s["turned"], g * TURN + after("turned", q + 1))
                    nc.scalar.copy(b["xgt"][:, x, 2 * q:2 * q + 2, :].rearrange("p k c -> p (k c)"), k.ps[2 + q % 2][:, 0:2 * CAP]).then_inc(s["xt_copied"], 1)

            def sigmoids(g):
                for fh in range(2):
                    act.wait_ge(s["up_mm"], g * 2 + after("up_mm", fh + 1))
                    nc.scalar.activation(b["sg"][:, fh, :], k.ps[fh][:, 0:CAP], ACT.Sigmoid).then_inc(s["sg_done"], 1)

            def second_rows(g, x):
                n = CAP - P
                act.wait_ge(s["down_mm"], g * 2 + after("down_mm", 2))
                act.wait_ge(s["y_free"], g + after("y_free", -1))
                nc.scalar.copy(b["y_out"][0:n, x, 1, :], k.psum[0:n, 6:8, :].rearrange("p b c -> p (b c)")).then_inc(s["y1_done"], 1)

            def one_round(rnd):
                G = rnd * NE

                def pair(i, last):
                    for x in range(2):
                        sigmoids(G + i * 2 + x)
                        if not (last and x == 1):
                            copies(G + i * 2 + (x + 1), 1 - x)
                        second_rows(G + i * 2 + x, x)

                copies(G, 0)
                with act.Fori(0, NE // 2 - 1) as i:
                    pair(i, False)
                pair(NE // 2 - 1, True)
            all_rounds(act, one_round)

        @block.vector
        def _(dve):
            def one_round(rnd):
                with dve.Fori(0, NE // 2) as i:
                    for x in range(2):
                        g = rnd * NE + i * 2 + x
                        for fh in range(2):
                            dve.wait_ge(s["sg_done"], g * 2 + (fh + 1))
                            nc.vector.tensor_tensor(b["sg"][:, fh, :], b["sg"][:, fh, :], k.ps[fh][:, 0:CAP], ALU.mult).then_inc(s["silu_done"], 1)
                            dve.wait_ge(s["silu_done"], g * 2 + (fh + 1))
                            nc.vector.tensor_tensor(b["hid"][:, fh, :], b["sg"][:, fh, :], k.ps[fh][:, CAP:2 * CAP], ALU.mult).then_inc(s["hid_done"], 1)
                        dve.wait_ge(s["down_mm"], g * 2 + after("down_mm", 1))
                        dve.wait_ge(s["y_free"], g + after("y_free", -1))
                        nc.vector.tensor_copy(b["y_out"][:, x, 0, :], k.psum[:, 4:6, :].rearrange("p b c -> p (b c)")).then_inc(s["y0_done"], 1)
            all_rounds(dve, one_round)


def combine_norm(k, x1, weight):
    nc, io = k.nc, k.io
    RB = 3
    st, b, s = phase(k, "final", dict(l2w=[P, D], l2b=[P, D], stats2=[P, 12], mv2=[P, NT, 2], ve2=[P, NT], rstd2=[P, NT], pair=[P, RB, 2, D]),
                     ["ln2_par", "row1_scaled", "sum1", "sum2", "st2", "mv2_done", "ve2_done", "rs2", "xh2", "y_mul", "y_done", "y_stored"]
                     + [f"rows_loaded{i}" for i in range(RB)])
    with st, nc.Block() as block:
        @block.sync
        def _(sp):
            sp.dma_start(b["l2w"][:, :], io["ln2_w"][0].partition_broadcast(P)).then_inc(s["ln2_par"], 16)
            sp.dma_start(b["l2b"][:, :], io["ln2_b"][0].partition_broadcast(P)).then_inc(s["ln2_par"], 16)
            def fetch(t):
                sp.dma_start(b["pair"][0:rows(t), t % RB].rearrange("p i d -> p (i d)"), k.y_dram[0:2 * T, :].rearrange("(t i) d -> t (i d)", i=2)[t * P:t * P + rows(t), :]).then_inc(s[f"rows_loaded{t % RB}"], 16)
            for t in range(RB):
                fetch(t)
            for t in range(NT):
                if t + RB < NT:
                    sp.wait_ge(s["sum2"], t + 1)
                    fetch(t + RB)
                sp.wait_ge(s["y_done"], t + 1)
                dst = io["y_prompt"][0, t * P:(t + 1) * P, :] if t < PT else io["y_sample"].rearrange("b t d -> (b t) d")
                sp.dma_start(dst, x1[0:rows(t), t, :]).then_inc(s["y_stored"], 16)
            sp.wait_ge(s["y_stored"], 16 * NT)

        @block.gpsimd
        def _(pool):
            for t in range(NT):
                r = rows(t)
                pool.wait_ge(s["ve2_done"], t + 1)
                nc.gpsimd.tensor_tensor(b["rstd2"][0:r, t:t + 1], b["ve2"][0:r, t:t + 1], k.c("minus_half", r, 0, 1), ALU.pow).then_inc(s["rs2"], 1)

        @block.scalar
        def _(act):
            def scale_row(t):
                r = rows(t)
                act.wait_ge(s[f"rows_loaded{t % RB}"], 16 * (t // RB + 1))
                row = b["pair"][0:r, t % RB, 0, :]
                nc.scalar.activation(row, row, ACT.Copy, scale=weight[0:r, 0, t:t + 1]).then_inc(s["row1_scaled"], 1)
            scale_row(0)
            for t in range(NT):
                if t + 1 < NT:
                    scale_row(t + 1)

        @block.vector
        def _(dve):
            def add(t):
                r = rows(t)
                x = x1[0:r, t, :]
                dve.wait_ge(s["row1_scaled"], t + 1)
                nc.vector.scalar_tensor_tensor(x, x, ALPHA, b["pair"][0:r, t % RB, 0, :], ALU.mult, ALU.add).then_inc(s["sum1"], 1)
                dve.wait_ge(s["sum1"], t + 1)
                dve.wait_ge(s[f"rows_loaded{t % RB}"], 16 * (t // RB + 1))
                nc.vector.scalar_tensor_tensor(x, b["pair"][0:r, t % RB, 1, :], weight[0:r, 1, t:t + 1], x, ALU.mult, ALU.add).then_inc(s["sum2"], 1)
                dve.wait_ge(s["sum2"], t + 1)
                for half in range(2):
                    nc.vector.bn_stats(b["stats2"][0:r, 6 * half:6 * half + 6], x[:, 512 * half:512 * half + 512]).then_inc(s["st2"], 1)
                dve.wait_ge(s["st2"], 2 * t + 2)
                nc.vector.bn_aggr(b["mv2"][0:r, t, :], b["stats2"][0:r, :]).then_inc(s["mv2_done"], 1)
                dve.wait_ge(s["mv2_done"], t + 1)
                nc.vector.tensor_scalar(b["ve2"][0:r, t:t + 1], b["mv2"][0:r, t, 1:2], EPS, None, ALU.add).then_inc(s["ve2_done"], 1)

            def norm(t):
                r = rows(t)
                x = x1[0:r, t, :]
                dve.wait_ge(s["rs2"], t + 1)
                nc.vector.tensor_scalar(x, x, b["mv2"][0:r, t, 0:1], b["rstd2"][0:r, t:t + 1], ALU.subtract, ALU.mult).then_inc(s["xh2"], 1)
                dve.wait_ge(s["xh2"], t + 1)
                nc.vector.tensor_tensor(x, x, b["l2w"][0:r, :], ALU.mult).then_inc(s["y_mul"], 1)
                dve.wait_ge(s["y_mul"], t + 1)
                nc.vector.tensor_tensor(x, x, b["l2b"][0:r, :], ALU.add).then_inc(s["y_done"], 1)

            dve.wait_ge(s["ln2_par"], 32)
            add(0)
            for t in range(1, NT):
                add(t)
                norm(t - 1)
            norm(NT - 1)


def build(nc, io):
    with ExitStack() as stack:
        k = Core(nc, stack, io)

        def left(st, name, shape):
            return st.enter_context(nc.sbuf_tensor(name, shape, F32))

        zd = left(stack, "z_dec", [P, 1, ZW])
        td = {n: left(stack, f"new_{n}_t", [P, 2, ND]) for n in ("nq", "mq", "fq", "mk", "fk")}
        td |= {n: left(stack, f"new_{n}_t", [P, ND]) for n in ("kcv", "ksel", "kwin")}
        a = {"sc": left(stack, "token_scalars", [P, NT, 12])}
        right_kcv, right_xt = ExitStack(), ExitStack()
        kcv = right_kcv.enter_context(nc.sbuf_tensor("kcv_t_p", [P, SEQ], F32, side="right"))
        xt = right_xt.enter_context(nc.sbuf_tensor("x_t", [P, KD, T], F32, side="right"))
        normalise_input(k, xt)
        with ExitStack() as att:
            z = left(att, "z", [P, PT, ZW])
            tb = {n: left(att, f"{n}_t", [P, 2, SEQ]) for n in ("nq", "mq", "fq", "mk", "fk")}
            tb |= {n: left(att, f"{n}_t", [P, SEQ]) for n in ("ksel", "kwin")}
            tb["kcv"] = kcv
            project(k, xt, z, tb, zd, td)
            right_xt.close()
            log_sigmoid_and_gates(k, z, zd, a)
            a |= {"u": left(att, "u", [P, PT, H]), "exp_neg_m": left(att, "exp_neg_m", [P, PT, H]), "cm": left(att, "neg_cm", [P, H, SEQ]),
                  "fneg": left(att, "neg_f_rows", [P, H, SEQ]), "kc": left(att, "kc", [P, 32]), "vc": left(att, "vc", [P, BW])}
            prompt_setup(k, z, tb, a)
            right_kcv.close()
            prompt_attention(k, z, tb, a)
        nc.clear_and_free_semaphores(k.used)
        nc.all_engine_barrier()
        decode_mixers(k, zd, td, a)
        with ExitStack() as ts:
            ys = ExitStack()
            y = ys.enter_context(nc.sbuf_tensor("y_t", [P, KD, T], F32, side="right"))
            merge_branches(k, y)
            x1 = left(stack, "x1", [P, NT, D])
            weight = left(stack, "expert_weight", [P, 2, NT])
            most = stack.enter_context(nc.sbuf_tensor("most_tokens", [P, 1], I32))
            x1t = left(ts, "x1_t", [P, KD, T])
            mix_out_norm(k, y, x1t, x1)
            ys.close()
            route(k, x1t, weight, most)
        experts(k, most)
        combine_norm(k, x1, weight)


INS = ["x_prompt", "x_sample", "cache_nsa", "cache_nsa_win", "cache_fox_kv", "cache_fox_logf", "state_mlstm_c", "state_mlstm_n",
       "state_mlstm_m", "page_table", "ln_in_w", "ln_in_b", "w_in", "b_in", "nsa_w_ck", "nsa_w_cv", "mlstm_norm_w", "w_branch", "w_out",
       "ln1_w", "ln1_b", "moe_w_group", "moe_b_group", "moe_w_expert", "moe_b_expert", "moe_w_gate", "moe_w_up", "moe_w_down", "ln2_w", "ln2_b"]
OUTS = [("y_prompt", (1, SEQ, D)), ("y_sample", (DB, DT, D)), ("p_nsa_rows", (1, 1, SEQ, 4, HD)), ("p_nsa_win", (1, 1, WIN, 2, HD)),
        ("p_fox_kv", (1, 1, SEQ, 2, H, HD)), ("p_fox_logf", (1, 1, SEQ, H)), ("p_mlstm_c", (1, 1, H, HD, HD)), ("p_mlstm_n", (1, 1, H, HD)),
        ("p_mlstm_m", (1, 1, H)), ("s_nsa_rows", (1, DB, DT, 4, HD)), ("s_nsa_win", (1, DB, PAST, 2, HD)), ("s_fox_kv", (1, DB, DT, 2, H, HD)),
        ("s_fox_logf", (1, DB, DT, H)), ("s_mlstm_c", (1, DB, H, HD, HD)), ("s_mlstm_n", (1, DB, H, HD)), ("s_mlstm_m", (1, DB, H))]


def kernel(**inputs):
    import concourse.bacc as bacc
    from concourse.bass_utils import run_bass_kernel_spmd

    nc = bacc.Bacc("TRN2", target_bir_lowering=False, num_devices=1)
    arrays = {f"in_{n}": np.ascontiguousarray(inputs[n]) for n in INS}
    arrays |= {"in_table": TABLE, "in_alibi": ALIBI, "in_empty_slots": EMPTY_SLOTS}
    io = {n[3:]: nc.dram_tensor(n, a.shape, mybir.dt.from_np(a.dtype), kind="ExternalInput").ap() for n, a in arrays.items()}
    io |= {n: nc.dram_tensor(f"out_{n}", shape, F32, kind="ExternalOutput").ap() for n, shape in OUTS}
    build(nc, io)
    r = run_bass_kernel_spmd(nc, [arrays], core_ids=[0])
    return tuple(r.results[0][f"out_{n}"] for n, _ in OUTS)
```
